# Optimizing a Trainium2 kernel written in Bass

```python
import jax, jax.numpy as jnp
from jax import lax
import numpy as np

D_MODEL = 1024
BATCH = 1
SEQ = 512
DEPTH = 1

SB_HEADS = 8
SB_HEAD_DIM = 64
SB_BLOCK = 128
DN_HEADS = 4
DN_KEY_DIM = 128
DN_VALUE_DIM = 128
DN_CONV = 4
DN_CHUNK = 64
D_FF = 2816
N_MOD = 9
EPS = 1e-6

SB_W = SB_HEADS * SB_HEAD_DIM
DN_QK_W = DN_HEADS * DN_KEY_DIM
DN_V_W = DN_HEADS * DN_VALUE_DIM
IN_SPLITS = (SB_W, SB_W, SB_W, DN_QK_W, DN_QK_W, DN_V_W, DN_V_W, DN_HEADS, DN_HEADS, D_MODEL, D_MODEL)
IN_WIDTH = 3 * SB_W + 2 * DN_QK_W + 2 * DN_V_W + 2 * DN_HEADS + 2 * D_MODEL

kernel_name = "hybrid_stickbreak_gdn_macaron_adaln"

def rms_norm(x, gain):
    xf = x.astype(jnp.float32)
    y = xf * lax.rsqrt(jnp.mean(xf * xf, axis=-1, keepdims=True) + EPS)
    return (y * gain.astype(jnp.float32)).astype(x.dtype)

def l2_norm(x):
    xf = x.astype(jnp.float32)
    return xf * lax.rsqrt(jnp.sum(xf * xf, axis=-1, keepdims=True) + EPS)

def modulate(x, shift, scale):
    return x * (1.0 + scale) + shift

def swiglu(u, w_in, w_out):
    a, b = jnp.split(u @ w_in, 2, axis=-1)
    return (jax.nn.silu(a) * b) @ w_out

def causal_depthwise_conv(x, w):
    k = w.shape[0]
    return lax.conv_general_dilated(
        x, w[:, None, :].astype(x.dtype), window_strides=(1,), padding=[(k - 1, 0)],
        dimension_numbers=("NWC", "WIO", "NWC"), feature_group_count=x.shape[-1])

def stick_breaking_attention(q, k, v):
    seq = q.shape[2]
    scale = SB_HEAD_DIM ** -0.5
    outs = []
    for blk in range(seq // SB_BLOCK):
        start = blk * SB_BLOCK
        end = start + SB_BLOCK
        qb = q[:, :, start:end]
        kb = k[:, :, :end]
        vb = v[:, :, :end]
        z = jnp.einsum("bhqd,bhkd->bhqk", qb, kb, preferred_element_type=jnp.float32) * scale
        t_pos = start + jnp.arange(SB_BLOCK)[:, None]
        s_pos = jnp.arange(end)[None, :]
        causal = s_pos < t_pos
        log_beta = jax.nn.log_sigmoid(z)
        log_keep = jnp.where(causal, jax.nn.log_sigmoid(-z), 0.0)
        later = lax.cumsum(log_keep, axis=3, reverse=True) - log_keep
        w = jnp.where(causal, jnp.exp(log_beta + later), 0.0)
        outs.append(jnp.einsum("bhqk,bhkd->bhqd", w.astype(v.dtype), vb))
    return jnp.concatenate(outs, axis=2)

def gated_delta_rule_chunked(q, k, v, g, beta):
    bsz, seq, nh, dk = q.shape
    dv = v.shape[-1]
    c = DN_CHUNK
    n = seq // c
    f32 = jnp.float32
    q = q.astype(f32) * (dk ** -0.5)
    chunk = lambda a: a.astype(f32).transpose(0, 2, 1, 3).reshape(bsz, nh, n, c, a.shape[-1])
    q, k, v = chunk(q), chunk(k), chunk(v)
    g = jnp.cumsum(g.astype(f32).transpose(0, 2, 1).reshape(bsz, nh, n, c), axis=-1)
    beta = beta.astype(f32).transpose(0, 2, 1).reshape(bsz, nh, n, c)
    kb = k * beta[..., None]
    vb = v * beta[..., None]
    incl = jnp.tril(jnp.ones((c, c), dtype=bool))
    strict = jnp.tril(jnp.ones((c, c), dtype=bool), -1)
    diff = g[..., :, None] - g[..., None, :]
    decay = jnp.where(incl, jnp.exp(jnp.where(incl, diff, 0.0)), 0.0)
    lower = jnp.where(strict, jnp.einsum("bhnid,bhnjd->bhnij", kb, k) * decay, 0.0)
    rhs = jnp.concatenate([vb, kb * jnp.exp(g)[..., None]], axis=-1)
    sol = lax.linalg.triangular_solve(lower, rhs, left_side=True, lower=True, unit_diagonal=True)
    u, w = sol[..., :dv], sol[..., dv:]
    a_qk = jnp.where(incl, jnp.einsum("bhnid,bhnjd->bhnij", q, k) * decay, 0.0)

    def step(state, inp):
        q_c, k_c, u_c, w_c, g_c, a_c = inp
        v_new = u_c - jnp.matmul(w_c, state)
        o = jnp.matmul(q_c * jnp.exp(g_c)[..., None], state) + jnp.matmul(a_c, v_new)
        g_last = g_c[..., -1]
        k_dec = k_c * jnp.exp(g_last[..., None] - g_c)[..., None]
        state = state * jnp.exp(g_last)[..., None, None] + jnp.einsum("bhcd,bhce->bhde", k_dec, v_new)
        return state, o

    xs = tuple(jnp.moveaxis(a, 2, 0) for a in (q, k, u, w, g, a_qk))
    state0 = jnp.zeros((bsz, nh, dk, dv), f32)
    _, o = lax.scan(step, state0, xs)
    o = jnp.moveaxis(o, 0, 2).reshape(bsz, nh, seq, dv)
    return o.transpose(0, 2, 1, 3)

def hybrid_mixer(u, w_in, g_q_sb, g_k_sb, w_conv, a_log, dt_bias, g_dn_out, w_up_sb, w_up_dn, w_out):
    bsz, seq, _ = u.shape
    offsets = [int(o) for o in np.cumsum(IN_SPLITS)[:-1]]
    (q_sb, k_sb, v_sb, q_dn, k_dn, v_dn, z_dn, b_dn, a_dn, r_sb, r_dn) = jnp.split(u @ w_in, offsets, axis=-1)

    to_heads = lambda t: t.reshape(bsz, seq, SB_HEADS, SB_HEAD_DIM)
    q_a = rms_norm(to_heads(q_sb), g_q_sb).transpose(0, 2, 1, 3)
    k_a = rms_norm(to_heads(k_sb), g_k_sb).transpose(0, 2, 1, 3)
    v_a = to_heads(v_sb).transpose(0, 2, 1, 3)
    y_sb = stick_breaking_attention(q_a, k_a, v_a)
    y_sb = y_sb.transpose(0, 2, 1, 3).reshape(bsz, seq, SB_W) @ w_up_sb

    qkv = jax.nn.silu(causal_depthwise_conv(jnp.concatenate([q_dn, k_dn, v_dn], axis=-1), w_conv))
    q_b, k_b, v_b = jnp.split(qkv, [DN_QK_W, 2 * DN_QK_W], axis=-1)
    q_b = l2_norm(q_b.reshape(bsz, seq, DN_HEADS, DN_KEY_DIM))
    k_b = l2_norm(k_b.reshape(bsz, seq, DN_HEADS, DN_KEY_DIM))
    v_b = v_b.reshape(bsz, seq, DN_HEADS, DN_VALUE_DIM)
    beta = jax.nn.sigmoid(b_dn.astype(jnp.float32))
    g = -jnp.exp(a_log.astype(jnp.float32)) * jax.nn.softplus(a_dn.astype(jnp.float32) + dt_bias.astype(jnp.float32))
    o = gated_delta_rule_chunked(q_b, k_b, v_b, g, beta)
    o = rms_norm(o, g_dn_out) * jax.nn.silu(z_dn.reshape(bsz, seq, DN_HEADS, DN_VALUE_DIM).astype(jnp.float32))
    y_dn = o.reshape(bsz, seq, DN_V_W).astype(u.dtype) @ w_up_dn

    merged = jax.nn.sigmoid(r_sb) * y_sb + jax.nn.sigmoid(r_dn) * y_dn
    return merged @ w_out

def setup_inputs(seed: int = 0) -> dict:
    key = jax.random.key(seed)
    ks = jax.random.split(key, 24)
    nrm = lambda k, shape, fan_in: jax.random.normal(k, shape, jnp.float32) * (fan_in ** -0.5)
    gain = lambda k, shape: 1.0 + 0.02 * jax.random.normal(k, shape, jnp.float32)
    dt = jnp.exp(jax.random.uniform(ks[14], (DEPTH, DN_HEADS), jnp.float32, np.log(1e-3), np.log(1e-1)))
    return {
        "x": jax.random.normal(ks[0], (BATCH, SEQ, D_MODEL), jnp.float32),
        "c": jax.random.normal(ks[1], (BATCH, D_MODEL), jnp.float32),
        "w_ada": nrm(ks[2], (DEPTH, D_MODEL, N_MOD * D_MODEL), D_MODEL),
        "b_ada": 0.02 * jax.random.normal(ks[3], (DEPTH, N_MOD * D_MODEL), jnp.float32),
        "g_ffn1": gain(ks[4], (DEPTH, D_MODEL)),
        "w_ffn1_in": nrm(ks[5], (DEPTH, D_MODEL, 2 * D_FF), D_MODEL),
        "w_ffn1_out": nrm(ks[6], (DEPTH, D_FF, D_MODEL), D_FF),
        "g_mix": gain(ks[7], (DEPTH, D_MODEL)),
        "w_in": nrm(ks[8], (DEPTH, D_MODEL, IN_WIDTH), D_MODEL),
        "g_q_sb": gain(ks[9], (DEPTH, SB_HEAD_DIM)),
        "g_k_sb": gain(ks[10], (DEPTH, SB_HEAD_DIM)),
        "w_conv": nrm(ks[11], (DEPTH, DN_CONV, 2 * DN_QK_W + DN_V_W), DN_CONV),
        "a_log": jnp.log(jax.random.uniform(ks[12], (DEPTH, DN_HEADS), jnp.float32, 1.0, 16.0)),
        "dt_bias": dt + jnp.log(-jnp.expm1(-dt)),
        "g_dn_out": gain(ks[13], (DEPTH, DN_VALUE_DIM)),
        "w_up_sb": nrm(ks[15], (DEPTH, SB_W, D_MODEL), SB_W),
        "w_up_dn": nrm(ks[16], (DEPTH, DN_V_W, D_MODEL), DN_V_W),
        "w_out": nrm(ks[17], (DEPTH, D_MODEL, D_MODEL), D_MODEL),
        "g_ffn2": gain(ks[18], (DEPTH, D_MODEL)),
        "w_ffn2_in": nrm(ks[19], (DEPTH, D_MODEL, 2 * D_FF), D_MODEL),
        "w_ffn2_out": nrm(ks[20], (DEPTH, D_FF, D_MODEL), D_FF),
    }

def reference(x, c, w_ada, b_ada, g_ffn1, w_ffn1_in, w_ffn1_out, g_mix, w_in, g_q_sb, g_k_sb, w_conv,
              a_log, dt_bias, g_dn_out, w_up_sb, w_up_dn, w_out, g_ffn2, w_ffn2_in, w_ffn2_out):
    h = x
    cond = jax.nn.silu(c)
    for l in range(DEPTH):
        mod = cond @ w_ada[l] + b_ada[l]
        sh1, sc1, gt1, sh2, sc2, gt2, sh3, sc3, gt3 = [m[:, None, :] for m in jnp.split(mod, N_MOD, axis=-1)]
        u = modulate(rms_norm(h, g_ffn1[l]), sh1, sc1)
        h = h + 0.5 * gt1 * swiglu(u, w_ffn1_in[l], w_ffn1_out[l])
        u = modulate(rms_norm(h, g_mix[l]), sh2, sc2)
        h = h + gt2 * hybrid_mixer(u, w_in[l], g_q_sb[l], g_k_sb[l], w_conv[l], a_log[l], dt_bias[l],
                                   g_dn_out[l], w_up_sb[l], w_up_dn[l], w_out[l])
        u = modulate(rms_norm(h, g_ffn2[l]), sh3, sc3)
        h = h + 0.5 * gt3 * swiglu(u, w_ffn2_in[l], w_ffn2_out[l])
    return h.astype(x.dtype)


_drawn_inputs = setup_inputs


def setup_inputs(seed=0):
    import zlib

    import numpy as np

    out = dict(_drawn_inputs(seed))
    spreads = {}
    factors = {'g_ffn1': 6.603,
     'g_mix': 5.443,
     'g_q_sb': 32.003,
     'g_k_sb': 32.314,
     'g_dn_out': 24.198,
     'g_ffn2': 21.437}
    for name, (base, spread) in spreads.items():
        noise = np.random.default_rng([zlib.crc32(name.encode()), seed]).standard_normal(out[name].shape)
        drawn = base * np.exp(spread * noise) if base else spread * noise
        out[name] = __import__('jax').numpy.asarray(drawn.astype(out[name].dtype))
    for name, factor in factors.items():
        out[name] = (out[name] * factor).astype(out[name].dtype)
    return out
```

```python
from contextlib import ExitStack

import concourse.bass as bass
from concourse import mybir

P = 128
S = 512
D = 1024
KD = D // P
FF = 2816
KF = FF // P
HALF = KF // 2
SBH, SBD = 8, 64
DNH = 4
NB = S // P
TAPS = 4
EPS = 1e-6
MODS = 9
PIECE = 256
EARLY = 2 * D // PIECE
RAW = 4

F1_IN = 0
F1_OUT = F1_IN + 2 * KF
SB_IN = F1_OUT + 2 * KD
DN_IN = SB_IN + 12
MERGE = DN_IN + 17
W_OUT = MERGE + 3 * KD
F2_IN = W_OUT + KD
F2_OUT = F2_IN + 2 * KF
UNITS = F2_OUT + 2 * KD

COL_DN = 3 * 512
COL_BA = COL_DN + 4 * 512
COL_RSB = COL_BA + 8
COL_RDN = COL_RSB + D


def unit_chunks(n):
    return HALF if F1_OUT <= n < SB_IN or n >= F2_OUT else KD


def is_static(i):
    return isinstance(i, int)


def laps(engine, count, lo=1, hi=1):
    for i in range(lo):
        yield i
    if count - hi > lo:
        with engine.Fori(lo, count - hi) as i:
            yield i
    for i in range(count - hi, count):
        yield i


def build(nc, x, c, w_ada, b_ada, g_ffn1, w_ffn1_in, w_ffn1_out, g_mix, w_in, g_q_sb, g_k_sb, w_conv,
          a_log, dt_bias, g_dn_out, w_up_sb, w_up_dn, w_out, g_ffn2, w_ffn2_in, w_ffn2_out, out):
    f32, f32r = mybir.dt.float32, mybir.dt.float32r
    ALU, ACT = mybir.AluOpType, mybir.ActivationFunctionType
    ds = bass.ds

    def rows(w):
        return w[0].rearrange("(k p) n -> p k n", p=P)

    w_ada_v, w_in_v = rows(w_ada), rows(w_in)
    ffn_in_v = [rows(w_ffn1_in), rows(w_ffn2_in)]
    ffn_out_v = [rows(w_ffn1_out), rows(w_ffn2_out)]
    up_sb_v, up_dn_v, w_out_v = rows(w_up_sb), rows(w_up_dn), rows(w_out)

    with ExitStack() as ctx:
        def sb(name, shape, dt=f32, stack=ctx):
            return stack.enter_context(nc.sbuf_tensor(name, shape, dt))[tuple(slice(None) for _ in shape)]

        def sem(name):
            return ctx.enter_context(nc.semaphore(name))

        hT = sb("hT", [P, KD, S])
        u_hi, u_lo = sb("u_hi", [P, KD, S], f32r), sb("u_lo", [P, KD, S], f32r)
        raw = sb("raw", [P, RAW, HALF, P])
        w_hi, w_lo = sb("w_hi", [P, 2, HALF, P], f32r), sb("w_lo", [P, 2, HALF, P], f32r)
        ident, ones = sb("ident", [P, P]), sb("ones", [P, P])
        mean_d, mean_p = sb("mean_d", [P, P]), sb("mean_p", [P, P])
        mean_64 = sb("mean_64", [P, P])
        below = sb("below", [P, P])
        above = sb("above", [P, P])
        upto = sb("upto", [P, P])
        vec = sb("vec", [P, 104])
        vec2 = sb("vec2", [P, 51])
        alog_dt = sb("alog_dt", [P, 2, DNH])
        cond = sb("cond", [P, KD])
        qk_gain = sb("qk_gain", [P, 2])
        mod = sb("mod", [P, MODS * KD])
        scale_col = sb("scale_col", [P, 3, KD])
        gate_col = sb("gate_col", [P, 3, KD])
        ada_acc = sb("ada_acc", [P, 2, PIECE])
        eps = sb("eps", [P, 1])
        ssq = sb("ssq", [P, S])
        rstd = sb("rstd", [P, S])
        work = sb("work", [P, 2, S])

        with ExitStack() as s:
            vec_rows = sb("vec_rows", [104, P], stack=s)
            vec2_rows = sb("vec2_rows", [51, P], stack=s)
            x_nat = sb("x_nat", [P, NB, D], stack=s)
            ada_early = sb("ada_early", [P, EARLY, KD, PIECE], stack=s)
        with ExitStack() as s:
            g_hi, g_lo = sb("g_hi", [P, KF, S], f32r, stack=s), sb("g_lo", [P, KF, S], f32r, stack=s)
            with ExitStack() as t:
                ada_raw = sb("ada_raw", [P, KD, PIECE], stack=t)
            with ExitStack() as t:
                out_nat = sb("out_nat", [P, 2, NB, P], stack=t)
        with ExitStack() as s:
            ysb_hi, ysb_lo = sb("ysb_hi", [P, 4, S], f32r, stack=s), sb("ysb_lo", [P, 4, S], f32r, stack=s)
            with ExitStack() as t:
                conv = sb("conv", [P, 12, S], stack=t)
                ab_T = sb("ab_T", [2 * DNH, S], stack=t)
                with ExitStack() as v:
                    sb_T = sb("sb_T", [P, 12, S], stack=v)
                    v_nat = sb("v_nat", [P, NB, SBH * SBD], stack=v)
                    pad = sb("pad", [P, 2, TAPS - 1 + S], stack=v)
                    att_a, att_b = sb("att_a", [P, 2, 1280], stack=v), sb("att_b", [P, 2, 1280], stack=v)
                with ExitStack() as v:
                    z_gate = sb("z_gate", [P, DNH, S], stack=v)
                    small = {n: sb("dn_" + n, [P, NB, DNH], stack=v) for n in
                             ("beta", "neg_beta", "a", "abs", "exp", "log", "g", "gsum", "gexp", "glast", "kdec")}
                    rate = sb("rate", [P, DNH], stack=v)
                    inv, inv_t, sys_t, link, prod = (sb("dn_" + n, [P, 2, DNH, P], stack=v) for n in
                                                    ("inv", "inv_t", "sys_t", "link", "prod"))
                    att_t, w_t = sb("att_t", [P, 2, DNH, P], stack=v), sb("w_t", [P, 2, DNH, P], stack=v)
                    state = sb("state", [P, DNH, P], stack=v)
                    level = sb("level", [P, 7, P], stack=v)
                    with ExitStack() as w:
                        k_dn = sb("k_dn", [P, NB, DNH, P], stack=w)
                        v_dn = sb("v_dn", [P, NB, DNH, P], stack=w)
                    with ExitStack() as w:
                        ydn_hi = sb("ydn_hi", [P, 4, S], f32r, stack=w)
                        ydn_lo = sb("ydn_lo", [P, 4, S], f32r, stack=w)
            with ExitStack() as t:
                m_hi, m_lo = sb("m_hi", [P, KD, S], f32r, stack=t), sb("m_lo", [P, KD, S], f32r, stack=t)

        v_new = ssq[:, :].rearrange("p (h e) -> p h e", h=DNH)
        out_nat_cols = out[0].rearrange("(b p) n -> p b n", p=P)

        region = [ctx.enter_context(nc.psum_tensor(f"region{r}", [P, 3 * S], f32)) for r in range(2)]
        tail = ctx.enter_context(nc.psum_tensor("tail", [P, 2 * S], f32))

        def bank(b):
            t, k = (region[b // 3], b % 3) if b < 6 else (tail, b - 6)
            return t[:, k * S:(k + 1) * S]

        def heads(ap):
            return ap.rearrange("p (h e) -> p h e", h=DNH)

        small_in, rates_in, x_in = sem("small_in"), sem("rates_in"), sem("x_in")
        ada_early_in = [sem(f"ada_early_in{q}") for q in range(EARLY)]
        ada_in = sem("ada_in")
        raw_in = [sem(f"raw_in{r}") for r in range(RAW)]
        out_done = [sem(f"out_done{k}") for k in range(2)]
        masks, mask_step = sem("masks"), sem("mask_step")
        vec_ps, vec_ready, cond_ready = sem("vec_ps"), sem("vec_ready"), sem("cond_ready")
        x_ps, h_ready, sq_ready, ssq_step = sem("x_ps"), sem("h_ready"), sem("sq_ready"), sem("ssq_step")
        stat_ps, root_ready, rstd_ready = sem("stat_ps"), sem("root_ready"), sem("rstd_ready")
        cols_ready, normed_ready = sem("cols_ready"), sem("normed_ready")
        u_hi_ready, u_lo_ready = sem("u_hi_ready"), sem("u_lo_ready")
        ada_step, mod_ps, mod_ready = sem("ada_step"), sem("mod_ps"), sem("mod_ready")
        hi_ready, lo_ready, unit_done = sem("hi_ready"), sem("lo_ready"), sem("unit_done")
        silu_ready, glu_ready = sem("silu_ready"), sem("glu_ready")
        g_hi_ready, g_lo_ready = sem("g_hi_ready"), sem("g_lo_ready")
        out_ps, out_ready = sem("out_ps"), sem("out_ready")
        proj_ready, pad_zero, conv_step = sem("proj_ready"), sem("pad_zero"), sem("conv_step")
        qk_sq, qk_stat, qk_root, qk_rs, qk_ready = (sem("qk_sq"), sem("qk_stat"), sem("qk_root"), sem("qk_rs"),
                                                    sem("qk_ready"))
        vt_ps, v_nat_ready = sem("vt_ps"), sem("v_nat_ready")
        gain_ready = sem("gain_ready")
        z_ps, soft_step, keep_ready, keep_masked = sem("z_ps"), sem("soft_step"), sem("keep_ready"), sem("keep_masked")
        beta_ready, later_ps, logw_ready, w_raw, w_masked = (sem("nb_ready"), sem("later_ps"), sem("logw_ready"),
                                                            sem("w_raw"), sem("w_masked"))
        y_ps, y_hi_ready, y_lo_ready = sem("y_ps"), sem("y_hi_ready"), sem("y_lo_ready")
        dn_silu, l2_sq, l2_stat, l2_root, l2_rs, l2_ready = (sem("dn_silu"), sem("l2_sq"), sem("l2_stat"),
                                                             sem("l2_root"), sem("l2_rs"), sem("l2_ready"))
        z_silu = sem("z_silu")
        ab_ps, gate_act, gate_dve, gsum_ps, gsum_act = (sem("ab_ps"), sem("gate_act"), sem("gate_dve"),
                                                        sem("gsum_ps"), sem("gsum_act"))
        nat_ps, nat_ready, nat_v_ready = sem("nat_ps"), sem("nat_ready"), sem("nat_v_ready")
        prep_ps, dec_raw, dec_exp, dec_masked, gexp_ready = (sem("prep_ps"), sem("dec_raw"), sem("dec_exp"),
                                                             sem("dec_masked"), sem("gexp_ready"))
        glast_ready, kdec_exp, sys_ready, att_ready = (sem("glast_ready"), sem("kdec_exp"), sem("sys_ready"),
                                                       sem("att_ready"))
        link_ready, inv_t0, inv0_ps, inv0_ready = sem("link_ready"), sem("inv_t0"), sem("inv0_ps"), sem("inv0_ready")
        prod_ps, prod_ready, corr_ps, inv_ready = sem("prod_ps"), sem("prod_ready"), sem("corr_ps"), sem("inv_ready")
        kexp_ready, kdec_ready, uw_ps, u_ready, w_ready = (sem("kexp_ready"), sem("kdec_ready"), sem("uw_ps"),
                                                           sem("u_ready"), sem("w_ready"))
        ws_ps, v_new_ready, o_ps, o_ready, ds_ps, state_ready = (sem("ws_ps"), sem("v_new_ready"), sem("o_ps"),
                                                                 sem("o_ready"), sem("ds_ps"), sem("state_ready"))
        on_sq, on_stat, on_root, on_rs, on_scaled, on_gated = (sem("on_sq"), sem("on_stat"), sem("on_root"),
                                                               sem("on_rs"), sem("on_scaled"), sem("on_gated"))
        ydn_hi_ready = sem("ydn_hi_ready")
        branch_lo = sem("branch_lo")
        sig_ready, part_ready, sum_ready, m_hi_ready = (sem("sig_ready"), sem("part_ready"), sem("sum_ready"),
                                                        sem("m_hi_ready"))

        SH, SC, GT = [0, 3, 6], [1, 4, 7], [2, 5, 8]
        OFF = [0, 512, 1024, 896]
        WID = [S - P * j for j in range(NB)]
        QK = [0, 4, 1, 5, 2, 6, 3, 7]
        block = ctx.enter_context(nc.Block())

        @block.sync
        def _(sp):
            def source(phase, i, u):
                if is_static(i):
                    n = phase + 4 * i + u
                    phase = max(f for f in (F1_IN, F1_OUT, SB_IN, DN_IN, MERGE, W_OUT, F2_IN, F2_OUT) if f <= n)
                    i, u = 0, n - phase
                f = int(phase >= F2_IN)
                if phase in (F1_IN, F2_IN):
                    v, col, k0, kn = ffn_in_v[f], (4 * i + u - u % 2) * (P // 2) + (u % 2) * FF, 0, KD
                elif phase in (F1_OUT, F2_OUT):
                    v, col, k0, kn = ffn_out_v[f], (4 * i + u - u % 2) * (P // 2), (u % 2) * HALF, HALF
                elif phase == SB_IN:
                    v, col, k0, kn = w_in_v, u * P, 0, KD
                elif phase == DN_IN:
                    v, k0, kn = w_in_v, 0, KD
                    col = COL_BA if u == 0 else COL_DN + P * ((u + 3) if u <= 4 else (u - 5) if u <= 8 else u - 1)
                elif phase == MERGE and u % 3 == 2:
                    col = (u // 3) * P
                    return [(0, 4, up_sb_v[:, :, col:col + P]), (4, 8, up_dn_v[:, :, col:col + P])]
                elif phase == MERGE:
                    v, col, k0, kn = w_in_v, (COL_RSB, COL_RDN)[u % 3] + (u // 3) * P, 0, KD
                else:
                    v, col, k0, kn = w_out_v, u * P, 0, KD
                cut = kn // 2
                return [(0, cut, v[:, k0:k0 + cut, ds(col, P)]), (cut, kn, v[:, k0 + cut:k0 + kn, ds(col, P)])]

            def load(phase, i, u):
                slot = (phase + u) % RAW
                for a, b, view in source(phase, i, u):
                    sp.dma_start(raw[:, slot, a:b, :], view).then_inc(raw_in[slot], 16)

            def load_next(phase, i, u):
                if is_static(i) and phase + 4 * i + u + RAW >= UNITS:
                    return
                sp.wait_ge(lo_ready, phase + 4 * i + u + 1)
                load(phase, i, u + RAW)

            sp.dma_start(vec_rows[0:8, :], c[0].rearrange("(k p) -> k p", p=P)).then_inc(small_in, 16)
            sp.dma_start(vec_rows[8:80, :], b_ada[0].rearrange("(k p) -> k p", p=P)).then_inc(small_in, 16)
            for n, g in enumerate((g_ffn1, g_mix, g_ffn2)):
                sp.dma_start(vec_rows[80 + 8 * n:88 + 8 * n, :], g[0].rearrange("(k p) -> k p", p=P)).then_inc(small_in, 16)
            for t in range(TAPS):
                sp.dma_start(vec2_rows[12 * t:12 * t + 12, :],
                             w_conv[0, t].rearrange("(k p) -> k p", p=P)).then_inc(small_in, 16)
            sp.dma_start(vec2_rows[48:49, :], g_dn_out).then_inc(small_in, 16)
            for n, g in enumerate((g_q_sb, g_k_sb)):
                for half in range(2):
                    sp.dma_start(vec2_rows[49 + n:50 + n, half * SBD:half * SBD + SBD], g).then_inc(small_in, 16)
            for n, g in enumerate((a_log, dt_bias)):
                sp.dma_start(alog_dt[:, n, :], g[0].partition_broadcast(P)).then_inc(rates_in, 16)
            for q in range(EARLY):
                sp.dma_start(ada_early[:, q], w_ada_v[:, :, q * PIECE:(q + 1) * PIECE]).then_inc(ada_early_in[q], 16)
                if q % 2:
                    b = q // 2
                    sp.dma_start(x_nat[:, b, :], x[0, b * P:(b + 1) * P, :]).then_inc(x_in, 16)
            for u in range(RAW):
                load(F1_IN, 0, u)

            for i in laps(sp, KF // 2, 0, 1):
                for u in range(4):
                    load_next(F1_IN, i, u)
                    if u % 2 == 0:
                        q = EARLY + 2 * i + u // 2
                        sp.wait_ge(ada_step, KD * q)
                        sp.dma_start(ada_raw, w_ada_v[:, :, ds(PIECE * q, PIECE)]).then_inc(ada_in, 16)
            for i in laps(sp, KD // 2, 0, 1):
                for u in range(4):
                    load_next(F1_OUT, i, u)
                    if u % 2 == 0 and not (is_static(i) and i == KD // 2 - 1):
                        q = EARLY + KF + 2 * i + u // 2
                        sp.wait_ge(ada_step, KD * q)
                        sp.dma_start(ada_raw, w_ada_v[:, :, ds(PIECE * q, PIECE)]).then_inc(ada_in, 16)
            for n in range(SB_IN, F2_IN):
                load_next(n, 0, 0)
            for phase, steps in ((F2_IN, KF // 2), (F2_OUT, KD // 2)):
                for i in laps(sp, steps, 0, 1):
                    for u in range(4):
                        load_next(phase, i, u)

        @block.gpsimd
        def _(pool):
            steps = [0]

            def then(ins):
                steps[0] += 1
                ins.then_inc(mask_step, 1)
                pool.wait_ge(mask_step, steps[0])

            def triangle(t, base, sign, op):
                then(pool.memset(t, 1.0))
                return pool.affine_select(out=t, in_=t, compare_op=op, fill=0.0, base=base,
                                          pattern=[[sign, P]], channel_multiplier=-sign)

            triangle(ident[:, :], 0, 1, ALU.is_equal).then_inc(masks, 1)
            pool.memset(ones[:, :], 1.0).then_inc(masks, 1)
            pool.memset(eps[:, :], EPS).then_inc(masks, 1)
            pool.memset(mean_d[:, :], 1.0 / D).then_inc(masks, 1)
            pool.memset(mean_p[:, :], 1.0 / P).then_inc(masks, 1)
            then(pool.memset(mean_64[:, :], 1.0 / SBD))
            for half, base, sign in ((mean_64[:, 0:SBD], SBD - 1, -1), (mean_64[:, SBD:P], -SBD, 1)):
                pool.affine_select(out=half, in_=half, compare_op=ALU.is_ge, fill=0.0, base=base,
                                   pattern=[[0, SBD]], channel_multiplier=sign).then_inc(masks, 1)
            triangle(below[:, :], 0, -1, ALU.is_gt).then_inc(masks, 1)
            triangle(above[:, :], 0, 1, ALU.is_gt).then_inc(masks, 1)
            triangle(upto[:, :], 0, 1, ALU.is_ge).then_inc(masks, 1)

            def sum_squares(s):
                for o in range(KD - 1):
                    pool.wait_ge(sq_ready, KD * s + o + 1)
                    if o == 0:
                        pool.tensor_copy(ssq[:, :], work[:, 0, :]).then_inc(ssq_step, 1)
                    else:
                        pool.wait_ge(ssq_step, (KD - 1) * s + o)
                        pool.tensor_tensor(ssq[:, :], ssq[:, :], work[:, o % 2, :], ALU.add).then_inc(ssq_step, 1)

            sum_squares(0)
            sum_squares(1)
            pool.wait_ge(u_lo_ready, 2 * KD)
            pool.memset(pad[:, :, 0:TAPS - 1], 0.0).then_inc(pad_zero, 1)

            def diagonal(t, done):
                for j in range(NB):
                    d = t[:, OFF[j]:OFF[j] + P]
                    ins = pool.tensor_tensor(d, d, above[:, :], ALU.mult)
                ins.then_inc(done, 1)

            for h in range(2):
                pool.wait_ge(keep_ready, h + 1)
                diagonal(att_b[:, h % 2, :], keep_masked)
            for h in range(SBH):
                pool.wait_ge(w_raw, h + 1)
                diagonal(att_a[:, h % 2, :], w_masked)
                if h + 2 < SBH:
                    pool.wait_ge(keep_ready, h + 3)
                    diagonal(att_b[:, h % 2, :], keep_masked)

            pool.wait_ge(y_ps, SBH)
            pool.wait_ge(conv_step, 48)
            for l in range(7):
                k = 1 << l
                m = level[:, l, :]
                then(pool.memset(m, 0.0))
                half = m.rearrange("p (a b r) -> p a b r", b=2, r=k)[:, :, 1, :]
                then(pool.memset(half, 1.0))
                then(pool.affine_select(out=half, in_=half, compare_op=ALU.is_ge, fill=0.0, base=0,
                                        pattern=[[-2 * k, P // (2 * k)], [0, k]], channel_multiplier=1))
                then(pool.affine_select(out=half, in_=half, compare_op=ALU.is_ge, fill=0.0, base=k - 1,
                                        pattern=[[2 * k, P // (2 * k)], [0, k]], channel_multiplier=-1))
            def each(t):
                return t.unsqueeze(1).to_broadcast([P, DNH, P])

            for pair in range(NB // 2):
                for b in (2 * pair, 2 * pair + 1):
                    pool.wait_ge(dec_exp, b + 1)
                    dec = heads(work[:, b % 2, :])
                    pool.tensor_tensor(dec, dec, each(upto[:, :]), ALU.mult).then_inc(dec_masked, 1)
                for b in (2 * pair, 2 * pair + 1):
                    pool.wait_ge(sys_ready, b + 1)
                    pool.tensor_tensor(link[:, b % 2], sys_t[:, b % 2], each(level[:, 0, :]), ALU.mult)\
                        .then_inc(link_ready, 1)
                    pool.wait_ge(link_ready, 14 * pair + b % 2 + 1)
                    pool.tensor_tensor(inv_t[:, b % 2], each(ident[:, :]), link[:, b % 2], ALU.subtract)\
                        .then_inc(inv_t0, 1)
                for l in range(1, 7):
                    for b in (2 * pair, 2 * pair + 1):
                        if l == 1:
                            pool.wait_ge(inv_t0, b + 1)
                        else:
                            pool.wait_ge(prod_ps, 12 * pair + 2 * (l - 2) + b % 2 + 1)
                        pool.tensor_tensor(link[:, b % 2], sys_t[:, b % 2], each(level[:, l, :]), ALU.mult)\
                            .then_inc(link_ready, 1)

            sum_squares(2)

        @block.scalar
        def _(act):
            def split_hi(phase, i, u):
                n = phase + 4 * i + u
                if is_static(i) and n >= UNITS:
                    return
                slot, k = (phase + u) % RAW, unit_chunks(n) if is_static(i) else unit_chunks(phase)
                act.wait_ge(raw_in[slot], 32 * ((phase + u) // RAW + i + 1))
                if not is_static(n) or n >= 2:
                    act.wait_ge(unit_done, n - 1)
                act.activation(w_hi[:, slot % 2, 0:k, :], raw[:, slot, 0:k, :], ACT.Copy).then_inc(hi_ready, 1)

            def squares(s, o, k):
                act.wait_ge(h_ready, KD * s + o + 1)
                if not is_static(o) or s > 0 or o >= 2:
                    act.wait_ge(ssq_step, (KD - 1) * s + o - 1)
                act.activation(work[:, k, :], hT[:, ds(o, 1), :].rearrange("p a s -> p (a s)"),
                               ACT.Square).then_inc(sq_ready, 1)

            def root(dst, b, done):
                act.activation(dst[:, :], bank(b), ACT.Sqrt, bias=eps[:, 0:1]).then_inc(done, 1)

            def norm_hi(s):
                act.wait_ge(stat_ps, s + 1)
                root(rstd, 4, root_ready)
                for k in range(KD):
                    act.wait_ge(normed_ready, KD * s + k + 1)
                    act.activation(u_hi[:, k, :], work[:, k % 2, :], ACT.Identity,
                                   bias=mod[:, SH[s] * KD + k:SH[s] * KD + k + 1]).then_inc(u_hi_ready, 1)

            def ffn(f, phase):
                for i in laps(act, KF // 2):
                    for jj in range(2):
                        j = 2 * i + jj
                        split_hi(phase, i, 2 * jj + 2)
                        act.wait_ge(unit_done, phase + 2 * j + 1)
                        if not is_static(j) or f or j:
                            act.wait_ge(glu_ready, KF * f + j)
                        act.activation(work[:, 0, :], bank(2 * jj), ACT.Silu).then_inc(silu_ready, 1)
                        split_hi(phase, i, 2 * jj + 3)
                        act.wait_ge(glu_ready, KF * f + j + 1)
                        act.activation(g_hi[:, ds(j, 1), :], work[:, 1:2, :], ACT.Copy).then_inc(g_hi_ready, 1)

            act.wait_ge(masks, 10)
            act.wait_ge(vec_ps, 1)
            act.activation(vec[:, :], bank(7)[:, 0:104], ACT.Copy).then_inc(vec_ready, 1)
            act.activation(vec2[:, :], bank(7)[:, 128:179], ACT.Copy).then_inc(vec_ready, 1)
            act.wait_ge(vec_ready, 2)
            act.activation(cond[:, :], vec[:, 0:KD], ACT.Silu).then_inc(cond_ready, 1)
            for k in range(KD):
                act.wait_ge(x_ps, k + 1)
                act.activation(hT[:, k, :], bank(k % 4), ACT.Copy).then_inc(h_ready, 1)
                squares(0, k, k % 2)
            split_hi(F1_IN, 0, 0)
            split_hi(F1_IN, 0, 1)
            norm_hi(0)
            ffn(0, F1_IN)
            for i in laps(act, KD // 2, 0, 1):
                for oo in range(2):
                    split_hi(F1_OUT, i, 2 * oo + 2)
                    split_hi(F1_OUT, i, 2 * oo + 3)
                    squares(1, 2 * i + oo, oo)

            norm_hi(1)

            def evacuate(p, unit, dst):
                act.wait_ge(unit_done, unit + 1)
                act.activation(dst, bank(6 + p % 2), ACT.Copy).then_inc(proj_ready, 1)

            with act.Fori(0, 3) as i:
                for u in range(4):
                    split_hi(SB_IN, i, u + 2)
                    act.wait_ge(unit_done, SB_IN + 4 * i + u + 1)
                    act.activation(sb_T[:, ds(4 * i + u, 1), :], bank(6 + u % 2), ACT.Copy).then_inc(proj_ready, 1)

            def dn_unit(d):
                split_hi(DN_IN + d + 2, 0, 0)
                act.wait_ge(unit_done, DN_IN + d + 1)
                if d == 0:
                    act.activation(ab_T[:, :], bank(6)[0:2 * DNH, :], ACT.Copy).then_inc(proj_ready, 1)
                    return
                if d == 1:
                    act.wait_ge(pad_zero, 1)
                if d >= 3:
                    act.wait_ge(conv_step, 4 * (d - 2))
                act.activation(pad[:, d % 2, TAPS - 1:], bank(6 + d % 2), ACT.Copy).then_inc(proj_ready, 1)

            for d in range(4):
                for r in (2 * d, 2 * d + 1):
                    if r >= 2:
                        act.wait_ge(qk_stat, r - 1)
                    act.activation(work[:, r % 2, :], sb_T[:, QK[r], :], ACT.Square).then_inc(qk_sq, 1)
                dn_unit(d)
                for r in (2 * d, 2 * d + 1):
                    act.wait_ge(qk_stat, r + 1)
                    if r >= 2:
                        act.wait_ge(qk_ready, r - 1)
                    root((ssq, rstd)[r % 2], r % 4, qk_root)
            for b in range(NB):
                act.wait_ge(vt_ps, b + 1)
                act.activation(v_nat[:, b, :], bank(4 + b % 2), ACT.Copy).then_inc(v_nat_ready, 1)

            def softplus_parts(h):
                e = h % 2
                act.wait_ge(z_ps, h + 1)
                if h >= 2:
                    act.wait_ge(y_ps, h - 1)
                act.activation(att_a[:, e, :], region[e][:, 0:1280], ACT.Abs).then_inc(soft_step, 1)
                act.wait_ge(soft_step, 3 * h + 1)
                act.activation(att_a[:, e, :], att_a[:, e, :], ACT.Exp, scale=-1.0).then_inc(soft_step, 1)
                act.wait_ge(soft_step, 3 * h + 2)
                act.activation(att_a[:, e, :], att_a[:, e, :], ACT.Ln, bias=1.0).then_inc(soft_step, 1)

            softplus_parts(0)
            softplus_parts(1)
            for h in range(SBH):
                act.wait_ge(logw_ready, h + 1)
                act.activation(att_a[:, h % 2, :], att_a[:, h % 2, :], ACT.Exp).then_inc(w_raw, 1)
                dn_unit(4 + h + (h > 0))
                act.wait_ge(y_ps, h + 1)
                rows_h = slice(SBD * (h % 2), SBD * (h % 2) + SBD)
                act.activation(ysb_hi[rows_h, h // 2, :], region[h % 2][rows_h, 0:S], ACT.Copy).then_inc(y_hi_ready, 1)
                if h == 0:
                    dn_unit(5)
                if h + 2 < SBH:
                    softplus_parts(h + 2)

            for m in range(DNH):
                for r, cc in ((2 * m, 4 + m), (2 * m + 1, m)):
                    act.wait_ge(conv_step, 48)
                    act.activation(conv[:, cc, :], conv[:, cc, :], ACT.Silu).then_inc(dn_silu, 1)
            for m in range(DNH):
                act.activation(conv[:, 8 + m, :], conv[:, 8 + m, :], ACT.Silu).then_inc(dn_silu, 1)
            for m in range(DNH):
                for r, cc in ((2 * m, 4 + m), (2 * m + 1, m)):
                    act.wait_ge(dn_silu, r + 1)
                    if r >= 2:
                        act.wait_ge(l2_stat, r - 1)
                    act.activation(work[:, r % 2, :], conv[:, cc, :], ACT.Square).then_inc(l2_sq, 1)
                split_hi(DN_IN + 13 + m + 2, 0, 0)
                act.wait_ge(unit_done, DN_IN + 13 + m + 1)
                act.activation(z_gate[:, m, :], bank(6 + (13 + m) % 2), ACT.Copy).then_inc(proj_ready, 1)
                for r in (2 * m, 2 * m + 1):
                    act.wait_ge(l2_stat, r + 1)
                    if r >= 2:
                        act.wait_ge(l2_ready, r - 1)
                    root((ssq, rstd)[r % 2], r % 4, l2_root)
            act.wait_ge(proj_ready, 12 + 17)
            act.activation(z_gate[:, :, :], z_gate[:, :, :], ACT.Silu).then_inc(z_silu, 1)
            act.wait_ge(ab_ps, 1)
            ab = bank(4)[:, 0:NB * 2 * DNH].rearrange("p (b c) -> p b c", b=NB)
            act.activation(small["beta"], ab[:, :, 0:DNH], ACT.Sigmoid).then_inc(gate_act, 1)
            act.wait_ge(gate_dve, 2)
            act.activation(small["exp"], small["abs"], ACT.Exp, scale=-1.0).then_inc(gate_act, 1)
            act.wait_ge(gate_act, 2)
            act.activation(small["log"], small["exp"], ACT.Ln, bias=1.0).then_inc(gate_act, 1)
            act.wait_ge(rates_in, 32)
            act.activation(rate[:, :], alog_dt[:, 0, :], ACT.Exp).then_inc(gate_act, 1)
            act.wait_ge(gsum_ps, 1)
            gsum = bank(5)[:, 0:NB * DNH].rearrange("p (b h) -> p b h", b=NB)
            act.activation(small["gsum"], gsum, ACT.Copy).then_inc(gsum_act, 1)
            act.activation(small["gexp"], gsum, ACT.Exp).then_inc(gsum_act, 1)
            for q in range(NB):
                act.wait_ge(nat_ps, 2 * q + 1)
                act.activation(k_dn[:, q], heads(bank(2 * (q % 2))), ACT.Copy).then_inc(nat_ready, 1)

            for pair in range(NB // 2):
                both = (2 * pair, 2 * pair + 1)
                for b in both:
                    e = b % 2
                    dec = work[:, e, :]
                    act.wait_ge(dec_raw, b + 1)
                    act.activation(dec, dec, ACT.Exp).then_inc(dec_exp, 1)
                    act.wait_ge(prep_ps, b + 1)
                    act.activation(inv[:, e], heads(region[e][:, 0:S]), ACT.Exp).then_inc(gexp_ready, 1)
                    act.wait_ge(glast_ready, b + 1)
                    act.activation(small["kdec"][:, b], small["kdec"][:, b], ACT.Exp).then_inc(kdec_exp, 1)
                for b in both:
                    act.wait_ge(inv0_ps, b + 1)
                    act.activation(inv[:, b % 2], heads(region[b % 2][:, 0:S]), ACT.Copy).then_inc(inv0_ready, 1)
                for l in range(1, 7):
                    for b in both:
                        act.wait_ge(prod_ps, 12 * pair + 2 * (l - 1) + b % 2 + 1)
                        act.activation(prod[:, b % 2], heads(region[b % 2][:, 0:S]), ACT.Copy).then_inc(prod_ready, 1)
                for b in both:
                    act.wait_ge(corr_ps, 12 * pair + 10 + b % 2 + 1)
                    for h in range(DNH):
                        ins = act.activation(prod[:, b % 2, h], k_dn[:, b, h], ACT.Copy,
                                             scale=small["gexp"][:, b, h:h + 1])
                    ins.then_inc(kexp_ready, 1)
                    act.wait_ge(kexp_ready, b + 1)
                    for h in range(DNH):
                        ins = act.activation(k_dn[:, b, h], k_dn[:, b, h], ACT.Copy,
                                             scale=small["kdec"][:, b, h:h + 1])
                    ins.then_inc(kdec_ready, 1)
                for b in both:
                    act.wait_ge(uw_ps, b + 1)
                    for h in range(DNH):
                        ins = act.activation(v_dn[:, b, h], region[b % 2][:, h * P:(h + 1) * P], ACT.Copy,
                                             scale=small["beta"][:, b, h:h + 1])
                    ins.then_inc(u_ready, 1)
                for b in both:
                    act.wait_ge(o_ps, b + 1)
                    act.activation(conv[:, 8:12, b * P:(b + 1) * P], heads(region[b % 2][:, 0:S]),
                                   ACT.Copy).then_inc(o_ready, 1)

            for h in range(DNH):
                act.wait_ge(o_ready, NB)
                if h >= 2:
                    act.wait_ge(on_stat, h - 1)
                act.activation(work[:, h % 2, :], conv[:, 8 + h, :], ACT.Square).then_inc(on_sq, 1)
                if h:
                    act.wait_ge(on_stat, h)
                    if h >= 3:
                        act.wait_ge(on_scaled, h - 2)
                    root((ssq, rstd)[(h - 1) % 2], h - 1, on_root)
            act.wait_ge(on_stat, DNH)
            act.wait_ge(on_scaled, DNH - 2)
            root(rstd, DNH - 1, on_root)
            for h in range(DNH):
                act.wait_ge(on_gated, h + 1)
                act.activation(ydn_hi[:, h, :], conv[:, 8 + h, :], ACT.Copy).then_inc(ydn_hi_ready, 1)

            act.wait_ge(branch_lo, DNH)
            with act.Fori(0, 2) as i:
                for oo in range(4):
                    e = oo % 2
                    split_hi(MERGE, 3 * i, 3 * oo + 2)
                    act.wait_ge(unit_done, MERGE + 12 * i + 3 * oo + 1)
                    act.wait_ge(branch_lo, DNH + 4 * i + oo)
                    act.activation(work[:, 0, :], bank(3 * e), ACT.Sigmoid).then_inc(sig_ready, 1)
                    split_hi(MERGE, 3 * i, 3 * oo + 3)
                    act.wait_ge(unit_done, MERGE + 12 * i + 3 * oo + 2)
                    act.activation(work[:, 1, :], bank(3 * e + 1), ACT.Sigmoid).then_inc(sig_ready, 1)
                    split_hi(MERGE, 3 * i, 3 * oo + 4)
                    act.wait_ge(sum_ready, 4 * i + oo + 1)
                    act.activation(m_hi[:, ds(4 * i + oo, 1), :], ssq[:, :].unsqueeze(1), ACT.Copy).then_inc(m_hi_ready, 1)
            with act.Fori(0, 2) as i:
                for u in range(4):
                    split_hi(W_OUT, i, u + 2)
                    squares(2, 4 * i + u, u % 2)
            norm_hi(2)
            ffn(1, F2_IN)

            def store(o, k, before):
                act.wait_ge(out_ps, o + 1)
                if before > 0:
                    act.wait_ge(out_done[k], 16 * before)
                act.activation(out_nat[:, k], bank(k).rearrange("p (b n) -> p b n", b=NB), ACT.Copy)\
                    .then_inc(out_ready, 1)
                act.wait_ge(out_ready, o + 1)
                act.dma_start(out_nat_cols[:, :, ds(o * P, P)], out_nat[:, k]).then_inc(out_done[k], 16)

            for i in range(KD // 2):
                for oo in range(2):
                    split_hi(F2_OUT, i, 2 * oo + 2)
                    split_hi(F2_OUT, i, 2 * oo + 3)
                    o = 2 * i + oo
                    if o > 0:
                        store(o - 1, 1 - oo, i - 1 + oo)
            store(KD - 1, 1, KD // 2 - 1)
            act.wait_ge(out_done[0], 16 * KD // 2)
            act.wait_ge(out_done[1], 16 * KD // 2)


        @block.vector
        def _(dve):
            def split_lo(phase, i, u):
                n = phase + 4 * i + u
                if is_static(i) and n >= UNITS:
                    return
                slot, k = (phase + u) % RAW, unit_chunks(n) if is_static(i) else unit_chunks(phase)
                dve.wait_ge(hi_ready, n + 1)
                dve.tensor_tensor(w_lo[:, slot % 2, 0:k, :], raw[:, slot, 0:k, :],
                                  w_hi[:, slot % 2, 0:k, :].bitcast(f32), ALU.subtract).then_inc(lo_ready, 1)

            def ada_piece(q, k2, raw_piece):
                for k in range(KD):
                    if k == 0:
                        ins = dve.tensor_scalar(ada_acc[:, k2, :], raw_piece[:, 0, :], cond[:, 0:1], None, ALU.mult)
                    else:
                        dve.wait_ge(ada_step, KD * q + k)
                        ins = dve.scalar_tensor_tensor(ada_acc[:, k2, :], raw_piece[:, k, :], cond[:, k:k + 1],
                                                       ada_acc[:, k2, :], ALU.mult, ALU.add)
                    ins.then_inc(ada_step, 1)

            def ada_mod(q):
                dve.wait_ge(mod_ps, q + 1)
                dve.tensor_tensor(mod[:, ds(2 * q, 2)], bank(5)[:, 0:2], vec[:, ds(2 * q + KD, 2)],
                                  ALU.add).then_inc(mod_ready, 1)

            def norm(s):
                dve.wait_ge(root_ready, s + 1)
                dve.reciprocal(rstd[:, :], rstd[:, :]).then_inc(rstd_ready, 1)
                dve.wait_ge(mod_ready, (4 * SC[s] + 4) if s else EARLY)
                gain = vec[:, 80 + 8 * s:88 + 8 * s]
                dve.scalar_tensor_tensor(scale_col[:, s, :], mod[:, SC[s] * KD:SC[s] * KD + KD], 1.0, gain,
                                         ALU.add, ALU.mult).then_inc(cols_ready, 1)
                dve.wait_ge(rstd_ready, s + 1)
                dve.wait_ge(cols_ready, 2 * s + 1)

                def low(k):
                    dve.wait_ge(u_hi_ready, KD * s + k + 1)
                    dve.scalar_tensor_tensor(u_lo[:, k, :], work[:, k % 2, :],
                                             mod[:, SH[s] * KD + k:SH[s] * KD + k + 1], u_hi[:, k, :].bitcast(f32),
                                             ALU.add, ALU.subtract).then_inc(u_lo_ready, 1)

                for k in range(KD):
                    if k >= 2:
                        low(k - 2)
                        dve.wait_ge(u_lo_ready, KD * s + k - 1)
                    dve.scalar_tensor_tensor(work[:, k % 2, :], hT[:, k, :], scale_col[:, s, k:k + 1], rstd[:, :],
                                             ALU.mult, ALU.mult).then_inc(normed_ready, 1)
                low(KD - 2)
                low(KD - 1)

            def gate_columns(s, factor):
                dve.wait_ge(mod_ready, 4 * GT[s] + 4)
                dve.tensor_scalar(gate_col[:, s, :], mod[:, GT[s] * KD:GT[s] * KD + KD], factor, None,
                                  ALU.mult).then_inc(cols_ready, 1)
                dve.wait_ge(cols_ready, 2 * s + 2)

            def residual(s, o, b):
                chunk = hT[:, ds(o, 1), :].rearrange("p a s -> p (a s)")
                result = work[:, b - 6, :] if s == 2 else chunk
                dve.scalar_tensor_tensor(result, bank(b), gate_col[:, s, ds(o, 1)], chunk, ALU.mult, ALU.add)\
                    .then_inc(h_ready, 1)

            def ffn_in(f, phase):
                for i in laps(dve, KF // 2):
                    for jj in range(2):
                        j = 2 * i + jj
                        split_lo(phase, i, 2 * jj + 2)
                        if f == 0:
                            dve.wait_ge(ada_in, 16 * (j + 1))
                            ada_piece(EARLY + j, jj, ada_raw)
                        dve.wait_ge(silu_ready, KF * f + j + 1)
                        dve.wait_ge(unit_done, phase + 2 * j + 2)
                        if not is_static(j) or f or j:
                            dve.wait_ge(g_lo_ready, KF * f + j)
                        dve.tensor_tensor(work[:, 1, :], work[:, 0, :], bank(2 * jj + 1), ALU.mult)\
                            .then_inc(glu_ready, 1)
                        split_lo(phase, i, 2 * jj + 3)
                        dve.wait_ge(g_hi_ready, KF * f + j + 1)
                        dve.tensor_tensor(g_lo[:, ds(j, 1), :], work[:, 1:2, :], g_hi[:, ds(j, 1), :].bitcast(f32),
                                          ALU.subtract).then_inc(g_lo_ready, 1)
                        if f == 0:
                            ada_mod(EARLY + j)

            def ffn_out(s, f, phase):
                gate_columns(s, 0.5)
                for i in laps(dve, KD // 2):
                    for oo in range(2):
                        o = 2 * i + oo
                        piece = f == 0 and not (is_static(i) and i == KD // 2 - 1)
                        split_lo(phase, i, 2 * oo + 2)
                        if piece:
                            dve.wait_ge(ada_in, 16 * (KF + o + 1))
                            ada_piece(EARLY + KF + o, oo, ada_raw)
                        split_lo(phase, i, 2 * oo + 3)
                        dve.wait_ge(unit_done, phase + 2 * o + 2)
                        if f and not (is_static(o) and o < 2):
                            dve.wait_ge(out_ps, o - 1)
                        residual(s, o, 6 + oo)
                        if piece:
                            ada_mod(EARLY + KF + o)

            dve.wait_ge(cond_ready, 1)
            for q in range(EARLY):
                dve.wait_ge(ada_early_in[q], 16)
                if q >= 2:
                    ada_mod(q - 2)
                ada_piece(q, q % 2, ada_early[:, q])
            split_lo(F1_IN, 0, 0)
            split_lo(F1_IN, 0, 1)
            ada_mod(EARLY - 2)
            ada_mod(EARLY - 1)
            norm(0)
            ffn_in(0, F1_IN)
            ffn_out(0, 0, F1_OUT)

            norm(1)
            gate_columns(1, 1.0)
            with dve.Fori(0, 3) as i:
                for u in range(4):
                    split_lo(SB_IN, i, u + 2)

            def convolution(d):
                cc = d + 3 if d <= 4 else d - 5 if d <= 8 else d - 1
                dve.wait_ge(proj_ready, 12 + d + 1)
                for t in range(TAPS):
                    tap = vec2[:, 12 * t + cc:12 * t + cc + 1]
                    if t == 0:
                        ins = dve.tensor_scalar(conv[:, cc, :], pad[:, d % 2, 0:S], tap, None, ALU.mult)
                    else:
                        dve.wait_ge(conv_step, 4 * (d - 1) + t)
                        ins = dve.scalar_tensor_tensor(conv[:, cc, :], pad[:, d % 2, t:t + S], tap, conv[:, cc, :],
                                                       ALU.mult, ALU.add)
                    ins.then_inc(conv_step, 1)

            def dn_unit(d):
                split_lo(DN_IN + d + 2, 0, 0)
                if d:
                    convolution(d)

            dve.tensor_scalar(qk_gain[:, 0:1], vec2[:, 49:50], SBD ** -0.5, None, ALU.mult).then_inc(gain_ready, 1)
            dve.tensor_copy(qk_gain[:, 1:2], vec2[:, 50:51]).then_inc(gain_ready, 1)
            dve.wait_ge(gain_ready, 2)
            for d in range(4):
                for r in (2 * d, 2 * d + 1):
                    rs = (ssq, rstd)[r % 2]
                    dve.wait_ge(qk_root, r + 1)
                    dve.reciprocal(rs[:, :], rs[:, :]).then_inc(qk_rs, 1)
                    dve.wait_ge(qk_rs, r + 1)
                    dve.scalar_tensor_tensor(sb_T[:, QK[r], :], sb_T[:, QK[r], :], qk_gain[:, r % 2:r % 2 + 1],
                                             rs[:, :], ALU.mult, ALU.mult).then_inc(qk_ready, 1)
                dn_unit(d)

            def keep_and_beta(h):
                e = h % 2
                z = region[e][:, 0:1280]
                dve.wait_ge(soft_step, 3 * h + 3)
                if h >= 2:
                    dve.wait_ge(later_ps, h - 1)
                dve.scalar_tensor_tensor(att_b[:, e, :], z, 0.0, att_a[:, e, :], ALU.max, ALU.add)\
                    .then_inc(keep_ready, 1)
                dve.wait_ge(keep_ready, h + 1)
                dve.scalar_tensor_tensor(att_a[:, e, :], z, 0.0, att_a[:, e, :], ALU.min, ALU.subtract)\
                    .then_inc(beta_ready, 1)

            keep_and_beta(0)
            keep_and_beta(1)
            for h in range(SBH):
                e = h % 2
                dve.wait_ge(later_ps, h + 1)
                dve.wait_ge(beta_ready, h + 1)
                dve.tensor_tensor(att_a[:, e, :], att_a[:, e, :], region[e][:, 0:1280], ALU.subtract)\
                    .then_inc(logw_ready, 1)
                dn_unit(4 + h + (h > 0))
                dve.wait_ge(y_hi_ready, h + 1)
                rows_h = slice(SBD * e, SBD * e + SBD)
                dve.tensor_tensor(ysb_lo[rows_h, h // 2, :], region[e][rows_h, 0:S],
                                  ysb_hi[rows_h, h // 2, :].bitcast(f32), ALU.subtract).then_inc(y_lo_ready, 1)
                if h == 0:
                    dn_unit(5)
                if h + 2 < SBH:
                    keep_and_beta(h + 2)

            for m in range(DNH):
                for r, cc in ((2 * m, 4 + m), (2 * m + 1, m)):
                    rs = (ssq, rstd)[r % 2]
                    dve.wait_ge(l2_root, r + 1)
                    dve.reciprocal(rs[:, :], rs[:, :]).then_inc(l2_rs, 1)
                    dve.wait_ge(l2_rs, r + 1)
                    dve.scalar_tensor_tensor(conv[:, cc, :], conv[:, cc, :], float(P) ** -0.5 if cc < 4 else 1.0,
                                             rs[:, :], ALU.mult, ALU.mult).then_inc(l2_ready, 1)
                split_lo(DN_IN + 13 + m + 2, 0, 0)
            dve.wait_ge(ab_ps, 1)
            ab = bank(4)[:, 0:NB * 2 * DNH].rearrange("p (b c) -> p b c", b=NB)

            def blocks(t):
                return t.unsqueeze(1).to_broadcast([P, NB, DNH])

            dve.wait_ge(rates_in, 32)
            dve.wait_ge(gate_act, 1)
            dve.tensor_tensor(small["a"], ab[:, :, DNH:], blocks(alog_dt[:, 1, :]), ALU.add).then_inc(gate_dve, 1)
            dve.wait_ge(gate_dve, 1)
            dve.scalar_tensor_tensor(small["abs"], small["a"], -1.0, small["a"], ALU.mult, ALU.max).then_inc(gate_dve, 1)
            dve.tensor_scalar(small["neg_beta"], small["beta"], -1.0, None, ALU.mult).then_inc(gate_dve, 1)
            dve.wait_ge(gate_act, 4)
            dve.scalar_tensor_tensor(small["a"], small["a"], 0.0, small["log"], ALU.max, ALU.add).then_inc(gate_dve, 1)
            dve.wait_ge(gate_dve, 4)
            dve.scalar_tensor_tensor(small["g"], small["a"], -1.0, blocks(rate[:, :]), ALU.mult, ALU.mult)\
                .then_inc(gate_dve, 1)
            for q in range(NB):
                dve.wait_ge(nat_ps, 2 * q + 2)
                dve.tensor_copy(v_dn[:, q], heads(bank(2 * (q % 2) + 1))).then_inc(nat_v_ready, 1)

            for pair in range(NB // 2):
                both = (2 * pair, 2 * pair + 1)
                for b in both:
                    e = b % 2
                    gsums = heads(region[e][:, 0:S])
                    dec = heads(work[:, e, :])
                    dve.wait_ge(prep_ps, b + 1)
                    dve.wait_ge(gsum_act, 2)
                    for h in range(DNH):
                        ins = dve.tensor_scalar(dec[:, h], gsums[:, h], small["gsum"][:, b, h:h + 1], 0.0,
                                                ALU.subtract, ALU.min)
                    ins.then_inc(dec_raw, 1)
                    dve.wait_ge(gexp_ready, b + 1)
                    dve.tensor_tensor(small["kdec"][:, b], gsums[:, :, P - 1], small["gsum"][:, b], ALU.subtract)
                    dve.tensor_copy(small["glast"][:, b], inv[:, e, :, P - 1]).then_inc(glast_ready, 1)
                    queries = conv[:, 0:4, b * P:(b + 1) * P]
                    dve.tensor_tensor(queries, queries, inv[:, e], ALU.mult)
                    dve.wait_ge(dec_masked, b + 1)
                    dve.tensor_tensor(att_t[:, e], heads(region[e][:, 2 * S:3 * S]), dec, ALU.mult)\
                        .then_inc(att_ready, 1)
                    for h in range(DNH):
                        ins = dve.scalar_tensor_tensor(sys_t[:, e, h], region[e][:, S + h * P:S + (h + 1) * P],
                                                       small["beta"][:, b, h:h + 1], dec[:, h], ALU.mult, ALU.mult)
                    ins.then_inc(sys_ready, 1)
                for l in range(1, 7):
                    for b in both:
                        e = b % 2
                        dve.wait_ge(corr_ps, 12 * pair + 2 * (l - 1) + e + 1)
                        if l < 6:
                            dve.tensor_tensor(inv[:, e], inv[:, e], heads(region[e][:, S:2 * S]), ALU.subtract)
                        dve.tensor_tensor(inv_t[:, e], inv_t[:, e], heads(region[e][:, 2 * S:3 * S]),
                                          ALU.subtract).then_inc(inv_ready, 1)
                for b in both:
                    dve.wait_ge(uw_ps, b + 1)
                    dve.tensor_copy(w_t[:, b % 2], heads(region[b % 2][:, S:2 * S])).then_inc(w_ready, 1)
                for b in both:
                    e = b % 2
                    if b == 0:
                        dve.wait_ge(u_ready, 1)
                        dve.tensor_copy(v_new, v_dn[:, 0]).then_inc(v_new_ready, 1)
                        dve.wait_ge(ds_ps, 1)
                        dve.tensor_copy(state, heads(region[e][:, S:2 * S])).then_inc(state_ready, 1)
                        continue
                    dve.wait_ge(ws_ps, b)
                    dve.wait_ge(u_ready, b + 1)
                    for h in range(DNH):
                        ins = dve.scalar_tensor_tensor(v_new[:, h], region[e][:, 2 * S + h * P:2 * S + (h + 1) * P],
                                                       small["neg_beta"][:, b, h:h + 1], v_dn[:, b, h],
                                                       ALU.mult, ALU.add)
                    ins.then_inc(v_new_ready, 1)
                    if b < NB - 1:
                        dve.wait_ge(ds_ps, b + 1)
                        dve.wait_ge(state_ready, b)
                        for h in range(DNH):
                            ins = dve.scalar_tensor_tensor(state[:, h], state[:, h], small["glast"][:, b, h:h + 1],
                                                           region[e][:, S + h * P:S + (h + 1) * P],
                                                           ALU.mult, ALU.add)
                        ins.then_inc(state_ready, 1)

            for h in range(DNH):
                rs = (ssq, rstd)[h % 2]
                dve.wait_ge(on_root, h + 1)
                dve.reciprocal(rs[:, :], rs[:, :]).then_inc(on_rs, 1)
                dve.wait_ge(on_rs, h + 1)
                dve.scalar_tensor_tensor(conv[:, 8 + h, :], conv[:, 8 + h, :], vec2[:, 48:49], rs[:, :],
                                         ALU.mult, ALU.mult).then_inc(on_scaled, 1)
                dve.wait_ge(on_scaled, h + 1)
                dve.wait_ge(z_silu, 1)
                dve.tensor_tensor(conv[:, 8 + h, :], conv[:, 8 + h, :], z_gate[:, h, :], ALU.mult)\
                    .then_inc(on_gated, 1)
            for h in range(DNH):
                dve.wait_ge(ydn_hi_ready, h + 1)
                dve.tensor_tensor(ydn_lo[:, h, :], conv[:, 8 + h, :], ydn_hi[:, h, :].bitcast(f32),
                                  ALU.subtract).then_inc(branch_lo, 1)

            with dve.Fori(0, 2) as i:
                for oo in range(4):
                    e, o = oo % 2, 4 * i + oo
                    split_lo(MERGE, 3 * i, 3 * oo + 2)
                    split_lo(MERGE, 3 * i, 3 * oo + 3)
                    dve.wait_ge(branch_lo, DNH + o)
                    dve.wait_ge(sig_ready, 2 * o + 2)
                    dve.wait_ge(unit_done, MERGE + 12 * i + 3 * oo + 3)
                    dve.tensor_tensor(ssq[:, :], work[:, 0, :], bank(3 * e + 2), ALU.mult).then_inc(part_ready, 1)
                    dve.tensor_tensor(rstd[:, :], work[:, 1, :], bank(6 + e), ALU.mult).then_inc(part_ready, 1)
                    dve.wait_ge(part_ready, 2 * o + 2)
                    dve.tensor_tensor(ssq[:, :], ssq[:, :], rstd[:, :], ALU.add).then_inc(sum_ready, 1)
                    split_lo(MERGE, 3 * i, 3 * oo + 4)
                    dve.wait_ge(m_hi_ready, o + 1)
                    dve.tensor_tensor(m_lo[:, ds(o, 1), :], ssq[:, :].unsqueeze(1), m_hi[:, ds(o, 1), :].bitcast(f32),
                                      ALU.subtract).then_inc(branch_lo, 1)
            with dve.Fori(0, 2) as i:
                for u in range(4):
                    split_lo(W_OUT, i, u + 2)
                    dve.wait_ge(unit_done, W_OUT + 4 * i + u + 1)
                    residual(1, 4 * i + u, 6 + u % 2)
            norm(2)
            ffn_in(1, F2_IN)
            ffn_out(2, 1, F2_OUT)

        @block.tensor
        def _(pe):
            def unit(phase, i, u, b, x_hi, x_lo, x0=0, w0=0, k=KD, start=True, stop=True, ready=None):
                slot = (phase + u) % 2
                if w0 == 0:
                    pe.wait_ge(lo_ready, phase + 4 * i + u + 1)
                for n in range(k):
                    if ready:
                        ready(n)
                    wh, wl = w_hi[:, slot, w0 + n, :], w_lo[:, slot, w0 + n, :]
                    xh, xl = x_hi[:, x0 + n, :], x_lo[:, x0 + n, :]
                    pe.matmul(bank(b), wh, xh, start=start and n == 0, stop=False)
                    pe.matmul(bank(b), wh, xl, start=False, stop=False)
                    ins = pe.matmul(bank(b), wl, xh, start=False, stop=stop and n == k - 1)
                return ins

            def normed_chunks(s):
                return lambda k: pe.wait_ge(u_lo_ready, KD * s + k + 1)

            def statistics(s):
                pe.wait_ge(ssq_step, (KD - 1) * (s + 1))
                pe.matmul(bank(4), mean_d[:, :], ssq[:, :], start=True, stop=False)
                pe.wait_ge(sq_ready, KD * (s + 1))
                pe.matmul(bank(4), mean_d[:, :], work[:, 1, :], start=False, stop=True).then_inc(stat_ps, 1)

            def ada_sum(q, k2):
                pe.wait_ge(ada_step, KD * (q + 1))
                if not is_static(q) or q > 0:
                    pe.wait_ge(mod_ready, q)
                pe.matmul(bank(5)[:, 0:1], ada_acc[:, k2, 0:P], ones[:, 0:1], start=True, stop=True)
                pe.matmul(bank(5)[:, 1:2], ada_acc[:, k2, P:2 * P], ones[:, 0:1], start=True, stop=True)\
                    .then_inc(mod_ps, 1)

            def ffn_in(f, phase):
                for i in laps(pe, KF // 2):
                    for jj in range(2):
                        j = 2 * i + jj
                        if not is_static(j) or f or j >= 2:
                            pe.wait_ge(glu_ready, KF * f + j - 1)
                        for ab in range(2):
                            ready = normed_chunks(2 * f) if is_static(i) and i == 0 and jj == ab == 0 else None
                            unit(phase, i, 2 * jj + ab, 2 * jj + ab, u_hi, u_lo, ready=ready).then_inc(unit_done, 1)
                        if f == 0:
                            ada_sum(EARLY + j, jj)

            def ffn_out(s, f, phase, after):
                def silu_chunks(k):
                    if k == HALF - 1:
                        pe.wait_ge(g_lo_ready, KF * (f + 1))

                for i in laps(pe, KD // 2):
                    for oo in range(2):
                        o = 2 * i + oo
                        pe.wait_ge(h_ready, KD * (s + 1) + o - 1)
                        first = is_static(o) and o == 0
                        if first:
                            pe.wait_ge(g_lo_ready, KF * (f + 1) - 1)
                        unit(phase, i, 2 * oo, 6 + oo, g_hi, g_lo, k=HALF, stop=False).then_inc(unit_done, 1)
                        unit(phase, i, 2 * oo + 1, 6 + oo, g_hi, g_lo, x0=HALF, k=HALF, start=False,
                             ready=silu_chunks if first else None).then_inc(unit_done, 1)
                        after(i, oo)

            pe.wait_ge(masks, 10)
            pe.wait_ge(small_in, 16 * 14)
            pe.transpose(bank(7)[:, 0:104], vec_rows[:, :], ident[0:104, 0:104])
            pe.transpose(bank(7)[:, 128:179], vec2_rows[:, :], ident[0:51, 0:51]).then_inc(vec_ps, 1)
            pe.wait_ge(x_in, 16 * NB)
            for k in range(KD):
                if k >= 4:
                    pe.wait_ge(h_ready, k - 3)
                for b in range(NB):
                    ins = pe.transpose(bank(k % 4)[:, b * P:(b + 1) * P], x_nat[:, b, k * P:(k + 1) * P], ident[:, :])
                ins.then_inc(x_ps, 1)
            statistics(0)
            for q in range(EARLY):
                ada_sum(q, q % 2)
            ffn_in(0, F1_IN)

            def piece_sum(i, oo):
                if not (is_static(i) and i == KD // 2 - 1):
                    ada_sum(EARLY + KF + 2 * i + oo, oo)

            ffn_out(0, 0, F1_OUT, piece_sum)
            statistics(1)

            for i in laps(pe, 3, 1, 0):
                for u in range(4):
                    if not is_static(i) or 4 * i + u >= 2:
                        pe.wait_ge(proj_ready, 4 * i + u - 1)
                    unit(SB_IN, i, u, 6 + u % 2, u_hi, u_lo, ready=normed_chunks(1) if u == 0 else None)\
                        .then_inc(unit_done, 1)

            def dn_unit(d):
                pe.wait_ge(proj_ready, 12 + d - 1)
                unit(DN_IN, 0, d, 6 + d % 2, u_hi, u_lo).then_inc(unit_done, 1)

            pe.wait_ge(proj_ready, 12)
            for d in range(4):
                dn_unit(d)
                for r in (2 * d, 2 * d + 1):
                    pe.wait_ge(qk_sq, r + 1)
                    if r >= 4:
                        pe.wait_ge(qk_root, r - 3)
                    pe.matmul(bank(r % 4), mean_64[:, :], work[:, r % 2, :], start=True, stop=True).then_inc(qk_stat, 1)
            for b in range(NB):
                if b >= 2:
                    pe.wait_ge(v_nat_ready, b - 1)
                for k in range(4):
                    ins = pe.transpose(bank(4 + b % 2)[:, k * P:(k + 1) * P], sb_T[:, 8 + k, b * P:(b + 1) * P],
                                       ident[:, :])
                ins.then_inc(vt_ps, 1)

            def scores(h):
                rows_h = slice(SBD * (h % 2), SBD * (h % 2) + SBD)
                if h >= 2:
                    pe.wait_ge(y_lo_ready, h - 1)
                for j in range(NB):
                    ins = pe.matmul(region[h % 2][:, OFF[j]:OFF[j] + WID[j]],
                                    sb_T[rows_h, 4 + h // 2, j * P:(j + 1) * P], sb_T[rows_h, h // 2, j * P:S],
                                    start=True, stop=True)
                ins.then_inc(z_ps, 1)

            pe.wait_ge(qk_ready, 8)
            pe.wait_ge(v_nat_ready, NB)
            scores(0)
            scores(1)
            for h in range(SBH):
                e = h % 2
                pe.wait_ge(keep_masked, h + 1)
                pe.wait_ge(beta_ready, h + 1)
                for j in range(NB):
                    for j2 in range(j, NB):
                        at = OFF[j] + P * (j2 - j)
                        ins = pe.matmul(region[e][:, at:at + WID[j2]], (below if j2 == j else ones)[:, :],
                                        att_b[:, e, OFF[j2]:OFF[j2] + WID[j2]], start=j2 == j, stop=j2 == NB - 1)
                ins.then_inc(later_ps, 1)
                dn_unit(4 + h + (h > 0))
                pe.wait_ge(w_masked, h + 1)
                for j in range(NB):
                    ins = pe.matmul(region[e][SBD * e:SBD * e + SBD, j * P:S], v_nat[:, j, SBD * h:SBD * h + SBD],
                                    att_a[:, e, OFF[j]:OFF[j] + WID[j]], start=j == 0, stop=j == NB - 1)
                ins.then_inc(y_ps, 1)
                if h == 0:
                    dn_unit(5)
                if h + 2 < SBH:
                    scores(h + 2)

            pe.wait_ge(y_lo_ready, SBH)
            for m in range(DNH):
                dn_unit(13 + m)
                for r in (2 * m, 2 * m + 1):
                    pe.wait_ge(l2_sq, r + 1)
                    if r >= 4:
                        pe.wait_ge(l2_root, r - 3)
                    pe.matmul(bank(r % 4), ones[:, :], work[:, r % 2, :], start=True, stop=True).then_inc(l2_stat, 1)
            for b in range(NB):
                ins = pe.transpose(bank(4)[:, 8 * b:8 * b + 8], ab_T[:, b * P:(b + 1) * P], ident[0:8, 0:8])
            ins.then_inc(ab_ps, 1)
            pe.wait_ge(gate_dve, 5)
            pe.matmul(bank(5)[:, 0:NB * DNH], upto[:, :], small["g"].rearrange("p b h -> p (b h)"),
                      start=True, stop=True).then_inc(gsum_ps, 1)
            pe.wait_ge(l2_ready, 8)
            pe.wait_ge(dn_silu, 12)
            for q in range(NB):
                if q >= 2:
                    pe.wait_ge(nat_ready, q - 1)
                for h in range(DNH):
                    ins = pe.transpose(bank(2 * (q % 2))[:, h * P:(h + 1) * P], conv[:, 4 + h, q * P:(q + 1) * P],
                                       ident[:, :])
                ins.then_inc(nat_ps, 1)
                if q >= 2:
                    pe.wait_ge(nat_v_ready, q - 1)
                for h in range(DNH):
                    ins = pe.transpose(bank(2 * (q % 2) + 1)[:, h * P:(h + 1) * P],
                                       conv[:, 8 + h, q * P:(q + 1) * P], ident[:, :])
                ins.then_inc(nat_ps, 1)

            for pair in range(NB // 2):
                both = (2 * pair, 2 * pair + 1)
                for b in both:
                    e, cols = b % 2, slice(b * P, (b + 1) * P)
                    if b < 2:
                        pe.wait_ge(nat_ready, NB)
                        pe.wait_ge(nat_v_ready, NB)
                        pe.wait_ge(gsum_act, 2)
                    else:
                        pe.wait_ge(o_ready, b - 1)
                        pe.wait_ge(state_ready, b - 1)
                        pe.wait_ge(v_new_ready, b - 1)
                    for h in range(DNH):
                        pe.matmul(region[e][:, h * P:(h + 1) * P], small["g"][:, b, h:h + 1].to_broadcast([P, P]),
                                  upto[:, :], start=True, stop=True)
                    for h in range(DNH):
                        pe.matmul(region[e][:, S + h * P:S + (h + 1) * P], conv[:, 4 + h, cols], conv[:, 4 + h, cols],
                                  start=True, stop=True)
                    for h in range(DNH):
                        ins = pe.matmul(region[e][:, 2 * S + h * P:2 * S + (h + 1) * P], conv[:, 4 + h, cols],
                                        conv[:, h, cols], start=True, stop=True)
                    ins.then_inc(prep_ps, 1)
                for b in both:
                    e = b % 2
                    pe.wait_ge(inv_t0, b + 1)
                    for h in range(DNH):
                        ins = pe.transpose(region[e][:, h * P:(h + 1) * P], inv_t[:, e, h], ident[:, :])
                    ins.then_inc(inv0_ps, 1)
                for l in range(1, 7):
                    for b in both:
                        e = b % 2
                        pe.wait_ge(link_ready, 14 * pair + 2 * l + e + 1)
                        if l == 1:
                            pe.wait_ge(inv0_ready, b + 1)
                        else:
                            pe.wait_ge(inv_ready, 12 * pair + 2 * (l - 2) + e + 1)
                        for h in range(DNH):
                            ins = pe.matmul(region[e][:, h * P:(h + 1) * P], link[:, e, h], inv[:, e, h],
                                            start=True, stop=True)
                        ins.then_inc(prod_ps, 1)
                    for b in both:
                        e = b % 2
                        pe.wait_ge(prod_ready, 12 * pair + 2 * (l - 1) + e + 1)
                        if l < 6:
                            for h in range(DNH):
                                pe.matmul(region[e][:, S + h * P:S + (h + 1) * P], inv_t[:, e, h], prod[:, e, h],
                                          start=True, stop=True)
                        for h in range(DNH):
                            ins = pe.matmul(region[e][:, 2 * S + h * P:2 * S + (h + 1) * P], prod[:, e, h],
                                            inv_t[:, e, h], start=True, stop=True)
                        ins.then_inc(corr_ps, 1)
                for b in both:
                    e = b % 2
                    pe.wait_ge(inv_ready, 12 * pair + 10 + e + 1)
                    pe.wait_ge(kexp_ready, b + 1)
                    for h in range(DNH):
                        pe.matmul(region[e][:, h * P:(h + 1) * P], inv_t[:, e, h], v_dn[:, b, h], start=True, stop=True)
                    for h in range(DNH):
                        ins = pe.matmul(region[e][:, S + h * P:S + (h + 1) * P], prod[:, e, h], inv_t[:, e, h],
                                        start=True, stop=True)
                    ins.then_inc(uw_ps, 1)
                for b in both:
                    e, cols = b % 2, slice(b * P, (b + 1) * P)
                    pe.wait_ge(w_ready, b + 1)
                    pe.wait_ge(u_ready, b + 1)
                    if b:
                        pe.wait_ge(state_ready, b)
                        for h in range(DNH):
                            ins = pe.matmul(region[e][:, 2 * S + h * P:2 * S + (h + 1) * P], w_t[:, e, h],
                                            state[:, h], start=True, stop=True)
                        ins.then_inc(ws_ps, 1)
                    pe.wait_ge(v_new_ready, b + 1)
                    pe.wait_ge(att_ready, b + 1)
                    for h in range(DNH):
                        o_h = region[e][:, h * P:(h + 1) * P]
                        if b:
                            pe.matmul(o_h, state[:, h], conv[:, h, cols], start=True, stop=False)
                        ins = pe.matmul(o_h, v_new[:, h], att_t[:, e, h], start=b == 0, stop=True)
                    ins.then_inc(o_ps, 1)
                    if b < NB - 1:
                        pe.wait_ge(kdec_ready, b + 1)
                        for h in range(DNH):
                            ins = pe.matmul(region[e][:, S + h * P:S + (h + 1) * P], k_dn[:, b, h], v_new[:, h],
                                            start=True, stop=True)
                        ins.then_inc(ds_ps, 1)
            for h in range(DNH):
                pe.wait_ge(on_sq, h + 1)
                pe.matmul(bank(h), mean_p[:, :], work[:, h % 2, :], start=True, stop=True).then_inc(on_stat, 1)

            pe.wait_ge(on_root, DNH)
            with pe.Fori(0, 2) as i:
                for oo in range(4):
                    e = oo % 2
                    pe.wait_ge(branch_lo, DNH + 4 * i + oo - 1)
                    unit(MERGE, 3 * i, 3 * oo, 3 * e, u_hi, u_lo).then_inc(unit_done, 1)
                    unit(MERGE, 3 * i, 3 * oo + 1, 3 * e + 1, u_hi, u_lo).then_inc(unit_done, 1)
                    pe.wait_ge(branch_lo, DNH)
                    unit(MERGE, 3 * i, 3 * oo + 2, 3 * e + 2, ysb_hi, ysb_lo, k=4)
                    unit(MERGE, 3 * i, 3 * oo + 2, 6 + e, ydn_hi, ydn_lo, w0=4, k=4).then_inc(unit_done, 1)
            with pe.Fori(0, 2) as i:
                for u in range(4):
                    pe.wait_ge(h_ready, 2 * KD + 4 * i + u - 1)
                    unit(W_OUT, i, u, 6 + u % 2, m_hi, m_lo,
                         ready=(lambda k: pe.wait_ge(branch_lo, DNH + k + 1)) if u == 0 else None)\
                        .then_inc(unit_done, 1)
            statistics(2)
            ffn_in(1, F2_IN)

            def transpose_out(o, b):
                pe.wait_ge(h_ready, 3 * KD + o + 1)
                if not is_static(o) or o >= 2:
                    pe.wait_ge(out_ready, o - 1)
                for q in range(NB):
                    ins = pe.transpose(bank(b)[:, q * P:(q + 1) * P],
                                       work[:, b, q * P:(q + 1) * P], ident[:, :])
                ins.then_inc(out_ps, 1)

            def transpose_last(i, oo):
                if not (is_static(i) and i == 0 and oo == 0):
                    transpose_out(2 * i + oo - 1, 1 - oo)

            ffn_out(2, 1, F2_OUT, transpose_last)
            transpose_out(KD - 1, 1)


_INS = ["x", "c", "w_ada", "b_ada", "g_ffn1", "w_ffn1_in", "w_ffn1_out", "g_mix", "w_in", "g_q_sb", "g_k_sb", "w_conv",
        "a_log", "dt_bias", "g_dn_out", "w_up_sb", "w_up_dn", "w_out", "g_ffn2", "w_ffn2_in", "w_ffn2_out"]


def kernel(**inputs):
    import numpy as np
    import concourse.bacc as bacc
    from concourse.bass_utils import run_bass_kernel_spmd

    nc = bacc.Bacc("TRN2", target_bir_lowering=False, num_devices=1)
    arrays, args = {}, []
    for name in _INS:
        a = np.ascontiguousarray(inputs[name])
        arrays[f"in_{name}"] = a
        args.append(nc.dram_tensor(f"in_{name}", a.shape, mybir.dt.from_np(a.dtype), kind="ExternalInput").ap())
    out = nc.dram_tensor("out_h", (1, S, D), mybir.dt.float32, kind="ExternalOutput").ap()
    build(nc, *args, out)
    result = run_bass_kernel_spmd(nc, [arrays], core_ids=[0])
    return result.results[0]["out_h"]
```

```python
from contextlib import ExitStack

import concourse.bass as bass
from concourse import mybir

P = 128
S = 512
D = 1024
KD = D // P
FF = 2816
KF = FF // P
HALF = KF // 2
SBH, SBD = 8, 64
DNH = 4
NB = S // P
TAPS = 4
EPS = 1e-6
MODS = 9
PIECE = 256
EARLY = 2 * D // PIECE
LATE = 2 * KD
RAW = 4

F1_IN = 0
F1_OUT = F1_IN + 2 * KF
SB_IN = F1_OUT + 2 * KD
DN_IN = SB_IN + 12
MERGE = DN_IN + 17 + 2 * KD
W_OUT = MERGE + KD
F2_IN = W_OUT + KD
F2_OUT = F2_IN + 2 * KF
UNITS = F2_OUT + 2 * KD

COL_DN = 3 * 512
COL_BA = COL_DN + 4 * 512
COL_RSB = COL_BA + 8
COL_RDN = COL_RSB + D

MIXED = [("ba", 0)] + [m for h in range(4) for m in (("conv", 1 + h), ("conv", 9 + h))] \
    + [m for h in range(4) for m in (("conv", 5 + h), ("gate", h))] \
    + [m for h in range(4) for m in (("z", h),)] + [("gate", g) for g in range(4, 16)]
CONVS = [d for kind, d in MIXED if kind == "conv"]
FILL = {"start": 16, "prep": 12, "inv0": 2, "level": 2, "solve": 4, "solved": 3, "step": 2}


def unit_chunks(n):
    return HALF if F1_OUT <= n < SB_IN or n >= F2_OUT else KD


def conv_chunk(d):
    return d + 3 if d <= 4 else d - 5 if d <= 8 else d - 1


def is_static(i):
    return isinstance(i, int)


def filler(step):
    class Fill:
        chunks, unit = 0, 21

        def __call__(self, point):
            self.chunks += FILL[point]
            while self.unit < len(MIXED) and self.chunks >= KD:
                step(self.unit)
                self.unit, self.chunks = self.unit + 1, self.chunks - KD

        def rest(self):
            for m in range(self.unit, len(MIXED)):
                step(m)
    return Fill()


def laps(engine, count, lo=1, hi=1):
    for i in range(lo):
        yield i
    if count - hi > lo:
        with engine.Fori(lo, count - hi) as i:
            yield i
    for i in range(count - hi, count):
        yield i


def build(nc, x, c, w_ada, b_ada, g_ffn1, w_ffn1_in, w_ffn1_out, g_mix, w_in, g_q_sb, g_k_sb, w_conv,
          a_log, dt_bias, g_dn_out, w_up_sb, w_up_dn, w_out, g_ffn2, w_ffn2_in, w_ffn2_out, out):
    f32, f32r = mybir.dt.float32, mybir.dt.float32r
    ALU, ACT = mybir.AluOpType, mybir.ActivationFunctionType
    ds = bass.ds

    def rows(w):
        return w[0].rearrange("(k p) n -> p k n", p=P)

    w_ada_v, w_in_v = rows(w_ada), rows(w_in)
    ffn_in_v = [rows(w_ffn1_in), rows(w_ffn2_in)]
    ffn_out_v = [rows(w_ffn1_out), rows(w_ffn2_out)]
    up_sb_v, up_dn_v, w_out_v = rows(w_up_sb), rows(w_up_dn), rows(w_out)

    with ExitStack() as ctx:
        def sb(name, shape, dt=f32, stack=ctx):
            return stack.enter_context(nc.sbuf_tensor(name, shape, dt))[tuple(slice(None) for _ in shape)]

        def sem(name):
            return ctx.enter_context(nc.semaphore(name))

        hT = sb("hT", [P, KD, S])
        u_hi, u_lo = sb("u_hi", [P, KD, S], f32r), sb("u_lo", [P, KD, S], f32r)
        raw = sb("raw", [P, RAW, HALF, P])
        w_hi, w_lo = sb("w_hi", [P, 2, HALF, P], f32r), sb("w_lo", [P, 2, HALF, P], f32r)
        ident, ones = sb("ident", [P, P]), sb("ones", [P, P])
        mean_d, mean_p = sb("mean_d", [P, P]), sb("mean_p", [P, P])
        mean_64 = sb("mean_64", [P, P])
        below = sb("below", [P, P])
        above = sb("above", [P, P])
        upto = sb("upto", [P, P])
        vec = sb("vec", [P, 96])
        vec2 = sb("vec2", [P, 51])
        alog_dt = sb("alog_dt", [P, 2, DNH])
        cond = sb("cond", [P, KD])
        qk_gain = sb("qk_gain", [P, 2])
        mod = sb("mod", [P, MODS * KD])
        scale_col = sb("scale_col", [P, 3, KD])
        gate_col = sb("gate_col", [P, 3, KD])
        ada_acc = sb("ada_acc", [P, 2, P])
        eps = sb("eps", [P, 1])
        ssq = sb("ssq", [P, S])
        rstd = sb("rstd", [P, S])
        work = sb("work", [P, 2, S])

        with ExitStack() as s:
            vec_rows = sb("vec_rows", [96, P], stack=s)
            c_rows = sb("c_rows", [KD, P], stack=s)
            vec2_rows = sb("vec2_rows", [51, P], stack=s)
            x_nat = sb("x_nat", [P, NB, D], stack=s)
            ada_early = sb("ada_early", [P, EARLY, KD, PIECE], stack=s)
        with ExitStack() as s:
            g_hi, g_lo = sb("g_hi", [P, KF, S], f32r, stack=s), sb("g_lo", [P, KF, S], f32r, stack=s)
            with ExitStack() as t:
                ada_raw = sb("ada_raw", [P, 2, KD, P], stack=t)
            with ExitStack() as t:
                out_nat = sb("out_nat", [P, 2, NB, P], stack=t)
        with ExitStack() as s:
            ysb_hi, ysb_lo = sb("ysb_hi", [P, 4, S], f32r, stack=s), sb("ysb_lo", [P, 4, S], f32r, stack=s)
            with ExitStack() as t:
                small = {n: sb("dn_" + n, [P, NB, DNH], stack=t) for n in
                         ("beta", "neg_beta", "a", "abs", "exp", "log", "g", "gsum", "gexp", "glast", "kdec")}
                rate = sb("rate", [P, DNH], stack=t)
                conv = sb("conv", [P, 12, S], stack=t)
                ab_T = sb("ab_T", [2 * DNH, S], stack=t)
                with ExitStack() as v:
                    sb_T = sb("sb_T", [P, 12, S], stack=v)
                    v_nat = sb("v_nat", [P, NB, SBH * SBD], stack=v)
                    pad = sb("pad", [P, 2, TAPS - 1 + S], stack=v)
                    att_a, att_b = sb("att_a", [P, 2, 1280], stack=v), sb("att_b", [P, 2, 1280], stack=v)
                with ExitStack() as v:
                    z_gate = sb("z_gate", [P, DNH, S], stack=v)
                    inv, inv_t, sys_t, link, prod = (sb("dn_" + n, [P, 2, DNH, P], stack=v) for n in
                                                    ("inv", "inv_t", "sys_t", "link", "prod"))
                    att_t, w_t = sb("att_t", [P, 2, DNH, P], stack=v), sb("w_t", [P, 2, DNH, P], stack=v)
                    state = sb("state", [P, DNH, P], stack=v)
                    level = sb("level", [P, 7, P], stack=v)
                    with ExitStack() as w:
                        k_dn = sb("k_dn", [P, NB, DNH, P], stack=w)
                        v_dn = sb("v_dn", [P, NB, DNH, P], stack=w)
                    with ExitStack() as w:
                        ydn_hi = sb("ydn_hi", [P, 4, S], f32r, stack=w)
                        ydn_lo = sb("ydn_lo", [P, 4, S], f32r, stack=w)
            with ExitStack() as t:
                m_hi, m_lo = sb("m_hi", [P, KD, S], f32r, stack=t), sb("m_lo", [P, KD, S], f32r, stack=t)
                gates = sb("gates", [P, 2, 2, S], stack=t)
        kept = nc.dram_tensor("kept_gates", (2 * KD, P, S), f32, kind="Internal").ap()

        v_new = ssq[:, :].rearrange("p (h e) -> p h e", h=DNH)
        out_nat_cols = out[0].rearrange("(b p) n -> p b n", p=P)

        region = [ctx.enter_context(nc.psum_tensor(f"region{r}", [P, 3 * S], f32)) for r in range(2)]
        tail = ctx.enter_context(nc.psum_tensor("tail", [P, 2 * S], f32))

        def bank(b):
            t, k = (region[b // 3], b % 3) if b < 6 else (tail, b - 6)
            return t[:, k * S:(k + 1) * S]

        def heads(ap):
            return ap.rearrange("p (h e) -> p h e", h=DNH)

        small_in, rates_in, x_in = sem("small_in"), sem("rates_in"), sem("x_in")
        ada_early_in = [sem(f"ada_early_in{q}") for q in range(EARLY)]
        ada_in = [sem(f"ada_in{k}") for k in range(2)]
        c_in, c_ps, early_step, early_ps, early_mod = (sem("c_in"), sem("c_ps"), sem("early_step"), sem("early_ps"),
                                                       sem("early_mod"))
        gate_stored = sem("gate_stored")
        gates_in = [sem(f"gates_in{k}") for k in range(2)]
        raw_in = [sem(f"raw_in{r}") for r in range(RAW)]
        out_done = [sem(f"out_done{k}") for k in range(2)]
        masks, mask_step = sem("masks"), sem("mask_step")
        vec_ps, vec_ready, cond_ready = sem("vec_ps"), sem("vec_ready"), sem("cond_ready")
        x_ps, h_ready, sq_ready, ssq_step = sem("x_ps"), sem("h_ready"), sem("sq_ready"), sem("ssq_step")
        stat_ps, root_ready, rstd_ready = sem("stat_ps"), sem("root_ready"), sem("rstd_ready")
        cols_ready, normed_ready = sem("cols_ready"), sem("normed_ready")
        u_hi_ready, u_lo_ready = sem("u_hi_ready"), sem("u_lo_ready")
        ada_step, mod_ps, mod_ready = sem("ada_step"), sem("mod_ps"), sem("mod_ready")
        hi_ready, lo_ready, unit_done = sem("hi_ready"), sem("lo_ready"), sem("unit_done")
        silu_ready, glu_ready = sem("silu_ready"), sem("glu_ready")
        g_hi_ready, g_lo_ready = sem("g_hi_ready"), sem("g_lo_ready")
        out_ps, out_ready = sem("out_ps"), sem("out_ready")
        proj_ready, pad_zero, conv_step = sem("proj_ready"), sem("pad_zero"), sem("conv_step")
        qk_sq, qk_stat, qk_root, qk_rs, qk_ready = (sem("qk_sq"), sem("qk_stat"), sem("qk_root"), sem("qk_rs"),
                                                    sem("qk_ready"))
        vt_ps, v_nat_ready = sem("vt_ps"), sem("v_nat_ready")
        gain_ready = sem("gain_ready")
        z_ps, soft_step, keep_ready, keep_masked = sem("z_ps"), sem("soft_step"), sem("keep_ready"), sem("keep_masked")
        beta_ready, later_ps, logw_ready, w_raw, w_masked = (sem("nb_ready"), sem("later_ps"), sem("logw_ready"),
                                                            sem("w_raw"), sem("w_masked"))
        y_ps, y_hi_ready, y_lo_ready = sem("y_ps"), sem("y_hi_ready"), sem("y_lo_ready")
        dn_silu, l2_sq, l2_stat, l2_root, l2_rs, l2_ready = (sem("dn_silu"), sem("l2_sq"), sem("l2_stat"),
                                                             sem("l2_root"), sem("l2_rs"), sem("l2_ready"))
        z_silu = sem("z_silu")
        ab_ps, gate_act, gate_dve, gsum_ps, gsum_act = (sem("ab_ps"), sem("gate_act"), sem("gate_dve"),
                                                        sem("gsum_ps"), sem("gsum_act"))
        nat_ps, nat_ready, nat_v_ready = sem("nat_ps"), sem("nat_ready"), sem("nat_v_ready")
        prep_ps, dec_raw, dec_exp, dec_masked, gexp_ready = (sem("prep_ps"), sem("dec_raw"), sem("dec_exp"),
                                                             sem("dec_masked"), sem("gexp_ready"))
        glast_ready, kdec_exp, sys_ready, att_ready = (sem("glast_ready"), sem("kdec_exp"), sem("sys_ready"),
                                                       sem("att_ready"))
        link_ready, inv_t0, inv0_ps, inv0_ready = sem("link_ready"), sem("inv_t0"), sem("inv0_ps"), sem("inv0_ready")
        prod_ps, prod_ready, corr_ps, inv_ready = sem("prod_ps"), sem("prod_ready"), sem("corr_ps"), sem("inv_ready")
        kexp_ready, kdec_ready, uw_ps, u_ready, w_ready = (sem("kexp_ready"), sem("kdec_ready"), sem("uw_ps"),
                                                           sem("u_ready"), sem("w_ready"))
        ws_ps, v_new_ready, o_ps, o_ready, ds_ps, state_ready = (sem("ws_ps"), sem("v_new_ready"), sem("o_ps"),
                                                                 sem("o_ready"), sem("ds_ps"), sem("state_ready"))
        on_sq, on_stat, on_root, on_rs, on_scaled, on_gated = (sem("on_sq"), sem("on_stat"), sem("on_root"),
                                                               sem("on_rs"), sem("on_scaled"), sem("on_gated"))
        ydn_hi_ready = sem("ydn_hi_ready")
        branch_lo = sem("branch_lo")
        sig_ready, part_ready, sum_ready, m_hi_ready = (sem("sig_ready"), sem("part_ready"), sem("sum_ready"),
                                                        sem("m_hi_ready"))

        SH, SC, GT = [0, 3, 6], [1, 4, 7], [2, 5, 8]
        OFF = [0, 512, 1024, 896]
        WID = [S - P * j for j in range(NB)]
        QK = [0, 4, 1, 5, 2, 6, 3, 7]
        block = ctx.enter_context(nc.Block())

        @block.sync
        def _(sp):
            def source(phase, i, u):
                if is_static(i):
                    n = phase + 4 * i + u
                    phase = max(f for f in (F1_IN, F1_OUT, SB_IN, DN_IN, MERGE, W_OUT, F2_IN, F2_OUT) if f <= n)
                    i, u = 0, n - phase
                f = int(phase >= F2_IN)
                if phase in (F1_IN, F2_IN):
                    v, col, k0, kn = ffn_in_v[f], (4 * i + u - u % 2) * (P // 2) + (u % 2) * FF, 0, KD
                elif phase in (F1_OUT, F2_OUT):
                    v, col, k0, kn = ffn_out_v[f], (4 * i + u - u % 2) * (P // 2), (u % 2) * HALF, HALF
                elif phase == SB_IN:
                    v, col, k0, kn = w_in_v, (u % 2 * 4 + u // 2 if u < 8 else u) * P, 0, KD
                elif phase == DN_IN:
                    v, k0, kn = w_in_v, 0, KD
                    kind, d = MIXED[u]
                    col = {"ba": COL_BA, "z": COL_DN + (12 + d) * P, "gate": COL_RSB + d * P,
                           "conv": COL_DN + P * conv_chunk(d)}[kind]
                elif phase == MERGE:
                    return [(0, 4, up_sb_v[:, :, u * P:u * P + P]), (4, 8, up_dn_v[:, :, u * P:u * P + P])]
                else:
                    v, col, k0, kn = w_out_v, u * P, 0, KD
                cut = kn // 2
                return [(0, cut, v[:, k0:k0 + cut, ds(col, P)]), (cut, kn, v[:, k0 + cut:k0 + kn, ds(col, P)])]

            def load(phase, i, u):
                slot = (phase + u) % RAW
                for a, b, view in source(phase, i, u):
                    sp.dma_start(raw[:, slot, a:b, :], view).then_inc(raw_in[slot], 16)

            def load_next(phase, i, u):
                if is_static(i) and phase + 4 * i + u + RAW >= UNITS:
                    return
                sp.wait_ge(lo_ready, phase + 4 * i + u + 1)
                load(phase, i, u + RAW)

            def load_gates(o):
                for k in range(2):
                    sp.dma_start(gates[:, o % 2, k, :], kept[k * KD + o]).then_inc(gates_in[o % 2], 16)

            sp.dma_start(c_rows[:, :], c[0].rearrange("(k p) -> k p", p=P)).then_inc(c_in, 16)
            sp.dma_start(ada_early[:, 0], w_ada_v[:, :, 0:PIECE]).then_inc(ada_early_in[0], 16)
            for b in range(NB):
                sp.dma_start(x_nat[:, b, :], x[0, b * P:(b + 1) * P, :]).then_inc(x_in, 16)
            for q in range(1, EARLY):
                sp.dma_start(ada_early[:, q], w_ada_v[:, :, q * PIECE:(q + 1) * PIECE]).then_inc(ada_early_in[q], 16)
            sp.dma_start(vec_rows[0:72, :], b_ada[0].rearrange("(k p) -> k p", p=P)).then_inc(small_in, 16)
            for n, g in enumerate((g_ffn1, g_mix, g_ffn2)):
                sp.dma_start(vec_rows[72 + 8 * n:80 + 8 * n, :], g[0].rearrange("(k p) -> k p", p=P)).then_inc(small_in, 16)
            sp.dma_start(vec2_rows[0:48, :], w_conv[0].rearrange("t (k p) -> (t k) p", p=P)).then_inc(small_in, 16)
            sp.dma_start(vec2_rows[48:49, :], g_dn_out).then_inc(small_in, 16)
            for n, g in enumerate((g_q_sb, g_k_sb)):
                for half in range(2):
                    sp.dma_start(vec2_rows[49 + n:50 + n, half * SBD:half * SBD + SBD], g).then_inc(small_in, 16)
            for n, g in enumerate((a_log, dt_bias)):
                sp.dma_start(alog_dt[:, n, :], g[0].partition_broadcast(P)).then_inc(rates_in, 16)
            for u in range(RAW):
                load(F1_IN, 0, u)

            def load_late(q, k):
                if not is_static(q) or q >= 2:
                    sp.wait_ge(ada_step, KD * (q - 1))
                sp.dma_start(ada_raw[:, k], w_ada_v[:, :, ds(P * (LATE + q), P)]).then_inc(ada_in[k], 16)

            for i in laps(sp, KF // 2):
                for u in range(4):
                    load_next(F1_IN, i, u)
                    load_late(4 * i + u, u % 2)
            for i in laps(sp, KD // 2, 0, 1):
                for u in range(4):
                    load_next(F1_OUT, i, u)
                    if not (is_static(i) and i == KD // 2 - 1):
                        load_late(2 * KF + 4 * i + u, u % 2)
            for n in range(SB_IN, F2_IN):
                load_next(n, 0, 0)
                m = n - 2 - DN_IN
                if 0 <= m < len(MIXED) and MIXED[m][0] == "gate":
                    g = MIXED[m][1]
                    sp.wait_ge(proj_ready, 12 + m + 1)
                    sp.dma_start(kept[g], rstd[:, :]).then_inc(gate_stored, 16)
                if n == MERGE + 1:
                    sp.wait_ge(gate_stored, 16 * 2 * KD)
                    sp.wait_ge(on_gated, DNH)
                    load_gates(0)
                    load_gates(1)
                if MERGE + 2 <= n < MERGE + KD:
                    sp.wait_ge(part_ready, 2 * (n - MERGE - 1))
                    load_gates(n - MERGE)
            for phase, steps in ((F2_IN, KF // 2), (F2_OUT, KD // 2)):
                for i in laps(sp, steps, 0, 1):
                    for u in range(4):
                        load_next(phase, i, u)

        @block.gpsimd
        def _(pool):
            steps = [0]

            def then(ins):
                steps[0] += 1
                ins.then_inc(mask_step, 1)
                pool.wait_ge(mask_step, steps[0])

            def triangle(t, base, sign, op):
                then(pool.memset(t, 1.0))
                return pool.affine_select(out=t, in_=t, compare_op=op, fill=0.0, base=base,
                                          pattern=[[sign, P]], channel_multiplier=-sign)

            triangle(ident[:, :], 0, 1, ALU.is_equal).then_inc(masks, 1)
            pool.memset(ones[:, :], 1.0).then_inc(masks, 1)
            pool.memset(eps[:, :], EPS).then_inc(masks, 1)
            pool.memset(mean_d[:, :], 1.0 / D).then_inc(masks, 1)
            pool.memset(mean_p[:, :], 1.0 / P).then_inc(masks, 1)
            then(pool.memset(mean_64[:, :], 1.0 / SBD))
            for half, base, sign in ((mean_64[:, 0:SBD], SBD - 1, -1), (mean_64[:, SBD:P], -SBD, 1)):
                pool.affine_select(out=half, in_=half, compare_op=ALU.is_ge, fill=0.0, base=base,
                                   pattern=[[0, SBD]], channel_multiplier=sign).then_inc(masks, 1)
            triangle(below[:, :], 0, -1, ALU.is_gt).then_inc(masks, 1)
            triangle(above[:, :], 0, 1, ALU.is_gt).then_inc(masks, 1)
            triangle(upto[:, :], 0, 1, ALU.is_ge).then_inc(masks, 1)

            def sum_squares(s):
                for o in range(KD - 1):
                    pool.wait_ge(sq_ready, KD * s + o + 1)
                    if o == 0:
                        pool.tensor_copy(ssq[:, :], work[:, 0, :]).then_inc(ssq_step, 1)
                    else:
                        pool.wait_ge(ssq_step, (KD - 1) * s + o)
                        pool.tensor_tensor(ssq[:, :], ssq[:, :], work[:, o % 2, :], ALU.add).then_inc(ssq_step, 1)

            sum_squares(0)
            sum_squares(1)
            pool.wait_ge(u_lo_ready, 2 * KD)
            pool.memset(pad[:, :, 0:TAPS - 1], 0.0).then_inc(pad_zero, 1)

            def diagonal(t, done):
                for j in range(NB):
                    d = t[:, OFF[j]:OFF[j] + P]
                    ins = pool.tensor_tensor(d, d, above[:, :], ALU.mult)
                ins.then_inc(done, 1)

            for h in range(2):
                pool.wait_ge(keep_ready, h + 1)
                diagonal(att_b[:, h % 2, :], keep_masked)
            for h in range(SBH):
                pool.wait_ge(w_raw, h + 1)
                diagonal(att_a[:, h % 2, :], w_masked)
                if h + 2 < SBH:
                    pool.wait_ge(keep_ready, h + 3)
                    diagonal(att_b[:, h % 2, :], keep_masked)

            pool.wait_ge(y_ps, SBH)
            pool.wait_ge(conv_step, 48)
            for l in range(7):
                k = 1 << l
                m = level[:, l, :]
                then(pool.memset(m, 0.0))
                half = m.rearrange("p (a b r) -> p a b r", b=2, r=k)[:, :, 1, :]
                then(pool.memset(half, 1.0))
                then(pool.affine_select(out=half, in_=half, compare_op=ALU.is_ge, fill=0.0, base=0,
                                        pattern=[[-2 * k, P // (2 * k)], [0, k]], channel_multiplier=1))
                then(pool.affine_select(out=half, in_=half, compare_op=ALU.is_ge, fill=0.0, base=k - 1,
                                        pattern=[[2 * k, P // (2 * k)], [0, k]], channel_multiplier=-1))
            def each(t):
                return t.unsqueeze(1).to_broadcast([P, DNH, P])

            for pair in range(NB // 2):
                for b in (2 * pair, 2 * pair + 1):
                    pool.wait_ge(dec_exp, b + 1)
                    dec = heads(work[:, b % 2, :])
                    pool.tensor_tensor(dec, dec, each(upto[:, :]), ALU.mult).then_inc(dec_masked, 1)
                for b in (2 * pair, 2 * pair + 1):
                    pool.wait_ge(sys_ready, b + 1)
                    pool.tensor_tensor(link[:, b % 2], sys_t[:, b % 2], each(level[:, 0, :]), ALU.mult)\
                        .then_inc(link_ready, 1)
                    pool.wait_ge(link_ready, 14 * pair + b % 2 + 1)
                    pool.tensor_tensor(inv_t[:, b % 2], each(ident[:, :]), link[:, b % 2], ALU.subtract)\
                        .then_inc(inv_t0, 1)
                for l in range(1, 7):
                    for b in (2 * pair, 2 * pair + 1):
                        if l == 1:
                            pool.wait_ge(inv_t0, b + 1)
                        else:
                            pool.wait_ge(prod_ps, 12 * pair + 2 * (l - 2) + b % 2 + 1)
                        pool.tensor_tensor(link[:, b % 2], sys_t[:, b % 2], each(level[:, l, :]), ALU.mult)\
                            .then_inc(link_ready, 1)

            sum_squares(2)

        @block.scalar
        def _(act):
            def split_hi(phase, i, u):
                n = phase + 4 * i + u
                if is_static(i) and n >= UNITS:
                    return
                slot, k = (phase + u) % RAW, unit_chunks(n) if is_static(i) else unit_chunks(phase)
                act.wait_ge(raw_in[slot], 32 * ((phase + u) // RAW + i + 1))
                if not is_static(n) or n >= 2:
                    act.wait_ge(unit_done, n - 1)
                act.activation(w_hi[:, slot % 2, 0:k, :], raw[:, slot, 0:k, :], ACT.Copy).then_inc(hi_ready, 1)

            def squares(s, o, k):
                act.wait_ge(h_ready, KD * s + o + 1)
                if not is_static(o) or s > 0 or o >= 2:
                    act.wait_ge(ssq_step, (KD - 1) * s + o - 1)
                act.activation(work[:, k, :], hT[:, ds(o, 1), :].rearrange("p a s -> p (a s)"),
                               ACT.Square).then_inc(sq_ready, 1)

            def inverse_root(dst, b, done, n):
                act.activation(dst[:, :], bank(b), ACT.Ln, bias=eps[:, 0:1]).then_inc(done, 1)
                act.wait_ge(done, 2 * n + 1)
                act.activation(dst[:, :], dst[:, :], ACT.Exp, scale=-0.5).then_inc(done, 1)

            def norm_hi(s):
                act.wait_ge(stat_ps, s + 1)
                inverse_root(rstd, 4, root_ready, s)
                for k in range(KD):
                    act.wait_ge(normed_ready, KD * s + k + 1)
                    act.activation(u_hi[:, k, :], work[:, k % 2, :], ACT.Identity,
                                   bias=mod[:, SH[s] * KD + k:SH[s] * KD + k + 1]).then_inc(u_hi_ready, 1)

            def ffn(f, phase):
                for i in laps(act, KF // 2):
                    for jj in range(2):
                        j = 2 * i + jj
                        split_hi(phase, i, 2 * jj + 2)
                        act.wait_ge(unit_done, phase + 2 * j + 1)
                        if not is_static(j) or f or j:
                            act.wait_ge(glu_ready, KF * f + j)
                        act.activation(work[:, 0, :], bank(2 * jj), ACT.Silu).then_inc(silu_ready, 1)
                        split_hi(phase, i, 2 * jj + 3)
                        act.wait_ge(glu_ready, KF * f + j + 1)
                        act.activation(g_hi[:, ds(j, 1), :], work[:, 1:2, :], ACT.Copy).then_inc(g_hi_ready, 1)

            act.wait_ge(masks, 10)
            act.wait_ge(c_ps, 1)
            act.activation(cond[:, :], bank(6)[:, 0:KD], ACT.Silu).then_inc(cond_ready, 1)
            for k in range(KD):
                act.wait_ge(x_ps, k + 1)
                act.activation(hT[:, k, :], bank(k % 4), ACT.Copy).then_inc(h_ready, 1)
                squares(0, k, k % 2)
            act.wait_ge(vec_ps, 1)
            act.activation(vec[:, :], bank(7)[:, 0:96], ACT.Copy).then_inc(vec_ready, 1)
            act.activation(vec2[:, :], bank(7)[:, 128:179], ACT.Copy).then_inc(vec_ready, 1)
            split_hi(F1_IN, 0, 0)
            split_hi(F1_IN, 0, 1)
            norm_hi(0)
            ffn(0, F1_IN)
            for i in laps(act, KD // 2, 0, 1):
                for oo in range(2):
                    split_hi(F1_OUT, i, 2 * oo + 2)
                    split_hi(F1_OUT, i, 2 * oo + 3)
                    squares(1, 2 * i + oo, oo)

            norm_hi(1)

            def evacuate(p, unit, dst):
                act.wait_ge(unit_done, unit + 1)
                act.activation(dst, bank(6 + p % 2), ACT.Copy).then_inc(proj_ready, 1)

            def qk_inverse_root(r):
                act.wait_ge(qk_stat, r + 1)
                if r >= 2:
                    act.wait_ge(qk_ready, r - 1)
                inverse_root((ssq, rstd)[r % 2], r % 4, qk_root, r)

            for n in range(12):
                split_hi(SB_IN, 0, n + 2)
                act.wait_ge(unit_done, SB_IN + n + 1)
                act.activation(sb_T[:, n, :], bank(6 + n % 2), ACT.Copy).then_inc(proj_ready, 1)
                if n < 8:
                    if n >= 2:
                        act.wait_ge(qk_stat, n - 1)
                    act.wait_ge(proj_ready, n + 1)
                    act.activation(work[:, n % 2, :], sb_T[:, n, :], ACT.Square).then_inc(qk_sq, 1)
                if 2 <= n < 10:
                    qk_inverse_root(n - 2)

            def mixed(m):
                kind, d = MIXED[m]
                split_hi(DN_IN + m + 2, 0, 0)
                act.wait_ge(unit_done, DN_IN + m + 1)
                b = bank(6 + m % 2)
                if kind == "ba":
                    act.activation(ab_T[:, :], b[0:2 * DNH, :], ACT.Copy).then_inc(proj_ready, 1)
                elif kind == "conv":
                    n = CONVS.index(d)
                    if n < 2:
                        act.wait_ge(pad_zero, 1)
                    else:
                        act.wait_ge(conv_step, 4 * (n - 1))
                    act.activation(pad[:, n % 2, TAPS - 1:], b, ACT.Copy).then_inc(proj_ready, 1)
                elif kind == "z":
                    act.activation(z_gate[:, d, :], b, ACT.Copy).then_inc(proj_ready, 1)
                else:
                    if d:
                        act.wait_ge(gate_stored, 16 * d)
                    act.activation(rstd[:, :], b, ACT.Copy).then_inc(proj_ready, 1)

            mixed(0)
            for b in range(NB):
                act.wait_ge(vt_ps, b + 1)
                act.activation(v_nat[:, b, :], bank(4 + b % 2), ACT.Copy).then_inc(v_nat_ready, 1)
            act.wait_ge(ab_ps, 1)
            ab = bank(3)[:, 0:NB * 2 * DNH].rearrange("p (b c) -> p b c", b=NB)
            act.activation(small["beta"], ab[:, :, 0:DNH], ACT.Sigmoid).then_inc(gate_act, 1)
            act.wait_ge(gate_dve, 2)
            act.activation(small["exp"], small["abs"], ACT.Exp, scale=-1.0).then_inc(gate_act, 1)
            act.wait_ge(gate_act, 2)
            act.activation(small["log"], small["exp"], ACT.Ln, bias=1.0).then_inc(gate_act, 1)
            act.wait_ge(rates_in, 32)
            act.activation(rate[:, :], alog_dt[:, 0, :], ACT.Exp).then_inc(gate_act, 1)
            act.wait_ge(gsum_ps, 1)
            gsum = bank(3)[:, 0:NB * DNH].rearrange("p (b h) -> p b h", b=NB)
            act.activation(small["gsum"], gsum, ACT.Copy).then_inc(gsum_act, 1)
            act.activation(small["gexp"], gsum, ACT.Exp).then_inc(gsum_act, 1)

            def softplus_parts(h):
                e = h % 2
                act.wait_ge(z_ps, h + 1)
                if h >= 2:
                    act.wait_ge(y_ps, h - 1)
                act.activation(att_a[:, e, :], region[e][:, 0:1280], ACT.Abs).then_inc(soft_step, 1)
                act.wait_ge(soft_step, 3 * h + 1)
                act.activation(att_a[:, e, :], att_a[:, e, :], ACT.Exp, scale=-1.0).then_inc(soft_step, 1)
                act.wait_ge(soft_step, 3 * h + 2)
                act.activation(att_a[:, e, :], att_a[:, e, :], ACT.Ln, bias=1.0).then_inc(soft_step, 1)

            softplus_parts(0)
            softplus_parts(1)
            for h in range(SBH):
                act.wait_ge(logw_ready, h + 1)
                act.activation(att_a[:, h % 2, :], att_a[:, h % 2, :], ACT.Exp).then_inc(w_raw, 1)
                mixed(1 + 2 * h)
                act.wait_ge(y_ps, h + 1)
                rows_h = slice(SBD * (h % 2), SBD * (h % 2) + SBD)
                act.activation(ysb_hi[rows_h, h // 2, :], region[h % 2][rows_h, 0:S], ACT.Copy).then_inc(y_hi_ready, 1)
                mixed(2 + 2 * h)
                if h + 2 < SBH:
                    softplus_parts(h + 2)

            fill = filler(mixed)
            for m in range(DNH):
                for r, cc in ((2 * m, 4 + m), (2 * m + 1, m)):
                    act.wait_ge(conv_step, 48)
                    act.activation(conv[:, cc, :], conv[:, cc, :], ACT.Silu).then_inc(dn_silu, 1)
            for m in range(DNH):
                act.activation(conv[:, 8 + m, :], conv[:, 8 + m, :], ACT.Silu).then_inc(dn_silu, 1)
            for m in range(DNH):
                for r, cc in ((2 * m, 4 + m), (2 * m + 1, m)):
                    act.wait_ge(dn_silu, r + 1)
                    if r >= 2:
                        act.wait_ge(l2_stat, r - 1)
                    act.activation(work[:, r % 2, :], conv[:, cc, :], ACT.Square).then_inc(l2_sq, 1)
                mixed(17 + m)
                for r in (2 * m, 2 * m + 1):
                    act.wait_ge(l2_stat, r + 1)
                    if r >= 2:
                        act.wait_ge(l2_ready, r - 1)
                    else:
                        act.wait_ge(gate_stored, 16 * 4)
                    inverse_root((ssq, rstd)[r % 2], r % 4, l2_root, r)
            act.wait_ge(proj_ready, 12 + 21)
            act.activation(z_gate[:, :, :], z_gate[:, :, :], ACT.Silu).then_inc(z_silu, 1)
            act.wait_ge(l2_ready, 8)
            fill("start")
            for q in range(NB):
                act.wait_ge(nat_ps, 2 * q + 1)
                act.activation(k_dn[:, q], heads(bank(2 * (q % 2))), ACT.Copy).then_inc(nat_ready, 1)

            for pair in range(NB // 2):
                both = (2 * pair, 2 * pair + 1)
                for b in both:
                    e = b % 2
                    dec = work[:, e, :]
                    act.wait_ge(dec_raw, b + 1)
                    act.activation(dec, dec, ACT.Exp).then_inc(dec_exp, 1)
                    act.wait_ge(prep_ps, b + 1)
                    act.activation(inv[:, e], heads(region[e][:, 0:S]), ACT.Exp).then_inc(gexp_ready, 1)
                    act.wait_ge(glast_ready, b + 1)
                    act.activation(small["kdec"][:, b], small["kdec"][:, b], ACT.Exp).then_inc(kdec_exp, 1)
                fill("prep")
                for b in both:
                    act.wait_ge(inv0_ps, b + 1)
                    act.activation(inv[:, b % 2], heads(region[b % 2][:, 0:S]), ACT.Copy).then_inc(inv0_ready, 1)
                fill("inv0")
                for l in range(1, 7):
                    for b in both:
                        act.wait_ge(prod_ps, 12 * pair + 2 * (l - 1) + b % 2 + 1)
                        act.activation(prod[:, b % 2], heads(region[b % 2][:, 0:S]), ACT.Copy).then_inc(prod_ready, 1)
                    fill("level")
                for b in both:
                    act.wait_ge(corr_ps, 12 * pair + 10 + b % 2 + 1)
                    for h in range(DNH):
                        ins = act.activation(prod[:, b % 2, h], k_dn[:, b, h], ACT.Copy,
                                             scale=small["gexp"][:, b, h:h + 1])
                    ins.then_inc(kexp_ready, 1)
                    act.wait_ge(kexp_ready, b + 1)
                    for h in range(DNH):
                        ins = act.activation(k_dn[:, b, h], k_dn[:, b, h], ACT.Copy,
                                             scale=small["kdec"][:, b, h:h + 1])
                    ins.then_inc(kdec_ready, 1)
                fill("solve")
                for b in both:
                    act.wait_ge(uw_ps, b + 1)
                    for h in range(DNH):
                        ins = act.activation(v_dn[:, b, h], region[b % 2][:, h * P:(h + 1) * P], ACT.Copy,
                                             scale=small["beta"][:, b, h:h + 1])
                    ins.then_inc(u_ready, 1)
                fill("solved")
                for b in both:
                    fill("step")
                    act.wait_ge(o_ps, b + 1)
                    act.activation(conv[:, 8:12, b * P:(b + 1) * P], heads(region[b % 2][:, 0:S]),
                                   ACT.Copy).then_inc(o_ready, 1)

            fill.rest()
            for h in range(DNH):
                act.wait_ge(o_ready, NB)
                if h >= 2:
                    act.wait_ge(on_stat, h - 1)
                act.activation(work[:, h % 2, :], conv[:, 8 + h, :], ACT.Square).then_inc(on_sq, 1)
                if h:
                    act.wait_ge(on_stat, h)
                    if h >= 3:
                        act.wait_ge(on_scaled, h - 2)
                    if h == 2:
                        act.wait_ge(gate_stored, 16 * 2 * KD)
                    inverse_root((ssq, rstd)[(h - 1) % 2], h - 1, on_root, h - 1)
            act.wait_ge(on_stat, DNH)
            act.wait_ge(on_scaled, DNH - 2)
            inverse_root(rstd, DNH - 1, on_root, DNH - 1)
            for h in range(DNH):
                act.wait_ge(on_gated, h + 1)
                act.activation(ydn_hi[:, h, :], conv[:, 8 + h, :], ACT.Copy).then_inc(ydn_hi_ready, 1)

            act.wait_ge(branch_lo, DNH)
            for i in laps(act, 2, 0, 0):
                for oo in range(4):
                    e, o = oo % 2, 4 * i + oo
                    act.wait_ge(gates_in[e], 32 * (2 * i + oo // 2 + 1))
                    act.activation(gates[:, e], gates[:, e], ACT.Sigmoid).then_inc(sig_ready, 1)
                    split_hi(MERGE, i, oo + 2)
                    act.wait_ge(sum_ready, o + 1)
                    act.activation(m_hi[:, ds(o, 1), :], ssq[:, :].unsqueeze(1), ACT.Copy).then_inc(m_hi_ready, 1)
            with act.Fori(0, 2) as i:
                for u in range(4):
                    split_hi(W_OUT, i, u + 2)
                    squares(2, 4 * i + u, u % 2)
            norm_hi(2)
            ffn(1, F2_IN)

            def store(o, k, before):
                act.wait_ge(out_ps, o + 1)
                if before > 0:
                    act.wait_ge(out_done[k], 16 * before)
                act.activation(out_nat[:, k], bank(k).rearrange("p (b n) -> p b n", b=NB), ACT.Copy)\
                    .then_inc(out_ready, 1)
                act.wait_ge(out_ready, o + 1)
                act.dma_start(out_nat_cols[:, :, ds(o * P, P)], out_nat[:, k]).then_inc(out_done[k], 16)

            for i in range(KD // 2):
                for oo in range(2):
                    split_hi(F2_OUT, i, 2 * oo + 2)
                    split_hi(F2_OUT, i, 2 * oo + 3)
                    o = 2 * i + oo
                    if o > 0:
                        store(o - 1, 1 - oo, i - 1 + oo)
            store(KD - 1, 1, KD // 2 - 1)
            act.wait_ge(out_done[0], 16 * KD // 2)
            act.wait_ge(out_done[1], 16 * KD // 2)


        @block.vector
        def _(dve):
            def split_lo(phase, i, u):
                n = phase + 4 * i + u
                if is_static(i) and n >= UNITS:
                    return
                slot, k = (phase + u) % RAW, unit_chunks(n) if is_static(i) else unit_chunks(phase)
                dve.wait_ge(hi_ready, n + 1)
                dve.tensor_tensor(w_lo[:, slot % 2, 0:k, :], raw[:, slot, 0:k, :],
                                  w_hi[:, slot % 2, 0:k, :].bitcast(f32), ALU.subtract).then_inc(lo_ready, 1)

            def ada_sum(acc, piece, done, q):
                for k in range(KD):
                    if k == 0:
                        ins = dve.tensor_scalar(acc, piece[:, 0, :], cond[:, 0:1], None, ALU.mult)
                    else:
                        dve.wait_ge(done, KD * q + k)
                        ins = dve.scalar_tensor_tensor(acc, piece[:, k, :], cond[:, k:k + 1], acc, ALU.mult, ALU.add)
                    ins.then_inc(done, 1)

            def ada_late(q, k, lap):
                dve.wait_ge(ada_in[k], 16 * (lap + 1))
                ada_sum(ada_acc[:, k, :], ada_raw[:, k], ada_step, q)

            def ada_mod(q):
                dve.wait_ge(mod_ps, q + 1)
                dve.tensor_tensor(mod[:, ds(LATE + q, 1)], bank(5)[:, 0:1], vec[:, ds(LATE + q, 1)],
                                  ALU.add).then_inc(mod_ready, 1)

            def newton(dst, b, tmp, done, n):
                dve.scalar_tensor_tensor(tmp, bank(b), EPS, dst[:, :], ALU.add, ALU.mult).then_inc(done, 1)
                dve.wait_ge(done, 3 * n + 1)
                dve.scalar_tensor_tensor(tmp, tmp, -0.5, dst[:, :], ALU.mult, ALU.mult).then_inc(done, 1)
                dve.wait_ge(done, 3 * n + 2)
                dve.scalar_tensor_tensor(dst[:, :], tmp, 1.5, dst[:, :], ALU.add, ALU.mult).then_inc(done, 1)
                dve.wait_ge(done, 3 * n + 3)

            def norm(s):
                if s:
                    dve.wait_ge(mod_ready, SC[s] * KD + KD - LATE)
                else:
                    dve.wait_ge(early_mod, 1)
                gain = vec[:, 72 + 8 * s:80 + 8 * s]
                dve.scalar_tensor_tensor(scale_col[:, s, :], mod[:, SC[s] * KD:SC[s] * KD + KD], 1.0, gain,
                                         ALU.add, ALU.mult).then_inc(cols_ready, 1)
                dve.wait_ge(root_ready, 2 * s + 2)
                newton(rstd, 4, work[:, 0, :], rstd_ready, s)
                dve.wait_ge(cols_ready, 2 * s + 1)

                def low(k):
                    dve.wait_ge(u_hi_ready, KD * s + k + 1)
                    dve.scalar_tensor_tensor(u_lo[:, k, :], work[:, k % 2, :],
                                             mod[:, SH[s] * KD + k:SH[s] * KD + k + 1], u_hi[:, k, :].bitcast(f32),
                                             ALU.add, ALU.subtract).then_inc(u_lo_ready, 1)

                for k in range(KD):
                    if k >= 2:
                        low(k - 2)
                        dve.wait_ge(u_lo_ready, KD * s + k - 1)
                    dve.scalar_tensor_tensor(work[:, k % 2, :], hT[:, k, :], scale_col[:, s, k:k + 1], rstd[:, :],
                                             ALU.mult, ALU.mult).then_inc(normed_ready, 1)
                low(KD - 2)
                low(KD - 1)

            def gate_columns(s, factor):
                dve.wait_ge(mod_ready, GT[s] * KD + KD - LATE)
                dve.tensor_scalar(gate_col[:, s, :], mod[:, GT[s] * KD:GT[s] * KD + KD], factor, None,
                                  ALU.mult).then_inc(cols_ready, 1)
                dve.wait_ge(cols_ready, 2 * s + 2)

            def residual(s, o, b):
                chunk = hT[:, ds(o, 1), :].rearrange("p a s -> p (a s)")
                result = work[:, b - 6, :] if s == 2 else chunk
                dve.scalar_tensor_tensor(result, bank(b), gate_col[:, s, ds(o, 1)], chunk, ALU.mult, ALU.add)\
                    .then_inc(h_ready, 1)

            def ffn_in(f, phase):
                for i in laps(dve, KF // 2):
                    for jj in range(2):
                        j = 2 * i + jj
                        split_lo(phase, i, 2 * jj + 2)
                        if f == 0:
                            if not is_static(j) or j:
                                ada_mod(2 * j - 1)
                            ada_late(2 * j, 0, j)
                        dve.wait_ge(silu_ready, KF * f + j + 1)
                        dve.wait_ge(unit_done, phase + 2 * j + 2)
                        if not is_static(j) or f or j:
                            dve.wait_ge(g_lo_ready, KF * f + j)
                        dve.tensor_tensor(work[:, 1, :], work[:, 0, :], bank(2 * jj + 1), ALU.mult)\
                            .then_inc(glu_ready, 1)
                        split_lo(phase, i, 2 * jj + 3)
                        dve.wait_ge(g_hi_ready, KF * f + j + 1)
                        dve.tensor_tensor(g_lo[:, ds(j, 1), :], work[:, 1:2, :], g_hi[:, ds(j, 1), :].bitcast(f32),
                                          ALU.subtract).then_inc(g_lo_ready, 1)
                        if f == 0:
                            ada_mod(2 * j)
                            ada_late(2 * j + 1, 1, j)

            def ffn_out(s, f, phase):
                gate_columns(s, 0.5)
                for i in laps(dve, KD // 2):
                    for oo in range(2):
                        o = 2 * i + oo
                        piece = f == 0 and not (is_static(i) and i == KD // 2 - 1)
                        split_lo(phase, i, 2 * oo + 2)
                        if piece or f == 0 and oo == 0:
                            ada_mod(2 * (KF + o) - 1)
                        if piece:
                            ada_late(2 * (KF + o), 0, KF + o)
                        split_lo(phase, i, 2 * oo + 3)
                        dve.wait_ge(unit_done, phase + 2 * o + 2)
                        if f and not (is_static(o) and o < 2):
                            dve.wait_ge(out_ps, o - 1)
                        residual(s, o, 6 + oo)
                        if piece:
                            ada_mod(2 * (KF + o))
                            ada_late(2 * (KF + o) + 1, 1, KF + o)

            dve.wait_ge(cond_ready, 1)
            for q in range(EARLY):
                dve.wait_ge(ada_early_in[q], 16)
                ada_sum(ada_early[:, q, 0, :], ada_early[:, q], early_step, q)
            split_lo(F1_IN, 0, 0)
            split_lo(F1_IN, 0, 1)
            dve.wait_ge(early_ps, 1)
            dve.wait_ge(vec_ready, 2)
            dve.tensor_tensor(mod[:, 0:LATE], bank(5)[:, 0:LATE], vec[:, 0:LATE], ALU.add).then_inc(early_mod, 1)
            dve.wait_ge(early_mod, 1)
            norm(0)
            ffn_in(0, F1_IN)
            ffn_out(0, 0, F1_OUT)

            norm(1)
            gate_columns(1, 1.0)
            dve.tensor_scalar(qk_gain[:, 0:1], vec2[:, 49:50], SBD ** -0.5, None, ALU.mult).then_inc(gain_ready, 1)
            dve.tensor_copy(qk_gain[:, 1:2], vec2[:, 50:51]).then_inc(gain_ready, 1)
            dve.wait_ge(gain_ready, 2)

            for n in range(12):
                split_lo(SB_IN, 0, n + 2)
                if 2 <= n < 10:
                    r = n - 2
                    rs = (ssq, rstd)[r % 2]
                    dve.wait_ge(qk_root, 2 * r + 2)
                    newton(rs, r % 4, att_a[:, 0, 0:S], qk_rs, r)
                    dve.scalar_tensor_tensor(sb_T[:, r, :], sb_T[:, r, :], qk_gain[:, r % 2:r % 2 + 1],
                                             rs[:, :], ALU.mult, ALU.mult).then_inc(qk_ready, 1)

            def mixed(m):
                kind, d = MIXED[m]
                split_lo(DN_IN + m + 2, 0, 0)
                if kind != "conv":
                    return
                n, cc = CONVS.index(d), conv_chunk(d)
                dve.wait_ge(proj_ready, 12 + m + 1)
                for t in range(TAPS):
                    tap = vec2[:, 12 * t + cc:12 * t + cc + 1]
                    if t == 0:
                        ins = dve.tensor_scalar(conv[:, cc, :], pad[:, n % 2, 0:S], tap, None, ALU.mult)
                    else:
                        dve.wait_ge(conv_step, 4 * n + t)
                        ins = dve.scalar_tensor_tensor(conv[:, cc, :], pad[:, n % 2, t:t + S], tap, conv[:, cc, :],
                                                       ALU.mult, ALU.add)
                    ins.then_inc(conv_step, 1)

            mixed(0)
            def blocks(t):
                return t.unsqueeze(1).to_broadcast([P, NB, DNH])

            dve.wait_ge(ab_ps, 1)
            ab = bank(3)[:, 0:NB * 2 * DNH].rearrange("p (b c) -> p b c", b=NB)
            dve.wait_ge(rates_in, 32)
            dve.wait_ge(gate_act, 1)
            dve.tensor_tensor(small["a"], ab[:, :, DNH:], blocks(alog_dt[:, 1, :]), ALU.add).then_inc(gate_dve, 1)
            dve.wait_ge(gate_dve, 1)
            dve.scalar_tensor_tensor(small["abs"], small["a"], -1.0, small["a"], ALU.mult, ALU.max).then_inc(gate_dve, 1)
            dve.tensor_scalar(small["neg_beta"], small["beta"], -1.0, None, ALU.mult).then_inc(gate_dve, 1)
            dve.wait_ge(gate_act, 4)
            dve.wait_ge(gate_dve, 2)
            dve.scalar_tensor_tensor(small["a"], small["a"], 0.0, small["log"], ALU.max, ALU.add).then_inc(gate_dve, 1)
            dve.wait_ge(gate_dve, 4)
            dve.scalar_tensor_tensor(small["g"], small["a"], -1.0, blocks(rate[:, :]), ALU.mult, ALU.mult)\
                .then_inc(gate_dve, 1)

            def keep_and_beta(h):
                e = h % 2
                z = region[e][:, 0:1280]
                dve.wait_ge(soft_step, 3 * h + 3)
                if h >= 2:
                    dve.wait_ge(later_ps, h - 1)
                dve.scalar_tensor_tensor(att_b[:, e, :], z, 0.0, att_a[:, e, :], ALU.max, ALU.add)\
                    .then_inc(keep_ready, 1)
                dve.wait_ge(keep_ready, h + 1)
                dve.scalar_tensor_tensor(att_a[:, e, :], z, 0.0, att_a[:, e, :], ALU.min, ALU.subtract)\
                    .then_inc(beta_ready, 1)

            keep_and_beta(0)
            keep_and_beta(1)
            for h in range(SBH):
                e = h % 2
                dve.wait_ge(later_ps, h + 1)
                dve.wait_ge(beta_ready, h + 1)
                dve.tensor_tensor(att_a[:, e, :], att_a[:, e, :], region[e][:, 0:1280], ALU.subtract)\
                    .then_inc(logw_ready, 1)
                mixed(1 + 2 * h)
                dve.wait_ge(y_hi_ready, h + 1)
                rows_h = slice(SBD * e, SBD * e + SBD)
                dve.tensor_tensor(ysb_lo[rows_h, h // 2, :], region[e][rows_h, 0:S],
                                  ysb_hi[rows_h, h // 2, :].bitcast(f32), ALU.subtract).then_inc(y_lo_ready, 1)
                mixed(2 + 2 * h)
                if h + 2 < SBH:
                    keep_and_beta(h + 2)

            fill = filler(mixed)
            tmp = prod[:, 0].rearrange("p h e -> p (h e)")
            for m in range(DNH):
                mixed(17 + m)
                for r, cc in ((2 * m, 4 + m), (2 * m + 1, m)):
                    rs = (ssq, rstd)[r % 2]
                    dve.wait_ge(l2_root, 2 * r + 2)
                    newton(rs, r % 4, tmp, l2_rs, r)
                    dve.scalar_tensor_tensor(conv[:, cc, :], conv[:, cc, :], float(P) ** -0.5 if cc < 4 else 1.0,
                                             rs[:, :], ALU.mult, ALU.mult).then_inc(l2_ready, 1)
            fill("start")
            for q in range(NB):
                dve.wait_ge(nat_ps, 2 * q + 2)
                dve.tensor_copy(v_dn[:, q], heads(bank(2 * (q % 2) + 1))).then_inc(nat_v_ready, 1)

            for pair in range(NB // 2):
                both = (2 * pair, 2 * pair + 1)
                for b in both:
                    e = b % 2
                    gsums = heads(region[e][:, 0:S])
                    dec = heads(work[:, e, :])
                    dve.wait_ge(prep_ps, b + 1)
                    dve.wait_ge(gsum_act, 2)
                    for h in range(DNH):
                        ins = dve.tensor_scalar(dec[:, h], gsums[:, h], small["gsum"][:, b, h:h + 1], 0.0,
                                                ALU.subtract, ALU.min)
                    ins.then_inc(dec_raw, 1)
                    dve.wait_ge(gexp_ready, b + 1)
                    dve.tensor_tensor(small["kdec"][:, b], gsums[:, :, P - 1], small["gsum"][:, b], ALU.subtract)
                    dve.tensor_copy(small["glast"][:, b], inv[:, e, :, P - 1]).then_inc(glast_ready, 1)
                    queries = conv[:, 0:4, b * P:(b + 1) * P]
                    dve.tensor_tensor(queries, queries, inv[:, e], ALU.mult)
                    dve.wait_ge(dec_masked, b + 1)
                    dve.tensor_tensor(att_t[:, e], heads(region[e][:, 2 * S:3 * S]), dec, ALU.mult)\
                        .then_inc(att_ready, 1)
                    for h in range(DNH):
                        ins = dve.scalar_tensor_tensor(sys_t[:, e, h], region[e][:, S + h * P:S + (h + 1) * P],
                                                       small["beta"][:, b, h:h + 1], dec[:, h], ALU.mult, ALU.mult)
                    ins.then_inc(sys_ready, 1)
                fill("prep")
                fill("inv0")
                for l in range(1, 7):
                    for b in both:
                        e = b % 2
                        dve.wait_ge(corr_ps, 12 * pair + 2 * (l - 1) + e + 1)
                        if l < 6:
                            dve.tensor_tensor(inv[:, e], inv[:, e], heads(region[e][:, S:2 * S]), ALU.subtract)
                        dve.tensor_tensor(inv_t[:, e], inv_t[:, e], heads(region[e][:, 2 * S:3 * S]),
                                          ALU.subtract).then_inc(inv_ready, 1)
                    fill("level")
                fill("solve")
                for b in both:
                    dve.wait_ge(uw_ps, b + 1)
                    dve.tensor_copy(w_t[:, b % 2], heads(region[b % 2][:, S:2 * S])).then_inc(w_ready, 1)
                fill("solved")
                for b in both:
                    e = b % 2
                    if b == 0:
                        dve.wait_ge(u_ready, 1)
                        dve.tensor_copy(v_new, v_dn[:, 0]).then_inc(v_new_ready, 1)
                        fill("step")
                        dve.wait_ge(ds_ps, 1)
                        dve.tensor_copy(state, heads(region[e][:, S:2 * S])).then_inc(state_ready, 1)
                        continue
                    dve.wait_ge(ws_ps, b)
                    dve.wait_ge(u_ready, b + 1)
                    for h in range(DNH):
                        ins = dve.scalar_tensor_tensor(v_new[:, h], region[e][:, 2 * S + h * P:2 * S + (h + 1) * P],
                                                       small["neg_beta"][:, b, h:h + 1], v_dn[:, b, h],
                                                       ALU.mult, ALU.add)
                    ins.then_inc(v_new_ready, 1)
                    fill("step")
                    if b < NB - 1:
                        dve.wait_ge(ds_ps, b + 1)
                        dve.wait_ge(state_ready, b)
                        for h in range(DNH):
                            ins = dve.scalar_tensor_tensor(state[:, h], state[:, h], small["glast"][:, b, h:h + 1],
                                                           region[e][:, S + h * P:S + (h + 1) * P],
                                                           ALU.mult, ALU.add)
                        ins.then_inc(state_ready, 1)

            fill.rest()
            for h in range(DNH):
                rs = (ssq, rstd)[h % 2]
                dve.wait_ge(on_root, 2 * h + 2)
                newton(rs, h, tmp, on_rs, h)
                dve.scalar_tensor_tensor(conv[:, 8 + h, :], conv[:, 8 + h, :], vec2[:, 48:49], rs[:, :],
                                         ALU.mult, ALU.mult).then_inc(on_scaled, 1)
                dve.wait_ge(on_scaled, h + 1)
                dve.wait_ge(z_silu, 1)
                dve.tensor_tensor(conv[:, 8 + h, :], conv[:, 8 + h, :], z_gate[:, h, :], ALU.mult)\
                    .then_inc(on_gated, 1)
            for h in range(DNH):
                dve.wait_ge(ydn_hi_ready, h + 1)
                dve.tensor_tensor(ydn_lo[:, h, :], conv[:, 8 + h, :], ydn_hi[:, h, :].bitcast(f32),
                                  ALU.subtract).then_inc(branch_lo, 1)

            with dve.Fori(0, 2) as i:
                for oo in range(4):
                    e, o = oo % 2, 4 * i + oo
                    split_lo(MERGE, i, oo + 2)
                    dve.wait_ge(branch_lo, DNH + o)
                    dve.wait_ge(sig_ready, o + 1)
                    dve.wait_ge(unit_done, MERGE + o + 1)
                    dve.tensor_tensor(ssq[:, :], gates[:, e, 0, :], bank(2 * e), ALU.mult).then_inc(part_ready, 1)
                    dve.tensor_tensor(rstd[:, :], gates[:, e, 1, :], bank(2 * e + 1), ALU.mult).then_inc(part_ready, 1)
                    dve.wait_ge(part_ready, 2 * o + 2)
                    dve.tensor_tensor(ssq[:, :], ssq[:, :], rstd[:, :], ALU.add).then_inc(sum_ready, 1)
                    dve.wait_ge(m_hi_ready, o + 1)
                    dve.tensor_tensor(m_lo[:, ds(o, 1), :], ssq[:, :].unsqueeze(1), m_hi[:, ds(o, 1), :].bitcast(f32),
                                      ALU.subtract).then_inc(branch_lo, 1)
            with dve.Fori(0, 2) as i:
                for u in range(4):
                    split_lo(W_OUT, i, u + 2)
                    dve.wait_ge(unit_done, W_OUT + 4 * i + u + 1)
                    residual(1, 4 * i + u, 6 + u % 2)
            norm(2)
            ffn_in(1, F2_IN)
            ffn_out(2, 1, F2_OUT)

        @block.tensor
        def _(pe):
            def unit(phase, i, u, b, x_hi, x_lo, x0=0, w0=0, k=KD, start=True, stop=True, ready=None):
                slot = (phase + u) % 2
                if w0 == 0:
                    pe.wait_ge(lo_ready, phase + 4 * i + u + 1)
                for n in range(k):
                    if ready:
                        ready(n)
                    wh, wl = w_hi[:, slot, w0 + n, :], w_lo[:, slot, w0 + n, :]
                    xh, xl = x_hi[:, x0 + n, :], x_lo[:, x0 + n, :]
                    pe.matmul(bank(b), wh, xh, start=start and n == 0, stop=False)
                    pe.matmul(bank(b), wh, xl, start=False, stop=False)
                    ins = pe.matmul(bank(b), wl, xh, start=False, stop=stop and n == k - 1)
                return ins

            def normed_chunks(s):
                return lambda k: pe.wait_ge(u_lo_ready, KD * s + k + 1)

            def statistics(s):
                pe.wait_ge(ssq_step, (KD - 1) * (s + 1))
                pe.matmul(bank(4), mean_d[:, :], ssq[:, :], start=True, stop=False)
                pe.wait_ge(sq_ready, KD * (s + 1))
                pe.matmul(bank(4), mean_d[:, :], work[:, 1, :], start=False, stop=True).then_inc(stat_ps, 1)

            def ada_total(q, k):
                pe.wait_ge(ada_step, KD * (q + 1))
                if not is_static(q) or q > 0:
                    pe.wait_ge(mod_ready, q)
                pe.matmul(bank(5)[:, 0:1], ada_acc[:, k, :], ones[:, 0:1], start=True, stop=True).then_inc(mod_ps, 1)

            def two_units(phase, banks, s):
                pe.wait_ge(lo_ready, phase + 2)
                for k in range(KD):
                    pe.wait_ge(u_lo_ready, KD * s + k + 1)
                    for u in range(2):
                        slot, out_u = (phase + u) % 2, bank(banks[u])
                        wh, wl, xh, xl = w_hi[:, slot, k, :], w_lo[:, slot, k, :], u_hi[:, k, :], u_lo[:, k, :]
                        pe.matmul(out_u, wh, xh, start=k == 0, stop=False)
                        pe.matmul(out_u, wh, xl, start=False, stop=False)
                        ins = pe.matmul(out_u, wl, xh, start=False, stop=k == KD - 1)
                        if k == KD - 1:
                            ins.then_inc(unit_done, 1)

            def ffn_in(f, phase):
                for i in laps(pe, KF // 2):
                    for jj in range(2):
                        j = 2 * i + jj
                        if not is_static(j) or f or j >= 2:
                            pe.wait_ge(glu_ready, KF * f + j - 1)
                        if is_static(j) and j == 0:
                            two_units(phase, (0, 1), 2 * f)
                        for ab in range(2):
                            if not (is_static(j) and j == 0):
                                unit(phase, i, 2 * jj + ab, 2 * jj + ab, u_hi, u_lo).then_inc(unit_done, 1)
                            if f == 0 and ab:
                                ada_total(2 * j, 0)
                            elif f == 0 and not (is_static(j) and j == 0):
                                ada_total(2 * j - 1, 1)

            def ffn_out(s, f, phase, after):
                def silu_chunks(k):
                    if k == HALF - 1:
                        pe.wait_ge(g_lo_ready, KF * (f + 1))

                for i in laps(pe, KD // 2):
                    for oo in range(2):
                        o = 2 * i + oo
                        pe.wait_ge(h_ready, KD * (s + 1) + o - 1)
                        first = is_static(o) and o == 0
                        if first:
                            pe.wait_ge(g_lo_ready, KF * (f + 1) - 1)
                        unit(phase, i, 2 * oo, 6 + oo, g_hi, g_lo, k=HALF, stop=False).then_inc(unit_done, 1)
                        if f == 0 and not (is_static(o) and o > 6):
                            ada_total(2 * (KF + o) - 1, 1)
                        unit(phase, i, 2 * oo + 1, 6 + oo, g_hi, g_lo, x0=HALF, k=HALF, start=False,
                             ready=silu_chunks if first else None).then_inc(unit_done, 1)
                        after(i, oo)

            pe.wait_ge(masks, 10)
            pe.wait_ge(c_in, 16)
            pe.transpose(bank(6)[:, 0:KD], c_rows[:, :], ident[0:KD, 0:KD]).then_inc(c_ps, 1)
            pe.wait_ge(x_in, 16 * NB)
            for k in range(KD):
                if k >= 4:
                    pe.wait_ge(h_ready, k - 3)
                for b in range(NB):
                    ins = pe.transpose(bank(k % 4)[:, b * P:(b + 1) * P], x_nat[:, b, k * P:(k + 1) * P], ident[:, :])
                ins.then_inc(x_ps, 1)
            statistics(0)
            pe.wait_ge(small_in, 16 * 10)
            pe.transpose(bank(7)[:, 0:96], vec_rows[:, :], ident[0:96, 0:96])
            pe.transpose(bank(7)[:, 128:179], vec2_rows[:, :], ident[0:51, 0:51]).then_inc(vec_ps, 1)
            for q in range(EARLY):
                pe.wait_ge(early_step, KD * (q + 1))
                for k in range(2):
                    ins = pe.matmul(bank(5)[:, 2 * q + k:2 * q + k + 1], ada_early[:, q, 0, k * P:(k + 1) * P],
                                    ones[:, 0:1], start=True, stop=True)
            ins.then_inc(early_ps, 1)
            ffn_in(0, F1_IN)

            def piece_sum(i, oo):
                if not (is_static(i) and i == KD // 2 - 1):
                    ada_total(2 * (KF + 2 * i + oo), 0)

            ffn_out(0, 0, F1_OUT, piece_sum)
            statistics(1)

            def qk_statistics(r):
                pe.wait_ge(qk_sq, r + 1)
                if r >= 4:
                    pe.wait_ge(qk_rs, 3 * (r - 4) + 1)
                pe.matmul(bank(r % 4), mean_64[:, :], work[:, r % 2, :], start=True, stop=True).then_inc(qk_stat, 1)

            two_units(SB_IN, (6, 7), 1)
            for n in range(2, 12):
                pe.wait_ge(proj_ready, n - 1)
                unit(SB_IN, 0, n, 6 + n % 2, u_hi, u_lo).then_inc(unit_done, 1)
                if n < 10:
                    qk_statistics(n - 2)

            def mixed(m, k0=0, k1=KD):
                if k0 == 0:
                    pe.wait_ge(proj_ready, 12 + m - 1)
                ins = unit(DN_IN, 0, m, 6 + m % 2, u_hi, u_lo, x0=k0, w0=k0, k=k1 - k0, start=k0 == 0, stop=k1 == KD)
                if k1 == KD:
                    ins.then_inc(unit_done, 1)

            mixed(0)
            pe.wait_ge(proj_ready, 12)
            for b in range(NB):
                if b >= 2:
                    pe.wait_ge(v_nat_ready, b - 1)
                for k in range(4):
                    ins = pe.transpose(bank(4 + b % 2)[:, k * P:(k + 1) * P], sb_T[:, 8 + k, b * P:(b + 1) * P],
                                       ident[:, :])
                ins.then_inc(vt_ps, 1)
            pe.wait_ge(qk_rs, 3 * 8)
            pe.wait_ge(proj_ready, 13)
            for b in range(NB):
                ins = pe.transpose(bank(3)[:, 8 * b:8 * b + 8], ab_T[:, b * P:(b + 1) * P], ident[0:8, 0:8])
            ins.then_inc(ab_ps, 1)

            def scores(h):
                rows_h = slice(SBD * (h % 2), SBD * (h % 2) + SBD)
                if h >= 2:
                    pe.wait_ge(y_lo_ready, h - 1)
                for j in range(NB):
                    ins = pe.matmul(region[h % 2][:, OFF[j]:OFF[j] + WID[j]],
                                    sb_T[rows_h, h // 2 * 2 + 1, j * P:(j + 1) * P], sb_T[rows_h, h // 2 * 2, j * P:S],
                                    start=True, stop=True)
                ins.then_inc(z_ps, 1)

            pe.wait_ge(qk_ready, 8)
            pe.wait_ge(v_nat_ready, NB)
            scores(0)
            pe.wait_ge(gate_dve, 5)
            pe.matmul(bank(3)[:, 0:NB * DNH], upto[:, :], small["g"].rearrange("p b h -> p (b h)"),
                      start=True, stop=True).then_inc(gsum_ps, 1)
            pe.wait_ge(gsum_act, 2)
            scores(1)
            for h in range(SBH):
                e = h % 2
                pe.wait_ge(keep_masked, h + 1)
                pe.wait_ge(beta_ready, h + 1)
                for j in range(NB):
                    for j2 in range(j, NB):
                        at = OFF[j] + P * (j2 - j)
                        ins = pe.matmul(region[e][:, at:at + WID[j2]], (below if j2 == j else ones)[:, :],
                                        att_b[:, e, OFF[j2]:OFF[j2] + WID[j2]], start=j2 == j, stop=j2 == NB - 1)
                ins.then_inc(later_ps, 1)
                mixed(1 + 2 * h)
                pe.wait_ge(w_masked, h + 1)
                for j in range(NB):
                    ins = pe.matmul(region[e][SBD * e:SBD * e + SBD, j * P:S], v_nat[:, j, SBD * h:SBD * h + SBD],
                                    att_a[:, e, OFF[j]:OFF[j] + WID[j]], start=j == 0, stop=j == NB - 1)
                ins.then_inc(y_ps, 1)
                mixed(2 + 2 * h)
                if h + 2 < SBH:
                    scores(h + 2)

            pe.wait_ge(y_lo_ready, SBH)
            done = [0]

            def fill(point, chunks=None):
                for _ in range(FILL[point] if chunks is None else chunks):
                    m, k = 21 + done[0] // KD, done[0] % KD
                    if m < len(MIXED):
                        mixed(m, k, k + 1)
                        done[0] += 1

            for m in range(DNH):
                mixed(17 + m)
                for r in (2 * m, 2 * m + 1):
                    pe.wait_ge(l2_sq, r + 1)
                    if r >= 4:
                        pe.wait_ge(l2_rs, 3 * (r - 4) + 1)
                    pe.matmul(bank(r % 4), ones[:, :], work[:, r % 2, :], start=True, stop=True).then_inc(l2_stat, 1)
            fill("start")
            pe.wait_ge(l2_ready, 8)
            pe.wait_ge(dn_silu, 12)
            for q in range(NB):
                if q >= 2:
                    pe.wait_ge(nat_ready, q - 1)
                for h in range(DNH):
                    ins = pe.transpose(bank(2 * (q % 2))[:, h * P:(h + 1) * P], conv[:, 4 + h, q * P:(q + 1) * P],
                                       ident[:, :])
                ins.then_inc(nat_ps, 1)
                if q >= 2:
                    pe.wait_ge(nat_v_ready, q - 1)
                for h in range(DNH):
                    ins = pe.transpose(bank(2 * (q % 2) + 1)[:, h * P:(h + 1) * P],
                                       conv[:, 8 + h, q * P:(q + 1) * P], ident[:, :])
                ins.then_inc(nat_ps, 1)

            for pair in range(NB // 2):
                both = (2 * pair, 2 * pair + 1)
                for b in both:
                    e, cols = b % 2, slice(b * P, (b + 1) * P)
                    if b < 2:
                        pe.wait_ge(nat_ready, NB)
                        pe.wait_ge(nat_v_ready, NB)
                        pe.wait_ge(gsum_act, 2)
                    else:
                        pe.wait_ge(o_ready, b - 1)
                        pe.wait_ge(state_ready, b - 1)
                        pe.wait_ge(v_new_ready, b - 1)
                    for h in range(DNH):
                        pe.matmul(region[e][:, h * P:(h + 1) * P], small["g"][:, b, h:h + 1].to_broadcast([P, P]),
                                  upto[:, :], start=True, stop=True)
                    for h in range(DNH):
                        pe.matmul(region[e][:, S + h * P:S + (h + 1) * P], conv[:, 4 + h, cols], conv[:, 4 + h, cols],
                                  start=True, stop=True)
                    for h in range(DNH):
                        ins = pe.matmul(region[e][:, 2 * S + h * P:2 * S + (h + 1) * P], conv[:, 4 + h, cols],
                                        conv[:, h, cols], start=True, stop=True)
                    ins.then_inc(prep_ps, 1)
                fill("prep")
                for b in both:
                    e = b % 2
                    pe.wait_ge(inv_t0, b + 1)
                    for h in range(DNH):
                        ins = pe.transpose(region[e][:, h * P:(h + 1) * P], inv_t[:, e, h], ident[:, :])
                    ins.then_inc(inv0_ps, 1)
                fill("inv0")
                for l in range(1, 7):
                    for b in both:
                        e = b % 2
                        pe.wait_ge(link_ready, 14 * pair + 2 * l + e + 1)
                        if l == 1:
                            pe.wait_ge(inv0_ready, b + 1)
                        else:
                            pe.wait_ge(inv_ready, 12 * pair + 2 * (l - 2) + e + 1)
                        for h in range(DNH):
                            ins = pe.matmul(region[e][:, h * P:(h + 1) * P], link[:, e, h], inv[:, e, h],
                                            start=True, stop=True)
                        ins.then_inc(prod_ps, 1)
                    for b in both:
                        e = b % 2
                        pe.wait_ge(prod_ready, 12 * pair + 2 * (l - 1) + e + 1)
                        if l < 6:
                            for h in range(DNH):
                                pe.matmul(region[e][:, S + h * P:S + (h + 1) * P], inv_t[:, e, h], prod[:, e, h],
                                          start=True, stop=True)
                        for h in range(DNH):
                            ins = pe.matmul(region[e][:, 2 * S + h * P:2 * S + (h + 1) * P], prod[:, e, h],
                                            inv_t[:, e, h], start=True, stop=True)
                        ins.then_inc(corr_ps, 1)
                    fill("level")
                fill("solve")
                for b in both:
                    e = b % 2
                    pe.wait_ge(inv_ready, 12 * pair + 10 + e + 1)
                    pe.wait_ge(kexp_ready, b + 1)
                    for h in range(DNH):
                        pe.matmul(region[e][:, h * P:(h + 1) * P], inv_t[:, e, h], v_dn[:, b, h], start=True, stop=True)
                    for h in range(DNH):
                        ins = pe.matmul(region[e][:, S + h * P:S + (h + 1) * P], prod[:, e, h], inv_t[:, e, h],
                                        start=True, stop=True)
                    ins.then_inc(uw_ps, 1)
                fill("solved")
                for b in both:
                    e, cols = b % 2, slice(b * P, (b + 1) * P)
                    pe.wait_ge(w_ready, b + 1)
                    pe.wait_ge(u_ready, b + 1)
                    if b:
                        pe.wait_ge(state_ready, b)
                        for h in range(DNH):
                            ins = pe.matmul(region[e][:, 2 * S + h * P:2 * S + (h + 1) * P], w_t[:, e, h],
                                            state[:, h], start=True, stop=True)
                        ins.then_inc(ws_ps, 1)
                    pe.wait_ge(att_ready, b + 1)
                    for h in range(DNH if b else 0):
                        pe.matmul(region[e][:, h * P:(h + 1) * P], state[:, h], conv[:, h, cols],
                                  start=h == 0, stop=False)
                    fill("step")
                    pe.wait_ge(v_new_ready, b + 1)
                    if b < NB - 1:
                        pe.wait_ge(kdec_ready, b + 1)
                        for h in range(DNH):
                            ins = pe.matmul(region[e][:, S + h * P:S + (h + 1) * P], k_dn[:, b, h], v_new[:, h],
                                            start=True, stop=True)
                        ins.then_inc(ds_ps, 1)
                    for h in range(DNH):
                        ins = pe.matmul(region[e][:, h * P:(h + 1) * P], v_new[:, h], att_t[:, e, h],
                                        start=b == 0 and h == 0, stop=h == DNH - 1)
                    ins.then_inc(o_ps, 1)
            fill("start", 2 * KD * KD)
            for h in range(DNH):
                pe.wait_ge(on_sq, h + 1)
                pe.matmul(bank(h), mean_p[:, :], work[:, h % 2, :], start=True, stop=True).then_inc(on_stat, 1)

            pe.wait_ge(on_rs, 3 * DNH)
            with pe.Fori(0, 2) as i:
                for oo in range(4):
                    e = oo % 2
                    pe.wait_ge(branch_lo, DNH + 4 * i + oo - 1)
                    unit(MERGE, i, oo, 2 * e, ysb_hi, ysb_lo, k=4)
                    pe.wait_ge(branch_lo, DNH)
                    unit(MERGE, i, oo, 2 * e + 1, ydn_hi, ydn_lo, w0=4, k=4).then_inc(unit_done, 1)
            with pe.Fori(0, 2) as i:
                for u in range(4):
                    pe.wait_ge(h_ready, 2 * KD + 4 * i + u - 1)
                    unit(W_OUT, i, u, 6 + u % 2, m_hi, m_lo,
                         ready=(lambda k: pe.wait_ge(branch_lo, DNH + k + 1)) if u == 0 else None)\
                        .then_inc(unit_done, 1)
            statistics(2)
            ffn_in(1, F2_IN)

            def transpose_out(o, b):
                pe.wait_ge(h_ready, 3 * KD + o + 1)
                if not is_static(o) or o >= 2:
                    pe.wait_ge(out_ready, o - 1)
                for q in range(NB):
                    ins = pe.transpose(bank(b)[:, q * P:(q + 1) * P],
                                       work[:, b, q * P:(q + 1) * P], ident[:, :])
                ins.then_inc(out_ps, 1)

            def transpose_last(i, oo):
                if not (is_static(i) and i == 0 and oo == 0):
                    transpose_out(2 * i + oo - 1, 1 - oo)

            ffn_out(2, 1, F2_OUT, transpose_last)
            transpose_out(KD - 1, 1)


_INS = ["x", "c", "w_ada", "b_ada", "g_ffn1", "w_ffn1_in", "w_ffn1_out", "g_mix", "w_in", "g_q_sb", "g_k_sb", "w_conv",
        "a_log", "dt_bias", "g_dn_out", "w_up_sb", "w_up_dn", "w_out", "g_ffn2", "w_ffn2_in", "w_ffn2_out"]


def kernel(**inputs):
    import numpy as np
    import concourse.bacc as bacc
    from concourse.bass_utils import run_bass_kernel_spmd

    nc = bacc.Bacc("TRN2", target_bir_lowering=False, num_devices=1)
    arrays, args = {}, []
    for name in _INS:
        a = np.ascontiguousarray(inputs[name])
        arrays[f"in_{name}"] = a
        args.append(nc.dram_tensor(f"in_{name}", a.shape, mybir.dt.from_np(a.dtype), kind="ExternalInput").ap())
    out = nc.dram_tensor("out_h", (1, S, D), mybir.dt.float32, kind="ExternalOutput").ap()
    build(nc, *args, out)
    result = run_bass_kernel_spmd(nc, [arrays], core_ids=[0])
    return result.results[0]["out_h"]
```

```python
from contextlib import ExitStack

import concourse.bass as bass
from concourse import mybir

P = 128
S = 512
D = 1024
KD = D // P
FF = 2816
KF = FF // P
HALF = KF // 2
SBH, SBD = 8, 64
DNH = 4
NB = S // P
TAPS = 4
EPS = 1e-6
MODS = 9
PIECE = 256
EARLY = 2 * D // PIECE
BY_ACT = (3, 5, 7)
BY_DVE = tuple(q for q in range(EARLY) if q not in BY_ACT)
LATE = 2 * KD
RAW = 4

F1_IN = 0
F1_OUT = F1_IN + 2 * KF
SB_IN = F1_OUT + 2 * KD
DN_IN = SB_IN + 12
MERGE = DN_IN + 17 + 2 * KD
W_OUT = MERGE + KD
F2_IN = W_OUT + KD
F2_OUT = F2_IN + 2 * KF
UNITS = F2_OUT + 2 * KD

COL_DN = 3 * 512
COL_BA = COL_DN + 4 * 512
COL_RSB = COL_BA + 8
COL_RDN = COL_RSB + D

MIXED = [("ba", 0)] + [m for h in range(4) for m in (("conv", 1 + h), ("conv", 9 + h))] \
    + [m for h in range(4) for m in (("conv", 5 + h), ("gate", h))] + [("z", h) for h in range(4)] \
    + [("gate", g) for g in range(4, 16)]
HEAD_0 = 3
SINGLE = 6
Z_0 = MIXED.index(("z", 0))
FILL_0 = Z_0 + 4
CONVS = [d for kind, d in MIXED if kind == "conv"]
FILL = {"l2": 8, "start": 8, "prep": 12, "inv0": 2, "norm": 4, "level": 2, "solve": 3, "solved": 2, "step": 1, "last": 2}


def unit_chunks(n):
    return HALF if F1_OUT <= n < SB_IN or n >= F2_OUT else KD


def conv_chunk(d):
    return d + 3 if d <= 4 else d - 5 if d <= 8 else d - 1


def head_unit(h):
    return HEAD_0 + h + min(h, SINGLE)


def is_static(i):
    return isinstance(i, int)


def filler(step):
    class Fill:
        chunks, unit = 0, FILL_0

        def __call__(self, point):
            self.chunks += FILL[point]
            while self.unit < len(MIXED) and self.chunks >= KD:
                step(self.unit)
                self.unit, self.chunks = self.unit + 1, self.chunks - KD

        def rest(self):
            for m in range(self.unit, len(MIXED)):
                step(m)
    return Fill()


def laps(engine, count, lo=1, hi=1):
    for i in range(lo):
        yield i
    if count - hi > lo:
        with engine.Fori(lo, count - hi) as i:
            yield i
    for i in range(count - hi, count):
        yield i


def build(nc, x, c, w_ada, b_ada, g_ffn1, w_ffn1_in, w_ffn1_out, g_mix, w_in, g_q_sb, g_k_sb, w_conv,
          a_log, dt_bias, g_dn_out, w_up_sb, w_up_dn, w_out, g_ffn2, w_ffn2_in, w_ffn2_out, out):
    f32, f32r = mybir.dt.float32, mybir.dt.float32r
    ALU, ACT = mybir.AluOpType, mybir.ActivationFunctionType
    ds = bass.ds

    def rows(w):
        return w[0].rearrange("(k p) n -> p k n", p=P)

    w_ada_v, w_in_v = rows(w_ada), rows(w_in)
    ffn_in_v = [rows(w_ffn1_in), rows(w_ffn2_in)]
    ffn_out_v = [rows(w_ffn1_out), rows(w_ffn2_out)]
    up_sb_v, up_dn_v, w_out_v = rows(w_up_sb), rows(w_up_dn), rows(w_out)

    with ExitStack() as ctx:
        def sb(name, shape, dt=f32, stack=ctx):
            return stack.enter_context(nc.sbuf_tensor(name, shape, dt))[tuple(slice(None) for _ in shape)]

        def sem(name):
            return ctx.enter_context(nc.semaphore(name))

        hT = sb("hT", [P, KD, S])
        u_hi, u_lo = sb("u_hi", [P, KD, S], f32r), sb("u_lo", [P, KD, S], f32r)
        raw = sb("raw", [P, RAW, HALF, P])
        w_hi, w_lo = sb("w_hi", [P, 2, HALF, P], f32r), sb("w_lo", [P, 2, HALF, P], f32r)
        ident, ones = sb("ident", [P, P]), sb("ones", [P, P])
        mean_d, mean_p = sb("mean_d", [P, P]), sb("mean_p", [P, P])
        mean_64 = sb("mean_64", [P, P])
        below = sb("below", [P, P])
        above = sb("above", [P, P])
        upto = sb("upto", [P, P])
        vec = sb("vec", [P, 96])
        vec2 = sb("vec2", [P, 51])
        alog_dt = sb("alog_dt", [P, 2, DNH])
        cond = sb("cond", [P, KD])
        qk_gain = sb("qk_gain", [P, 2])
        mod = sb("mod", [P, MODS * KD])
        scale_col = sb("scale_col", [P, 3, KD])
        gate_col = sb("gate_col", [P, 3, KD])
        ada_acc = sb("ada_acc", [P, 4, P])
        eps = sb("eps", [P, 1])
        ssq = sb("ssq", [P, S])
        rstd = sb("rstd", [P, S])
        work = sb("work", [P, 2, S])

        with ExitStack() as s:
            vec_rows = sb("vec_rows", [96, P], stack=s)
            c_rows = sb("c_rows", [KD, P], stack=s)
            vec2_rows = sb("vec2_rows", [51, P], stack=s)
            x_nat = sb("x_nat", [P, NB, D], stack=s)
            ada_early = sb("ada_early", [P, EARLY, KD, PIECE], stack=s)
        with ExitStack() as s:
            g_hi, g_lo = sb("g_hi", [P, KF, S], f32r, stack=s), sb("g_lo", [P, KF, S], f32r, stack=s)
            with ExitStack() as t:
                ada_raw = sb("ada_raw", [P, 2, KD, P], stack=t)
            with ExitStack() as t:
                out_nat = sb("out_nat", [P, 2, NB, P], stack=t)
        with ExitStack() as s:
            ysb_hi, ysb_lo = sb("ysb_hi", [P, 4, S], f32r, stack=s), sb("ysb_lo", [P, 4, S], f32r, stack=s)
            with ExitStack() as t:
                small = {n: sb("dn_" + n, [P, NB, DNH], stack=t) for n in
                         ("beta", "neg_beta", "a", "abs", "exp", "log", "g", "gsum", "gexp", "glast", "kdec")}
                rate = sb("rate", [P, DNH], stack=t)
                conv = sb("conv", [P, 12, S], stack=t)
                ab_T = sb("ab_T", [2 * DNH, S], stack=t)
                with ExitStack() as v:
                    sb_T = sb("sb_T", [P, 12, S], stack=v)
                    v_nat = sb("v_nat", [P, NB, SBH * SBD], stack=v)
                    pad = sb("pad", [P, 2, TAPS - 1 + S], stack=v)
                    att_a, att_b = sb("att_a", [P, 2, 1280], stack=v), sb("att_b", [P, 2, 1280], stack=v)
                with ExitStack() as v:
                    z_gate = sb("z_gate", [P, DNH, S], stack=v)
                    inv, inv_t, sys_t, link, prod = (sb("dn_" + n, [P, 2, DNH, P], stack=v) for n in
                                                    ("inv", "inv_t", "sys_t", "link", "prod"))
                    att_t, w_t = sb("att_t", [P, 2, DNH, P], stack=v), sb("w_t", [P, 2, DNH, P], stack=v)
                    state = sb("state", [P, DNH, P], stack=v)
                    level = sb("level", [P, 7, P], stack=v)
                    with ExitStack() as w:
                        k_dn = sb("k_dn", [P, NB, DNH, P], stack=w)
                        v_dn = sb("v_dn", [P, NB, DNH, P], stack=w)
                    with ExitStack() as w:
                        ydn_hi = sb("ydn_hi", [P, 4, S], f32r, stack=w)
                        ydn_lo = sb("ydn_lo", [P, 4, S], f32r, stack=w)
            with ExitStack() as t:
                m_hi, m_lo = sb("m_hi", [P, KD, S], f32r, stack=t), sb("m_lo", [P, KD, S], f32r, stack=t)
                sb("merge_gap", [P, 2 * KD * P], stack=t)
                gates = sb("gates", [P, 2, 2, S], stack=t)
        kept = nc.dram_tensor("kept_gates", (2 * KD, P, S), f32, kind="Internal").ap()

        v_new = ssq[:, :].rearrange("p (h e) -> p h e", h=DNH)
        out_nat_cols = out[0].rearrange("(b p) n -> p b n", p=P)

        region = [ctx.enter_context(nc.psum_tensor(f"region{r}", [P, 3 * S], f32)) for r in range(2)]
        tail = ctx.enter_context(nc.psum_tensor("tail", [P, 2 * S], f32))

        def bank(b):
            t, k = (region[b // 3], b % 3) if b < 6 else (tail, b - 6)
            return t[:, k * S:(k + 1) * S]

        def heads(ap):
            return ap.rearrange("p (h e) -> p h e", h=DNH)

        def each(t):
            return t.unsqueeze(1).to_broadcast([P, DNH, P])

        def flat(t, b):
            return t[:, b].rearrange("p h e -> p (h e)")

        small_in, rates_in, x_in = sem("small_in"), sem("rates_in"), sem("x_in")
        ada_early_in = [sem(f"ada_early_in{q}") for q in range(EARLY)]
        ada_in = [sem(f"ada_in{k}") for k in range(2)]
        c_in, c_ps, early_step, early_ps, early_mod = (sem("c_in"), sem("c_ps"), sem("early_step"), sem("early_ps"),
                                                       sem("early_mod"))
        early_halves = sem("early_halves")
        gate_stored = sem("gate_stored")
        gates_in = [sem(f"gates_in{k}") for k in range(2)]
        raw_in = [sem(f"raw_in{r}") for r in range(RAW)]
        out_done = [sem(f"out_done{k}") for k in range(2)]
        masks, mask_step = sem("masks"), sem("mask_step")
        vec_ps, vec_ready, cond_ready = sem("vec_ps"), sem("vec_ready"), sem("cond_ready")
        x_ps, h_ready, sq_ready, ssq_step = sem("x_ps"), sem("h_ready"), sem("sq_ready"), sem("ssq_step")
        stat_ps, root_ready, rstd_ready = sem("stat_ps"), sem("root_ready"), sem("rstd_ready")
        cols_ready, normed_ready = sem("cols_ready"), sem("normed_ready")
        u_hi_ready, u_lo_ready = sem("u_hi_ready"), sem("u_lo_ready")
        ada_step, mod_ps, mod_ready = sem("ada_step"), sem("mod_ps"), sem("mod_ready")
        ada_scaled, early_scaled, mod_step = sem("ada_scaled"), sem("early_scaled"), sem("mod_step")
        hi_ready, lo_ready, unit_done = sem("hi_ready"), sem("lo_ready"), sem("unit_done")
        silu_ready, glu_ready = sem("silu_ready"), sem("glu_ready")
        g_hi_ready, g_lo_ready = sem("g_hi_ready"), sem("g_lo_ready")
        out_ps, out_ready = sem("out_ps"), sem("out_ready")
        proj_ready, pad_zero, conv_step = sem("proj_ready"), sem("pad_zero"), sem("conv_step")
        qk_sq, qk_stat, qk_root, qk_rs, qk_ready = (sem("qk_sq"), sem("qk_stat"), sem("qk_root"), sem("qk_rs"),
                                                    sem("qk_ready"))
        vt_ps, v_nat_ready = sem("vt_ps"), sem("v_nat_ready")
        gain_ready = sem("gain_ready")
        z_ps, soft_step, keep_ready, keep_masked = sem("z_ps"), sem("soft_step"), sem("keep_ready"), sem("keep_masked")
        beta_ready, later_ps, logw_ready, w_raw, w_masked = (sem("nb_ready"), sem("later_ps"), sem("logw_ready"),
                                                            sem("w_raw"), sem("w_masked"))
        y_ps, y_hi_ready, y_lo_ready = sem("y_ps"), sem("y_hi_ready"), sem("y_lo_ready")
        dn_silu, l2_sq, l2_stat, l2_root, l2_rs, l2_ready = (sem("dn_silu"), sem("l2_sq"), sem("l2_stat"),
                                                             sem("l2_root"), sem("l2_rs"), sem("l2_ready"))
        z_silu = sem("z_silu")
        ab_ps, gate_act, gate_dve, gsum_ps, gsum_act = (sem("ab_ps"), sem("gate_act"), sem("gate_dve"),
                                                        sem("gsum_ps"), sem("gsum_act"))
        nat_ps, nat_ready, nat_v_ready = sem("nat_ps"), sem("nat_ready"), sem("nat_v_ready")
        prep_ps, dec_raw, dec_exp, dec_masked, gexp_ready = (sem("prep_ps"), sem("dec_raw"), sem("dec_exp"),
                                                             sem("dec_masked"), sem("gexp_ready"))
        glast_ready, kdec_exp, sys_ready, att_ready = (sem("glast_ready"), sem("kdec_exp"), sem("sys_ready"),
                                                       sem("att_ready"))
        link_ready, link_0, inv_t0, inv0_ps, inv0_ready = sem("link_ready"), sem("link_0"), sem("inv_t0"), sem("inv0_ps"), sem("inv0_ready")
        prod_ps, prod_ready, corr_ps, inv_ready = sem("prod_ps"), sem("prod_ready"), sem("corr_ps"), sem("inv_ready")
        kexp_ready, kdec_ready, uw_ps, u_ready, w_ready = (sem("kexp_ready"), sem("kdec_ready"), sem("uw_ps"),
                                                           sem("u_ready"), sem("w_ready"))
        ws_ps, v_new_ready, o_ps, o_ready, ds_ps, state_ready = (sem("ws_ps"), sem("v_new_ready"), sem("o_ps"),
                                                                 sem("o_ready"), sem("ds_ps"), sem("state_ready"))
        on_sq, on_stat, on_root, on_rs, on_scaled, on_gated = (sem("on_sq"), sem("on_stat"), sem("on_root"),
                                                               sem("on_rs"), sem("on_scaled"), sem("on_gated"))
        ydn_hi_ready = sem("ydn_hi_ready")
        branch_lo = sem("branch_lo")
        sig_ready, part_ready, sum_ready, m_hi_ready = (sem("sig_ready"), sem("part_ready"), sem("sum_ready"),
                                                        sem("m_hi_ready"))

        SH, SC, GT = [0, 3, 6], [1, 4, 7], [2, 5, 8]
        OFF = [0, 512, 1024, 896]
        WID = [S - P * j for j in range(NB)]
        L2 = [4, 0, 5, 1, 6, 2, 7, 3]
        block = ctx.enter_context(nc.Block())

        @block.sync
        def _(sp):
            def source(phase, i, u):
                if is_static(i):
                    n = phase + 4 * i + u
                    phase = max(f for f in (F1_IN, F1_OUT, SB_IN, DN_IN, MERGE, W_OUT, F2_IN, F2_OUT) if f <= n)
                    i, u = 0, n - phase
                f = int(phase >= F2_IN)
                if phase in (F1_IN, F2_IN):
                    v, col, k0, kn = ffn_in_v[f], (4 * i + u - u % 2) * (P // 2) + (u % 2) * FF, 0, KD
                elif phase in (F1_OUT, F2_OUT):
                    v, col, k0, kn = ffn_out_v[f], (4 * i + u - u % 2) * (P // 2), (u % 2) * HALF, HALF
                elif phase == SB_IN:
                    v, col, k0, kn = w_in_v, (u % 2 * 4 + u // 2 if u < 8 else u) * P, 0, KD
                elif phase == DN_IN:
                    v, k0, kn = w_in_v, 0, KD
                    kind, d = MIXED[u]
                    col = {"ba": COL_BA, "z": COL_DN + (12 + d) * P, "gate": COL_RSB + d * P,
                           "conv": COL_DN + P * conv_chunk(d)}[kind]
                elif phase == MERGE:
                    return [(0, 4, up_sb_v[:, :, u * P:u * P + P]), (4, 8, up_dn_v[:, :, u * P:u * P + P])]
                else:
                    v, col, k0, kn = w_out_v, u * P, 0, KD
                cut = kn // 2
                return [(0, cut, v[:, k0:k0 + cut, ds(col, P)]), (cut, kn, v[:, k0 + cut:k0 + kn, ds(col, P)])]

            def load(phase, i, u):
                slot = (phase + u) % RAW
                for a, b, view in source(phase, i, u):
                    sp.dma_start(raw[:, slot, a:b, :], view).then_inc(raw_in[slot], 16)

            def load_next(phase, i, u):
                if is_static(i) and phase + 4 * i + u + RAW >= UNITS:
                    return
                sp.wait_ge(lo_ready, phase + 4 * i + u + 1)
                load(phase, i, u + RAW)

            def load_gates(o):
                for k in range(2):
                    sp.dma_start(gates[:, o % 2, k, :], kept[k * KD + o]).then_inc(gates_in[o % 2], 16)

            sp.dma_start(c_rows[:, :], c[0].rearrange("(k p) -> k p", p=P)).then_inc(c_in, 16)
            sp.dma_start(ada_early[:, 0], w_ada_v[:, :, 0:PIECE]).then_inc(ada_early_in[0], 16)
            for b in range(NB):
                sp.dma_start(x_nat[:, b, :], x[0, b * P:(b + 1) * P, :]).then_inc(x_in, 16)
            for q in range(1, EARLY):
                sp.dma_start(ada_early[:, q], w_ada_v[:, :, q * PIECE:(q + 1) * PIECE]).then_inc(ada_early_in[q], 16)
            sp.dma_start(vec_rows[0:72, :], b_ada[0].rearrange("(k p) -> k p", p=P)).then_inc(small_in, 16)
            for n, g in enumerate((g_ffn1, g_mix, g_ffn2)):
                sp.dma_start(vec_rows[72 + 8 * n:80 + 8 * n, :], g[0].rearrange("(k p) -> k p", p=P)).then_inc(small_in, 16)
            sp.dma_start(vec2_rows[0:48, :], w_conv[0].rearrange("t (k p) -> (t k) p", p=P)).then_inc(small_in, 16)
            sp.dma_start(vec2_rows[48:49, :], g_dn_out).then_inc(small_in, 16)
            for n, g in enumerate((g_q_sb, g_k_sb)):
                for half in range(2):
                    sp.dma_start(vec2_rows[49 + n:50 + n, half * SBD:half * SBD + SBD], g).then_inc(small_in, 16)
            for n, g in enumerate((a_log, dt_bias)):
                sp.dma_start(alog_dt[:, n, :], g[0].partition_broadcast(P)).then_inc(rates_in, 16)
            for u in range(RAW):
                load(F1_IN, 0, u)

            def load_late(q, k):
                if not is_static(q) or q >= 2:
                    sp.wait_ge(ada_step, 3 * (q - 1))
                sp.dma_start(ada_raw[:, k], w_ada_v[:, :, ds(P * (LATE + q), P)]).then_inc(ada_in[k], 16)

            for i in laps(sp, KF // 2):
                for u in range(4):
                    load_next(F1_IN, i, u)
                    load_late(4 * i + u, u % 2)
            for i in laps(sp, KD // 2, 0, 1):
                for u in range(4):
                    load_next(F1_OUT, i, u)
                    if not (is_static(i) and i == KD // 2 - 1):
                        load_late(2 * KF + 4 * i + u, u % 2)
            for n in range(SB_IN, F2_IN):
                load_next(n, 0, 0)
                m = n - 2 - DN_IN
                if 0 <= m < len(MIXED) and MIXED[m][0] == "gate":
                    g = MIXED[m][1]
                    sp.wait_ge(proj_ready, 12 + m + 1)
                    sp.dma_start(kept[g], rstd[:, :]).then_inc(gate_stored, 16)
                if n == MERGE:
                    sp.wait_ge(gate_stored, 16 * (KD + 2))
                    sp.wait_ge(uw_ps, NB)
                    load_gates(0)
                    load_gates(1)
                if MERGE + 2 <= n < MERGE + KD:
                    sp.wait_ge(part_ready, 2 * (n - MERGE - 1))
                    sp.wait_ge(gate_stored, 16 * (n + 1 - MERGE + KD))
                    load_gates(n - MERGE)
            for phase, steps in ((F2_IN, KF // 2), (F2_OUT, KD // 2)):
                for i in laps(sp, steps, 0, 1):
                    for u in range(4):
                        load_next(phase, i, u)

        @block.gpsimd
        def _(pool):
            steps = [0]

            def then(ins):
                steps[0] += 1
                ins.then_inc(mask_step, 1)
                pool.wait_ge(mask_step, steps[0])

            def triangle(t, base, sign, op):
                then(pool.memset(t, 1.0))
                return pool.affine_select(out=t, in_=t, compare_op=op, fill=0.0, base=base,
                                          pattern=[[sign, P]], channel_multiplier=-sign)

            triangle(ident[:, :], 0, 1, ALU.is_equal).then_inc(masks, 1)
            pool.memset(ones[:, :], 1.0).then_inc(masks, 1)
            pool.memset(eps[:, :], EPS).then_inc(masks, 1)
            pool.memset(mean_d[:, :], 1.0 / D).then_inc(masks, 1)
            pool.memset(mean_p[:, :], 1.0 / P).then_inc(masks, 1)
            then(pool.memset(mean_64[:, :], 1.0 / SBD))
            for half, base, sign in ((mean_64[:, 0:SBD], SBD - 1, -1), (mean_64[:, SBD:P], -SBD, 1)):
                pool.affine_select(out=half, in_=half, compare_op=ALU.is_ge, fill=0.0, base=base,
                                   pattern=[[0, SBD]], channel_multiplier=sign).then_inc(masks, 1)
            triangle(below[:, :], 0, -1, ALU.is_gt).then_inc(masks, 1)
            triangle(above[:, :], 0, 1, ALU.is_gt).then_inc(masks, 1)
            triangle(upto[:, :], 0, 1, ALU.is_ge).then_inc(masks, 1)

            def sum_squares(s):
                for o in range(KD - 1):
                    pool.wait_ge(sq_ready, KD * s + o + 1)
                    if o == 0:
                        pool.tensor_copy(ssq[:, :], work[:, 0, :]).then_inc(ssq_step, 1)
                    else:
                        pool.wait_ge(ssq_step, (KD - 1) * s + o)
                        pool.tensor_tensor(ssq[:, :], ssq[:, :], work[:, o % 2, :], ALU.add).then_inc(ssq_step, 1)

            sum_squares(0)
            sum_squares(1)
            pool.wait_ge(u_lo_ready, 2 * KD)
            pool.memset(pad[:, :, 0:TAPS - 1], 0.0).then_inc(pad_zero, 1)

            def diagonal(t, done):
                for j in range(NB):
                    d = t[:, OFF[j]:OFF[j] + P]
                    ins = pool.tensor_tensor(d, d, above[:, :], ALU.mult)
                ins.then_inc(done, 1)

            pool.wait_ge(keep_ready, 1)
            diagonal(att_b[:, 0, :], keep_masked)
            for h in range(SBH):
                pool.wait_ge(w_raw, h + 1)
                diagonal(att_a[:, h % 2, :], w_masked)
                if h + 1 < SBH:
                    pool.wait_ge(keep_ready, h + 2)
                    diagonal(att_b[:, (h + 1) % 2, :], keep_masked)

            pool.wait_ge(y_ps, SBH)
            pool.wait_ge(conv_step, 48)
            for l in range(7):
                k = 1 << l
                m = level[:, l, :]
                then(pool.memset(m, 0.0))
                half = m.rearrange("p (a b r) -> p a b r", b=2, r=k)[:, :, 1, :]
                then(pool.memset(half, 1.0))
                then(pool.affine_select(out=half, in_=half, compare_op=ALU.is_ge, fill=0.0, base=0,
                                        pattern=[[-2 * k, P // (2 * k)], [0, k]], channel_multiplier=1))
                then(pool.affine_select(out=half, in_=half, compare_op=ALU.is_ge, fill=0.0, base=k - 1,
                                        pattern=[[2 * k, P // (2 * k)], [0, k]], channel_multiplier=-1))

            for pair in range(NB // 2):
                for b in (2 * pair, 2 * pair + 1):
                    pool.wait_ge(dec_exp, b + 1)
                    dec = heads(work[:, b % 2, :])
                    pool.tensor_tensor(dec, dec, each(upto[:, :]), ALU.mult).then_inc(dec_masked, 1)
                for l in range(1, 7):
                    for b in (2 * pair, 2 * pair + 1):
                        if l == 1:
                            pool.wait_ge(inv_t0, b + 1)
                        else:
                            pool.wait_ge(prod_ps, 12 * pair + 2 * (l - 2) + b % 2 + 1)
                        pool.tensor_tensor(link[:, b % 2], sys_t[:, b % 2], each(level[:, l, :]), ALU.mult)\
                            .then_inc(link_ready, 1)

            sum_squares(2)

        @block.scalar
        def _(act):
            def split_hi(phase, i, u):
                n = phase + 4 * i + u
                if is_static(i) and n >= UNITS:
                    return
                slot, k = (phase + u) % RAW, unit_chunks(n) if is_static(i) else unit_chunks(phase)
                act.wait_ge(raw_in[slot], 32 * ((phase + u) // RAW + i + 1))
                if not is_static(n) or n >= 2:
                    act.wait_ge(unit_done, n - 1)
                act.activation(w_hi[:, slot % 2, 0:k, :], raw[:, slot, 0:k, :], ACT.Copy).then_inc(hi_ready, 1)

            def squares(s, o, k):
                act.wait_ge(h_ready, KD * s + o + 1)
                if not is_static(o) or s > 0 or o >= 2:
                    act.wait_ge(ssq_step, (KD - 1) * s + o - 1)
                act.activation(work[:, k, :], hT[:, ds(o, 1), :].rearrange("p a s -> p (a s)"),
                               ACT.Square).then_inc(sq_ready, 1)

            def inverse_root(dst, b, done, n):
                act.activation(dst, bank(b), ACT.Ln, bias=eps[:, 0:1]).then_inc(done, 1)
                act.wait_ge(done, 2 * n + 1)
                act.activation(dst, dst, ACT.Exp, scale=-0.5).then_inc(done, 1)

            def ada_scale(piece, done, arrived):
                act.wait_ge(*arrived)
                for k in range(KD):
                    ins = act.activation(piece[:, k, :], piece[:, k, :], ACT.Copy, scale=cond[:, k:k + 1])
                ins.then_inc(done, 1)

            def rough_root(s):
                act.wait_ge(stat_ps, s + 1)
                inverse_root(rstd[:, :], 4, root_ready, s)

            def norm_hi(s):
                if s:
                    rough_root(s)
                for k in range(KD):
                    act.wait_ge(normed_ready, KD * s + k + 1)
                    act.activation(u_hi[:, k, :], work[:, k % 2, :], ACT.Identity,
                                   bias=mod[:, SH[s] * KD + k:SH[s] * KD + k + 1]).then_inc(u_hi_ready, 1)

            def ffn(f, phase):
                for i in laps(act, KF // 2):
                    for jj in range(2):
                        j = 2 * i + jj
                        split_hi(phase, i, 2 * jj + 2)
                        act.wait_ge(unit_done, phase + 2 * j + 1)
                        if not is_static(j) or f or j:
                            act.wait_ge(glu_ready, KF * f + j)
                        act.activation(work[:, 0, :], bank(2 * jj), ACT.Silu).then_inc(silu_ready, 1)
                        split_hi(phase, i, 2 * jj + 3)
                        act.wait_ge(glu_ready, KF * f + j + 1)
                        act.activation(g_hi[:, ds(j, 1), :], work[:, 1:2, :], ACT.Copy).then_inc(g_hi_ready, 1)
                        if f == 0:
                            for k in range(2):
                                ada_scale(ada_raw[:, k], ada_scaled, (ada_in[k], 16 * (j + 1)))

            act.wait_ge(masks, 10)
            act.wait_ge(c_ps, 1)
            act.activation(cond[:, :], bank(6)[:, 0:KD], ACT.Silu).then_inc(cond_ready, 1)
            act.wait_ge(cond_ready, 1)
            for k in range(KD):
                act.wait_ge(x_ps, k + 1)
                act.activation(hT[:, k, :], bank(k % 4), ACT.Copy).then_inc(h_ready, 1)
                squares(0, k, k % 2)
            ada_scale(ada_early[:, BY_ACT[0]], early_scaled, (ada_early_in[BY_ACT[0]], 16))
            rough_root(0)
            act.wait_ge(vec_ps, 1)
            act.activation(vec[:, :], bank(7)[:, 0:96], ACT.Copy).then_inc(vec_ready, 1)
            act.activation(vec2[:, :], bank(7)[:, 128:179], ACT.Copy).then_inc(vec_ready, 1)
            for q in BY_ACT[1:]:
                ada_scale(ada_early[:, q], early_scaled, (ada_early_in[q], 16))
            split_hi(F1_IN, 0, 0)
            split_hi(F1_IN, 0, 1)
            norm_hi(0)
            ffn(0, F1_IN)
            for i in laps(act, KD // 2, 0, 1):
                for oo in range(2):
                    split_hi(F1_OUT, i, 2 * oo + 2)
                    split_hi(F1_OUT, i, 2 * oo + 3)
                    squares(1, 2 * i + oo, oo)
                    if not (is_static(i) and i == KD // 2 - 1):
                        for k in range(2):
                            ada_scale(ada_raw[:, k], ada_scaled, (ada_in[k], 16 * (KF + 2 * i + oo + 1)))

            norm_hi(1)

            def evacuate(p, unit, dst):
                act.wait_ge(unit_done, unit + 1)
                act.activation(dst, bank(6 + p % 2), ACT.Copy).then_inc(proj_ready, 1)

            def qk_inverse_root(r):
                act.wait_ge(qk_stat, r + 1)
                if r >= 2:
                    act.wait_ge(qk_ready, r - 1)
                inverse_root((ssq, rstd)[r % 2][:, :], r % 4, qk_root, r)

            for n in range(12):
                split_hi(SB_IN, 0, n + 2)
                act.wait_ge(unit_done, SB_IN + n + 1)
                act.activation(sb_T[:, n, :], bank(6 + n % 2), ACT.Copy).then_inc(proj_ready, 1)
                if n < 8:
                    if n >= 2:
                        act.wait_ge(qk_stat, n - 1)
                    act.wait_ge(proj_ready, n + 1)
                    act.activation(work[:, n % 2, :], sb_T[:, n, :], ACT.Square).then_inc(qk_sq, 1)
                if 2 <= n < 10:
                    qk_inverse_root(n - 2)

            def mixed(m):
                kind, d = MIXED[m]
                split_hi(DN_IN + m + 2, 0, 0)
                act.wait_ge(unit_done, DN_IN + m + 1)
                b = bank(6 + m % 2)
                if kind == "ba":
                    act.activation(ab_T[:, :], b[0:2 * DNH, :], ACT.Copy).then_inc(proj_ready, 1)
                elif kind == "conv":
                    n = CONVS.index(d)
                    if n < 2:
                        act.wait_ge(pad_zero, 1)
                    else:
                        act.wait_ge(conv_step, 4 * (n - 1))
                    act.activation(pad[:, n % 2, TAPS - 1:], b, ACT.Copy).then_inc(proj_ready, 1)
                elif kind == "z":
                    act.activation(z_gate[:, d, :], b, ACT.Copy).then_inc(proj_ready, 1)
                else:
                    if d:
                        act.wait_ge(gate_stored, 16 * d)
                    act.activation(rstd[:, :], b, ACT.Copy).then_inc(proj_ready, 1)

            mixed(0)
            for b in range(NB):
                act.wait_ge(vt_ps, b + 1)
                act.activation(v_nat[:, b, :], bank(4 + b % 2), ACT.Copy).then_inc(v_nat_ready, 1)
            act.wait_ge(ab_ps, 1)
            ab = bank(3)[:, 0:NB * 2 * DNH].rearrange("p (b c) -> p b c", b=NB)
            act.activation(small["beta"], ab[:, :, 0:DNH], ACT.Sigmoid).then_inc(gate_act, 1)
            act.wait_ge(gate_dve, 2)
            act.activation(small["exp"], small["abs"], ACT.Exp, scale=-1.0).then_inc(gate_act, 1)
            act.wait_ge(gate_act, 2)
            act.activation(small["log"], small["exp"], ACT.Ln, bias=1.0).then_inc(gate_act, 1)
            act.wait_ge(rates_in, 32)
            act.activation(rate[:, :], alog_dt[:, 0, :], ACT.Exp).then_inc(gate_act, 1)
            mixed(1)
            act.wait_ge(gsum_ps, 1)
            gsum = bank(3)[:, 0:NB * DNH].rearrange("p (b h) -> p b h", b=NB)
            act.activation(small["gsum"], gsum, ACT.Copy).then_inc(gsum_act, 1)
            act.activation(small["gexp"], gsum, ACT.Exp).then_inc(gsum_act, 1)

            def exp_abs(h):
                e = h % 2
                act.wait_ge(z_ps, h + 1)
                if h >= 2:
                    act.wait_ge(y_ps, h - 1)
                act.activation(att_a[:, e, :], region[e][:, 0:1280], ACT.Abs).then_inc(soft_step, 1)
                act.wait_ge(soft_step, 3 * h + 1)
                act.activation(att_a[:, e, :], att_a[:, e, :], ACT.Exp, scale=-1.0).then_inc(soft_step, 1)

            def softplus(h):
                e = h % 2
                act.wait_ge(soft_step, 3 * h + 2)
                act.activation(att_a[:, e, :], att_a[:, e, :], ACT.Ln, bias=1.0).then_inc(soft_step, 1)

            def weights(h):
                act.wait_ge(logw_ready, h + 1)
                act.activation(att_a[:, h % 2, :], att_a[:, h % 2, :], ACT.Exp).then_inc(w_raw, 1)

            exp_abs(0)
            softplus(0)
            exp_abs(1)
            mixed(2)
            weights(0)
            softplus(1)
            for h in range(SBH):
                mixed(head_unit(h))
                act.wait_ge(y_ps, h + 1)
                rows_h = slice(SBD * (h % 2), SBD * (h % 2) + SBD)
                act.activation(ysb_hi[rows_h, h // 2, :], region[h % 2][rows_h, 0:S], ACT.Copy).then_inc(y_hi_ready, 1)
                if h < SINGLE:
                    mixed(head_unit(h) + 1)
                if h + 2 < SBH:
                    exp_abs(h + 2)
                if h + 1 < SBH:
                    weights(h + 1)
                if h + 2 < SBH:
                    softplus(h + 2)

            fill = filler(mixed)
            act.wait_ge(conv_step, 48)
            for r in range(8):
                act.activation(conv[:, L2[r], :], conv[:, L2[r], :], ACT.Silu).then_inc(dn_silu, 1)
            act.activation(conv[:, 8:12, :], conv[:, 8:12, :], ACT.Silu).then_inc(dn_silu, 1)
            mixed(Z_0)

            def l2_squares(m):
                for r in (2 * m, 2 * m + 1):
                    act.wait_ge(dn_silu, r + 1)
                    if r >= 2:
                        act.wait_ge(l2_stat, r - 1)
                    act.activation(work[:, r % 2, :], conv[:, L2[r], :], ACT.Square).then_inc(l2_sq, 1)

            for m in range(DNH):
                both = (2 * m, 2 * m + 1)
                l2_squares(m)
                if m < DNH - 1:
                    mixed(Z_0 + 1 + m)
                else:
                    fill("l2")
                for r in both:
                    act.wait_ge(l2_stat, r + 1)
                    if r >= 2:
                        act.wait_ge(l2_ready, r - 1)
                    act.activation(flat(link, r % 2), bank(r % 4), ACT.Ln, bias=eps[:, 0:1]).then_inc(l2_root, 1)
                for r in both:
                    act.wait_ge(l2_root, 4 * m + r % 2 + 1)
                    rs = flat(link, r % 2)
                    act.activation(rs, rs, ACT.Exp, scale=-0.5).then_inc(l2_root, 1)
            fill("start")
            for q in range(NB):
                act.wait_ge(nat_ps, q + 1)
                act.activation(v_dn[:, q], heads(bank(4 + q % 2)), ACT.Copy).then_inc(nat_v_ready, 1)
            act.wait_ge(l2_ready, 8)
            for q in range(NB):
                act.wait_ge(nat_ps, NB + q + 1)
                act.activation(k_dn[:, q], heads(bank(2 * (q % 2))), ACT.Copy).then_inc(nat_ready, 1)
            act.wait_ge(proj_ready, 12 + FILL_0)
            act.activation(z_gate[:, :, :], z_gate[:, :, :], ACT.Silu).then_inc(z_silu, 1)

            for pair in range(NB // 2):
                both = (2 * pair, 2 * pair + 1)
                for b in both:
                    e = b % 2
                    dec = work[:, e, :]
                    act.wait_ge(dec_raw, b + 1)
                    act.activation(dec, dec, ACT.Exp).then_inc(dec_exp, 1)
                    act.wait_ge(prep_ps, b + 1)
                    act.activation(inv[:, e], heads(region[e][:, 0:S]), ACT.Exp).then_inc(gexp_ready, 1)
                    act.wait_ge(glast_ready, b + 1)
                    act.activation(small["kdec"][:, b], small["kdec"][:, b], ACT.Exp).then_inc(kdec_exp, 1)
                fill("prep")
                for b in both:
                    act.wait_ge(inv0_ps, b + 1)
                    act.activation(inv[:, b % 2], heads(region[b % 2][:, 0:S]), ACT.Copy).then_inc(inv0_ready, 1)
                fill("inv0")
                if pair:
                    fill("norm")
                for l in range(1, 7):
                    for b in both:
                        act.wait_ge(prod_ps, 12 * pair + 2 * (l - 1) + b % 2 + 1)
                        act.activation(prod[:, b % 2], heads(region[b % 2][:, 0:S]), ACT.Copy).then_inc(prod_ready, 1)
                    if pair and l == 1:
                        for b in range(2):
                            act.wait_ge(on_stat, b + 1)
                            act.activation(flat(k_dn, b), bank(3 * b + 1), ACT.Ln, bias=eps[:, 0:1]).then_inc(on_root, 1)
                        for b in range(2):
                            act.wait_ge(on_root, b + 1)
                            act.activation(flat(k_dn, b), flat(k_dn, b), ACT.Exp, scale=-0.5).then_inc(on_root, 1)
                    fill("level")
                for b in both:
                    act.wait_ge(corr_ps, 12 * pair + 10 + b % 2 + 1)
                    for h in range(DNH):
                        ins = act.activation(prod[:, b % 2, h], k_dn[:, b, h], ACT.Copy,
                                             scale=small["gexp"][:, b, h:h + 1])
                    ins.then_inc(kexp_ready, 1)
                    act.wait_ge(kexp_ready, b + 1)
                    for h in range(DNH):
                        ins = act.activation(k_dn[:, b, h], k_dn[:, b, h], ACT.Copy,
                                             scale=small["kdec"][:, b, h:h + 1])
                    ins.then_inc(kdec_ready, 1)
                fill("solve")
                for b in both:
                    act.wait_ge(uw_ps, b + 1)
                    for h in range(DNH):
                        ins = act.activation(v_dn[:, b, h], region[b % 2][:, h * P:(h + 1) * P], ACT.Copy,
                                             scale=small["beta"][:, b, h:h + 1])
                    ins.then_inc(u_ready, 1)
                fill("solved")
                for b in both:
                    fill("step")
                    if b == NB - 1:
                        act.wait_ge(on_stat, b)
                        inverse_root(flat(k_dn, b - 1), 1, on_root, b - 1)
                    act.wait_ge(o_ps, b + 1)
                    act.wait_ge(v_new_ready, b + 1)
                    act.activation(flat(v_dn, b), region[b % 2][:, 0:S], ACT.Square).then_inc(on_sq, 1)
                    act.activation(conv[:, 8:12, b * P:(b + 1) * P], heads(region[b % 2][:, 0:S]),
                                   ACT.Copy).then_inc(o_ready, 1)

            fill("last")
            act.wait_ge(on_stat, NB)
            inverse_root(flat(k_dn, NB - 1), 4, on_root, NB - 1)
            fill.rest()
            act.wait_ge(on_gated, NB)
            for h in range(DNH):
                act.activation(ydn_hi[:, h, :], conv[:, 8 + h, :], ACT.Copy).then_inc(ydn_hi_ready, 1)

            act.wait_ge(branch_lo, DNH)
            def sigmoids(i, oo):
                act.wait_ge(gates_in[oo % 2], 32 * (2 * i + oo // 2 + 1))
                act.activation(gates[:, oo % 2], gates[:, oo % 2], ACT.Sigmoid).then_inc(sig_ready, 1)

            sigmoids(0, 0)
            for i in range(2):
                for oo in range(4):
                    o = 4 * i + oo
                    split_hi(MERGE, i, oo + 2)
                    if o + 1 < KD:
                        sigmoids(i, oo + 1)
                    act.wait_ge(sum_ready, o + 1)
                    act.activation(m_hi[:, ds(o, 1), :], ssq[:, :].unsqueeze(1), ACT.Copy).then_inc(m_hi_ready, 1)
            with act.Fori(0, 2) as i:
                for u in range(4):
                    split_hi(W_OUT, i, u + 2)
                    squares(2, 4 * i + u, u % 2)
            norm_hi(2)
            ffn(1, F2_IN)

            def store(o, k, before):
                act.wait_ge(out_ps, o + 1)
                if before > 0:
                    act.wait_ge(out_done[k], 16 * before)
                act.activation(out_nat[:, k], bank(k).rearrange("p (b n) -> p b n", b=NB), ACT.Copy)\
                    .then_inc(out_ready, 1)
                act.wait_ge(out_ready, o + 1)
                act.dma_start(out_nat_cols[:, :, ds(o * P, P)], out_nat[:, k]).then_inc(out_done[k], 16)

            for i in range(KD // 2):
                for oo in range(2):
                    split_hi(F2_OUT, i, 2 * oo + 2)
                    split_hi(F2_OUT, i, 2 * oo + 3)
                    o = 2 * i + oo
                    if o > 0:
                        store(o - 1, 1 - oo, i - 1 + oo)
            store(KD - 1, 1, KD // 2 - 1)
            act.wait_ge(out_done[0], 16 * KD // 2)
            act.wait_ge(out_done[1], 16 * KD // 2)


        @block.vector
        def _(dve):
            def split_lo(phase, i, u):
                n = phase + 4 * i + u
                if is_static(i) and n >= UNITS:
                    return
                slot, k = (phase + u) % RAW, unit_chunks(n) if is_static(i) else unit_chunks(phase)
                dve.wait_ge(hi_ready, n + 1)
                dve.tensor_tensor(w_lo[:, slot % 2, 0:k, :], raw[:, slot, 0:k, :],
                                  w_hi[:, slot % 2, 0:k, :].bitcast(f32), ALU.subtract).then_inc(lo_ready, 1)

            def ada_sum(acc, piece, done, q):
                for k in range(KD):
                    if k == 0:
                        ins = dve.tensor_scalar(acc, piece[:, 0, :], cond[:, 0:1], None, ALU.mult)
                    else:
                        dve.wait_ge(done, KD * q + k)
                        ins = dve.scalar_tensor_tensor(acc, piece[:, k, :], cond[:, k:k + 1], acc, ALU.mult, ALU.add)
                    ins.then_inc(done, 1)

            def halve(acc, piece, done, q):
                for n, (dst, k) in enumerate(((piece[:, 0:4, :], 4), (piece[:, 0:2, :], 2), (acc, 1))):
                    if n:
                        dve.wait_ge(done, 3 * q + n)
                    dve.tensor_tensor(dst, piece[:, 0:k, :], piece[:, k:2 * k, :], ALU.add).then_inc(done, 1)

            def ada_late(q, k, place):
                dve.wait_ge(ada_scaled, q + 1)
                halve(ada_acc[:, place:place + 1, :], ada_raw[:, k], ada_step, q)

            def columns(col, b, cols, tmp, biased, step0):
                n, steps = cols // P, [step0]

                def then(ins):
                    steps[0] = steps[0] + 1
                    ins.then_inc(mod_step, 1)
                    dve.wait_ge(mod_step, steps[0])

                t = tmp[:, 0:cols].rearrange("p (n e) -> p n e", n=n)
                then(dve.tensor_tensor(t, bank(b)[:, 0:cols].rearrange("p (n e) -> p n e", n=n),
                                       ident[:, :].unsqueeze(1).to_broadcast([P, n, P]), ALU.mult))
                then(dve.tensor_reduce(mod[:, ds(col, n)], t, axis=mybir.AxisListType.X, op=ALU.add))
                dve.tensor_tensor(mod[:, ds(col, n)], mod[:, ds(col, n)], vec[:, ds(col, n)], ALU.add)\
                    .then_inc(biased, 1)

            def ada_mod(r):
                dve.wait_ge(mod_ps, r + 1)
                columns(LATE + 4 * r, 5, 4 * P, rstd, mod_ready, 2 * r)

            def newton(dst, b, tmp, done, n):
                dve.scalar_tensor_tensor(tmp, bank(b), EPS, dst, ALU.add, ALU.mult).then_inc(done, 1)
                dve.wait_ge(done, 3 * n + 1)
                dve.scalar_tensor_tensor(tmp, tmp, -0.5, dst, ALU.mult, ALU.mult).then_inc(done, 1)
                dve.wait_ge(done, 3 * n + 2)
                dve.scalar_tensor_tensor(dst, tmp, 1.5, dst, ALU.add, ALU.mult).then_inc(done, 1)
                dve.wait_ge(done, 3 * n + 3)

            def refine(s):
                dve.wait_ge(root_ready, 2 * s + 2)
                newton(rstd[:, :], 4, work[:, 0, :], rstd_ready, s)

            def norm(s):
                if s:
                    dve.wait_ge(mod_ready, (SC[s] * KD + KD - LATE) // 4)
                else:
                    dve.wait_ge(early_mod, 1)
                gain = vec[:, 72 + 8 * s:80 + 8 * s]
                dve.scalar_tensor_tensor(scale_col[:, s, :], mod[:, SC[s] * KD:SC[s] * KD + KD], 1.0, gain,
                                         ALU.add, ALU.mult).then_inc(cols_ready, 1)
                if s:
                    refine(s)
                dve.wait_ge(cols_ready, 2 * s + 1)

                def low(k):
                    dve.wait_ge(u_hi_ready, KD * s + k + 1)
                    dve.scalar_tensor_tensor(u_lo[:, k, :], work[:, k % 2, :],
                                             mod[:, SH[s] * KD + k:SH[s] * KD + k + 1], u_hi[:, k, :].bitcast(f32),
                                             ALU.add, ALU.subtract).then_inc(u_lo_ready, 1)

                for k in range(KD):
                    if k >= 2:
                        low(k - 2)
                        dve.wait_ge(u_lo_ready, KD * s + k - 1)
                    dve.scalar_tensor_tensor(work[:, k % 2, :], hT[:, k, :], scale_col[:, s, k:k + 1], rstd[:, :],
                                             ALU.mult, ALU.mult).then_inc(normed_ready, 1)
                low(KD - 2)
                low(KD - 1)

            def gate_columns(s, factor):
                dve.wait_ge(mod_ready, (GT[s] * KD + KD - LATE) // 4)
                dve.tensor_scalar(gate_col[:, s, :], mod[:, GT[s] * KD:GT[s] * KD + KD], factor, None,
                                  ALU.mult).then_inc(cols_ready, 1)
                dve.wait_ge(cols_ready, 2 * s + 2)

            def residual(s, o, b):
                chunk = hT[:, ds(o, 1), :].rearrange("p a s -> p (a s)")
                result = work[:, b - 6, :] if s == 2 else chunk
                dve.scalar_tensor_tensor(result, bank(b), gate_col[:, s, ds(o, 1)], chunk, ALU.mult, ALU.add)\
                    .then_inc(h_ready, 1)

            def ffn_in(f, phase):
                for i in laps(dve, KF // 2):
                    for jj in range(2):
                        j = 2 * i + jj
                        split_lo(phase, i, 2 * jj + 2)
                        dve.wait_ge(silu_ready, KF * f + j + 1)
                        dve.wait_ge(unit_done, phase + 2 * j + 2)
                        if not is_static(j) or f or j:
                            dve.wait_ge(g_lo_ready, KF * f + j)
                        dve.tensor_tensor(work[:, 1, :], work[:, 0, :], bank(2 * jj + 1), ALU.mult)\
                            .then_inc(glu_ready, 1)
                        split_lo(phase, i, 2 * jj + 3)
                        dve.wait_ge(g_hi_ready, KF * f + j + 1)
                        dve.tensor_tensor(g_lo[:, ds(j, 1), :], work[:, 1:2, :], g_hi[:, ds(j, 1), :].bitcast(f32),
                                          ALU.subtract).then_inc(g_lo_ready, 1)
                        if f == 0:
                            if jj == 0 and (not is_static(i) or i):
                                ada_mod(i - 1)
                            ada_late(2 * j, 0, 2 * jj)
                            ada_late(2 * j + 1, 1, 2 * jj + 1)

            def ffn_out(s, f, phase):
                gate_columns(s, 0.5)
                for i in laps(dve, KD // 2):
                    for oo in range(2):
                        o = 2 * i + oo
                        piece = f == 0 and not (is_static(i) and i == KD // 2 - 1)
                        split_lo(phase, i, 2 * oo + 2)
                        dve.wait_ge(unit_done, phase + 2 * o + 2)
                        if f and not (is_static(o) and o < 2):
                            dve.wait_ge(out_ps, o - 1)
                        residual(s, o, 6 + oo)
                        split_lo(phase, i, 2 * oo + 3)
                        if f == 0 and oo == 0:
                            ada_mod(KF // 2 + i - 1)
                        if piece:
                            ada_late(2 * (KF + o), 0, 2 * oo)
                            ada_late(2 * (KF + o) + 1, 1, 2 * oo + 1)

            dve.wait_ge(cond_ready, 1)
            for q in range(EARLY):
                if q in BY_ACT:
                    n = BY_ACT.index(q)
                    dve.wait_ge(early_scaled, n + 1)
                    halve(ada_early[:, q, 0:1, :], ada_early[:, q], early_halves, n)
                else:
                    dve.wait_ge(ada_early_in[q], 16)
                    ada_sum(ada_early[:, q, 0, :], ada_early[:, q], early_step, BY_DVE.index(q))
                if q == 4:
                    refine(0)
            split_lo(F1_IN, 0, 0)
            split_lo(F1_IN, 0, 1)
            dve.wait_ge(early_ps, 1)
            dve.wait_ge(vec_ready, 2)
            dve.tensor_tensor(mod[:, 0:LATE], bank(5)[:, 0:LATE], vec[:, 0:LATE], ALU.add).then_inc(early_mod, 1)
            dve.wait_ge(early_mod, 1)
            norm(0)
            ffn_in(0, F1_IN)
            ffn_out(0, 0, F1_OUT)

            norm(1)
            gate_columns(1, 1.0)
            dve.tensor_scalar(qk_gain[:, 0:1], vec2[:, 49:50], SBD ** -0.5, None, ALU.mult).then_inc(gain_ready, 1)
            dve.tensor_copy(qk_gain[:, 1:2], vec2[:, 50:51]).then_inc(gain_ready, 1)
            dve.wait_ge(gain_ready, 2)

            for n in range(12):
                split_lo(SB_IN, 0, n + 2)
                if 2 <= n < 10:
                    r = n - 2
                    rs = (ssq, rstd)[r % 2]
                    dve.wait_ge(qk_root, 2 * r + 2)
                    newton(rs[:, :], r % 4, att_a[:, 0, 0:S], qk_rs, r)
                    dve.scalar_tensor_tensor(sb_T[:, r, :], sb_T[:, r, :], qk_gain[:, r % 2:r % 2 + 1],
                                             rs[:, :], ALU.mult, ALU.mult).then_inc(qk_ready, 1)

            def mixed(m):
                split_lo(DN_IN + m + 2, 0, 0)
                convolve(m)

            def convolve(m):
                kind, d = MIXED[m]
                if kind != "conv":
                    return
                n, cc = CONVS.index(d), conv_chunk(d)
                dve.wait_ge(proj_ready, 12 + m + 1)
                for t in range(TAPS):
                    tap = vec2[:, 12 * t + cc:12 * t + cc + 1]
                    if t == 0:
                        ins = dve.tensor_scalar(conv[:, cc, :], pad[:, n % 2, 0:S], tap, None, ALU.mult)
                    else:
                        dve.wait_ge(conv_step, 4 * n + t)
                        ins = dve.scalar_tensor_tensor(conv[:, cc, :], pad[:, n % 2, t:t + S], tap, conv[:, cc, :],
                                                       ALU.mult, ALU.add)
                    ins.then_inc(conv_step, 1)

            mixed(0)
            def blocks(t):
                return t.unsqueeze(1).to_broadcast([P, NB, DNH])

            dve.wait_ge(ab_ps, 1)
            ab = bank(3)[:, 0:NB * 2 * DNH].rearrange("p (b c) -> p b c", b=NB)
            dve.wait_ge(rates_in, 32)
            dve.wait_ge(gate_act, 1)
            dve.tensor_tensor(small["a"], ab[:, :, DNH:], blocks(alog_dt[:, 1, :]), ALU.add).then_inc(gate_dve, 1)
            dve.wait_ge(gate_dve, 1)
            dve.scalar_tensor_tensor(small["abs"], small["a"], -1.0, small["a"], ALU.mult, ALU.max).then_inc(gate_dve, 1)
            dve.tensor_scalar(small["neg_beta"], small["beta"], -1.0, None, ALU.mult).then_inc(gate_dve, 1)
            dve.wait_ge(gate_act, 4)
            dve.wait_ge(gate_dve, 2)
            dve.scalar_tensor_tensor(small["a"], small["a"], 0.0, small["log"], ALU.max, ALU.add).then_inc(gate_dve, 1)
            dve.wait_ge(gate_dve, 4)
            dve.scalar_tensor_tensor(small["g"], small["a"], -1.0, blocks(rate[:, :]), ALU.mult, ALU.mult)\
                .then_inc(gate_dve, 1)
            mixed(1)

            def keep_and_beta(h):
                e = h % 2
                z = region[e][:, 0:1280]
                dve.wait_ge(soft_step, 3 * h + 3)
                if h >= 2:
                    dve.wait_ge(later_ps, h - 1)
                dve.scalar_tensor_tensor(att_b[:, e, :], z, 0.0, att_a[:, e, :], ALU.max, ALU.add)\
                    .then_inc(keep_ready, 1)
                dve.wait_ge(keep_ready, h + 1)
                dve.scalar_tensor_tensor(att_a[:, e, :], z, 0.0, att_a[:, e, :], ALU.min, ALU.subtract)\
                    .then_inc(beta_ready, 1)

            def log_weights(h):
                e = h % 2
                dve.wait_ge(later_ps, h + 1)
                dve.wait_ge(beta_ready, h + 1)
                dve.tensor_tensor(att_a[:, e, :], att_a[:, e, :], region[e][:, 0:1280], ALU.subtract)\
                    .then_inc(logw_ready, 1)

            keep_and_beta(0)
            mixed(2)
            log_weights(0)
            keep_and_beta(1)
            for h in range(SBH):
                e = h % 2
                split_lo(DN_IN + head_unit(h) + 2, 0, 0)
                dve.wait_ge(y_hi_ready, h + 1)
                rows_h = slice(SBD * e, SBD * e + SBD)
                dve.tensor_tensor(ysb_lo[rows_h, h // 2, :], region[e][rows_h, 0:S],
                                  ysb_hi[rows_h, h // 2, :].bitcast(f32), ALU.subtract).then_inc(y_lo_ready, 1)
                convolve(head_unit(h))
                if h < SINGLE:
                    mixed(head_unit(h) + 1)
                if h + 1 < SBH:
                    log_weights(h + 1)
                if h + 2 < SBH:
                    keep_and_beta(h + 2)

            fill = filler(mixed)
            tmp = prod[:, 0].rearrange("p h e -> p (h e)")
            mixed(Z_0)
            for m in range(DNH):
                if m < DNH - 1:
                    mixed(Z_0 + 1 + m)
                else:
                    fill("l2")
                for r in (2 * m, 2 * m + 1):
                    rs, cc = flat(link, r % 2), L2[r]
                    dve.wait_ge(l2_root, 4 * m + r % 2 + 3)
                    newton(rs, r % 4, tmp, l2_rs, r)
                    dve.scalar_tensor_tensor(conv[:, cc, :], conv[:, cc, :], float(P) ** -0.5 if cc < 4 else 1.0,
                                             rs, ALU.mult, ALU.mult).then_inc(l2_ready, 1)
            fill("start")

            def output_norm(b):
                dve.wait_ge(on_root, b + 3 if b < 2 else 2 * b + 2)
                newton(flat(k_dn, b), 3 * (b % 2) + 1, flat(v_dn, b), on_rs, b)
                o_b = conv[:, 8:12, b * P:(b + 1) * P]
                dve.wait_ge(o_ready, b + 1)
                dve.scalar_tensor_tensor(o_b, o_b, vec2[:, 48:49], k_dn[:, b], ALU.mult, ALU.mult)\
                    .then_inc(on_scaled, 1)
                dve.wait_ge(on_scaled, b + 1)
                dve.wait_ge(z_silu, 1)
                dve.tensor_tensor(o_b, o_b, z_gate[:, :, b * P:(b + 1) * P], ALU.mult).then_inc(on_gated, 1)

            for pair in range(NB // 2):
                both = (2 * pair, 2 * pair + 1)
                for b in both:
                    e = b % 2
                    gsums = heads(region[e][:, 0:S])
                    dec = heads(work[:, e, :])
                    dve.wait_ge(prep_ps, b + 1)
                    dve.wait_ge(gsum_act, 2)
                    for h in range(DNH):
                        ins = dve.tensor_scalar(dec[:, h], gsums[:, h], small["gsum"][:, b, h:h + 1], 0.0,
                                                ALU.subtract, ALU.min)
                    ins.then_inc(dec_raw, 1)
                    dve.wait_ge(gexp_ready, b + 1)
                    dve.tensor_tensor(small["kdec"][:, b], gsums[:, :, P - 1], small["gsum"][:, b], ALU.subtract)
                    dve.tensor_copy(small["glast"][:, b], inv[:, e, :, P - 1]).then_inc(glast_ready, 1)
                    queries = conv[:, 0:4, b * P:(b + 1) * P]
                    dve.tensor_tensor(queries, queries, inv[:, e], ALU.mult)
                    dve.wait_ge(dec_masked, b + 1)
                    dve.tensor_tensor(att_t[:, e], heads(region[e][:, 2 * S:3 * S]), dec, ALU.mult)\
                        .then_inc(att_ready, 1)
                    for h in range(DNH):
                        ins = dve.scalar_tensor_tensor(sys_t[:, e, h], region[e][:, S + h * P:S + (h + 1) * P],
                                                       small["beta"][:, b, h:h + 1], dec[:, h], ALU.mult, ALU.mult)
                    ins.then_inc(sys_ready, 1)
                    dve.wait_ge(sys_ready, b + 1)
                    dve.wait_ge(dec_masked, 1)
                    dve.tensor_tensor(link[:, e], sys_t[:, e], each(level[:, 0, :]), ALU.mult).then_inc(link_0, 1)
                    dve.wait_ge(link_0, b + 1)
                    dve.tensor_tensor(inv_t[:, e], each(ident[:, :]), link[:, e], ALU.subtract).then_inc(inv_t0, 1)
                fill("prep")
                fill("inv0")
                if pair:
                    fill("norm")
                    for b in range(2):
                        output_norm(b)
                for l in range(1, 7):
                    for b in both:
                        e = b % 2
                        dve.wait_ge(corr_ps, 12 * pair + 2 * (l - 1) + e + 1)
                        if l < 6:
                            dve.tensor_tensor(inv[:, e], inv[:, e], heads(region[e][:, S:2 * S]), ALU.subtract)
                        dve.tensor_tensor(inv_t[:, e], inv_t[:, e], heads(region[e][:, 2 * S:3 * S]),
                                          ALU.subtract).then_inc(inv_ready, 1)
                    fill("level")
                fill("solve")
                for b in both:
                    dve.wait_ge(uw_ps, b + 1)
                    dve.tensor_copy(w_t[:, b % 2], heads(region[b % 2][:, S:2 * S])).then_inc(w_ready, 1)
                fill("solved")
                for b in both:
                    e = b % 2
                    if b == 0:
                        dve.wait_ge(u_ready, 1)
                        dve.tensor_copy(v_new, v_dn[:, 0]).then_inc(v_new_ready, 1)
                        fill("step")
                        dve.wait_ge(ds_ps, 1)
                        dve.tensor_copy(state, heads(region[e][:, S:2 * S])).then_inc(state_ready, 1)
                        continue
                    dve.wait_ge(ws_ps, b)
                    dve.wait_ge(u_ready, b + 1)
                    for h in range(DNH):
                        ins = dve.scalar_tensor_tensor(v_new[:, h], region[e][:, 2 * S + h * P:2 * S + (h + 1) * P],
                                                       small["neg_beta"][:, b, h:h + 1], v_dn[:, b, h],
                                                       ALU.mult, ALU.add)
                    ins.then_inc(v_new_ready, 1)
                    fill("step")
                    if b == NB - 1:
                        output_norm(b - 1)
                    if b < NB - 1:
                        dve.wait_ge(ds_ps, b + 1)
                        dve.wait_ge(state_ready, b)
                        for h in range(DNH):
                            ins = dve.scalar_tensor_tensor(state[:, h], state[:, h], small["glast"][:, b, h:h + 1],
                                                           region[e][:, S + h * P:S + (h + 1) * P],
                                                           ALU.mult, ALU.add)
                        ins.then_inc(state_ready, 1)

            fill("last")
            output_norm(NB - 1)
            fill.rest()
            for h in range(DNH):
                dve.wait_ge(ydn_hi_ready, h + 1)
                dve.tensor_tensor(ydn_lo[:, h, :], conv[:, 8 + h, :], ydn_hi[:, h, :].bitcast(f32),
                                  ALU.subtract).then_inc(branch_lo, 1)

            dve.wait_ge(gate_stored, 16 * 2 * KD)
            with dve.Fori(0, 2) as i:
                for oo in range(4):
                    e, o = oo % 2, 4 * i + oo
                    split_lo(MERGE, i, oo + 2)
                    dve.wait_ge(branch_lo, DNH + o)
                    dve.wait_ge(sig_ready, o + 1)
                    dve.wait_ge(unit_done, MERGE + o + 1)
                    dve.tensor_tensor(ssq[:, :], gates[:, e, 0, :], bank(2 * e), ALU.mult).then_inc(part_ready, 1)
                    dve.tensor_tensor(rstd[:, :], gates[:, e, 1, :], bank(2 * e + 1), ALU.mult).then_inc(part_ready, 1)
                    dve.wait_ge(part_ready, 2 * o + 2)
                    dve.tensor_tensor(ssq[:, :], ssq[:, :], rstd[:, :], ALU.add).then_inc(sum_ready, 1)
                    dve.wait_ge(m_hi_ready, o + 1)
                    dve.tensor_tensor(m_lo[:, ds(o, 1), :], ssq[:, :].unsqueeze(1), m_hi[:, ds(o, 1), :].bitcast(f32),
                                      ALU.subtract).then_inc(branch_lo, 1)
            with dve.Fori(0, 2) as i:
                for u in range(4):
                    dve.wait_ge(unit_done, W_OUT + 4 * i + u + 1)
                    residual(1, 4 * i + u, 6 + u % 2)
                    split_lo(W_OUT, i, u + 2)
            norm(2)
            ffn_in(1, F2_IN)
            ffn_out(2, 1, F2_OUT)

        @block.tensor
        def _(pe):
            def unit(phase, i, u, b, x_hi, x_lo, x0=0, w0=0, k=KD, start=True, stop=True, ready=None):
                slot = (phase + u) % 2
                if w0 == 0:
                    pe.wait_ge(lo_ready, phase + 4 * i + u + 1)
                for n in range(k):
                    if ready:
                        ready(n)
                    wh, wl = w_hi[:, slot, w0 + n, :], w_lo[:, slot, w0 + n, :]
                    xh, xl = x_hi[:, x0 + n, :], x_lo[:, x0 + n, :]
                    pe.matmul(bank(b), wh, xh, start=start and n == 0, stop=False)
                    pe.matmul(bank(b), wh, xl, start=False, stop=False)
                    ins = pe.matmul(bank(b), wl, xh, start=False, stop=stop and n == k - 1)
                return ins

            def normed_chunks(s):
                return lambda k: pe.wait_ge(u_lo_ready, KD * s + k + 1)

            def statistics(s):
                pe.wait_ge(ssq_step, (KD - 1) * (s + 1))
                pe.matmul(bank(4), mean_d[:, :], ssq[:, :], start=True, stop=False)
                pe.wait_ge(sq_ready, KD * (s + 1))
                pe.matmul(bank(4), mean_d[:, :], work[:, 1, :], start=False, stop=True).then_inc(stat_ps, 1)

            def ada_total(r):
                pe.wait_ge(ada_step, 12 * (r + 1))
                pe.matmul(bank(5), ones[:, :], ada_acc.rearrange("p n e -> p (n e)"), start=True, stop=True)\
                    .then_inc(mod_ps, 1)

            def two_units(phase, banks, s):
                pe.wait_ge(lo_ready, phase + 2)
                for k in range(KD):
                    pe.wait_ge(u_lo_ready, KD * s + k + 1)
                    for u in range(2):
                        slot, out_u = (phase + u) % 2, bank(banks[u])
                        wh, wl, xh, xl = w_hi[:, slot, k, :], w_lo[:, slot, k, :], u_hi[:, k, :], u_lo[:, k, :]
                        pe.matmul(out_u, wh, xh, start=k == 0, stop=False)
                        pe.matmul(out_u, wh, xl, start=False, stop=False)
                        ins = pe.matmul(out_u, wl, xh, start=False, stop=k == KD - 1)
                        if k == KD - 1:
                            ins.then_inc(unit_done, 1)

            def ffn_in(f, phase):
                for i in laps(pe, KF // 2):
                    for jj in range(2):
                        j = 2 * i + jj
                        if not is_static(j) or f or j >= 2:
                            pe.wait_ge(glu_ready, KF * f + j - 1)
                        if is_static(j) and j == 0:
                            two_units(phase, (0, 1), 2 * f)
                        for ab in range(2):
                            if not (is_static(j) and j == 0):
                                unit(phase, i, 2 * jj + ab, 2 * jj + ab, u_hi, u_lo).then_inc(unit_done, 1)
                            if f == 0 and jj == 0 and ab == 1 and (not is_static(i) or i):
                                ada_total(i - 1)

            def ffn_out(s, f, phase, after):
                def silu_chunks(k):
                    if k == HALF - 1:
                        pe.wait_ge(g_lo_ready, KF * (f + 1))

                for i in laps(pe, KD // 2):
                    for oo in range(2):
                        o = 2 * i + oo
                        pe.wait_ge(h_ready, KD * (s + 1) + o - 1)
                        first = is_static(o) and o == 0
                        if first:
                            pe.wait_ge(g_lo_ready, KF * (f + 1) - 1)
                        unit(phase, i, 2 * oo, 6 + oo, g_hi, g_lo, k=HALF, stop=False).then_inc(unit_done, 1)
                        unit(phase, i, 2 * oo + 1, 6 + oo, g_hi, g_lo, x0=HALF, k=HALF, start=False,
                             ready=silu_chunks if first else None).then_inc(unit_done, 1)
                        if f == 0 and oo == 0:
                            ada_total(KF // 2 + i - 1)
                        after(i, oo)

            pe.wait_ge(masks, 10)
            pe.wait_ge(c_in, 16)
            pe.transpose(bank(6)[:, 0:KD], c_rows[:, :], ident[0:KD, 0:KD]).then_inc(c_ps, 1)
            pe.wait_ge(x_in, 16 * NB)
            for k in range(KD):
                if k >= 4:
                    pe.wait_ge(h_ready, k - 3)
                for b in range(NB):
                    ins = pe.transpose(bank(k % 4)[:, b * P:(b + 1) * P], x_nat[:, b, k * P:(k + 1) * P], ident[:, :])
                ins.then_inc(x_ps, 1)

            statistics(0)
            pe.wait_ge(small_in, 16 * 10)
            pe.transpose(bank(7)[:, 0:96], vec_rows[:, :], ident[0:96, 0:96])
            pe.transpose(bank(7)[:, 128:179], vec2_rows[:, :], ident[0:51, 0:51]).then_inc(vec_ps, 1)
            for q in range(EARLY):
                if q in BY_ACT:
                    pe.wait_ge(early_halves, 3 * (BY_ACT.index(q) + 1))
                else:
                    pe.wait_ge(early_step, KD * (BY_DVE.index(q) + 1))
                for k in range(2):
                    ins = pe.matmul(bank(5)[:, 2 * q + k:2 * q + k + 1], ada_early[:, q, 0, k * P:(k + 1) * P],
                                    ones[:, 0:1], start=True, stop=True)
            ins.then_inc(early_ps, 1)
            ffn_in(0, F1_IN)

            ffn_out(0, 0, F1_OUT, lambda i, oo: None)
            statistics(1)

            def qk_statistics(r):
                pe.wait_ge(qk_sq, r + 1)
                if r >= 4:
                    pe.wait_ge(qk_rs, 3 * (r - 4) + 1)
                pe.matmul(bank(r % 4), mean_64[:, :], work[:, r % 2, :], start=True, stop=True).then_inc(qk_stat, 1)

            two_units(SB_IN, (6, 7), 1)
            for n in range(2, 12):
                pe.wait_ge(proj_ready, n - 1)
                unit(SB_IN, 0, n, 6 + n % 2, u_hi, u_lo).then_inc(unit_done, 1)
                if n < 10:
                    qk_statistics(n - 2)

            def mixed(m, k0=0, k1=KD):
                if k0 == 0:
                    pe.wait_ge(proj_ready, 12 + m - 1)
                ins = unit(DN_IN, 0, m, 6 + m % 2, u_hi, u_lo, x0=k0, w0=k0, k=k1 - k0, start=k0 == 0, stop=k1 == KD)
                if k1 == KD:
                    ins.then_inc(unit_done, 1)

            mixed(0)
            pe.wait_ge(proj_ready, 12)
            for b in range(NB):
                if b >= 2:
                    pe.wait_ge(v_nat_ready, b - 1)
                for k in range(4):
                    ins = pe.transpose(bank(4 + b % 2)[:, k * P:(k + 1) * P], sb_T[:, 8 + k, b * P:(b + 1) * P],
                                       ident[:, :])
                ins.then_inc(vt_ps, 1)
            pe.wait_ge(qk_rs, 3 * 8)
            pe.wait_ge(proj_ready, 13)
            for b in range(NB):
                ins = pe.transpose(bank(3)[:, 8 * b:8 * b + 8], ab_T[:, b * P:(b + 1) * P], ident[0:8, 0:8])
            ins.then_inc(ab_ps, 1)

            def scores(h):
                rows_h = slice(SBD * (h % 2), SBD * (h % 2) + SBD)
                if h >= 2:
                    pe.wait_ge(y_lo_ready, h - 1)
                for j in range(NB):
                    ins = pe.matmul(region[h % 2][:, OFF[j]:OFF[j] + WID[j]],
                                    sb_T[rows_h, h // 2 * 2 + 1, j * P:(j + 1) * P], sb_T[rows_h, h // 2 * 2, j * P:S],
                                    start=True, stop=True)
                ins.then_inc(z_ps, 1)

            pe.wait_ge(qk_ready, 8)
            pe.wait_ge(v_nat_ready, NB)
            scores(0)
            mixed(1)
            pe.wait_ge(gate_dve, 5)
            pe.matmul(bank(3)[:, 0:NB * DNH], upto[:, :], small["g"].rearrange("p b h -> p (b h)"),
                      start=True, stop=True).then_inc(gsum_ps, 1)
            pe.wait_ge(gsum_act, 2)
            scores(1)
            mixed(2)
            for h in range(SBH):
                e = h % 2
                pe.wait_ge(keep_masked, h + 1)
                pe.wait_ge(beta_ready, h + 1)
                for j in range(NB):
                    for j2 in range(j, NB):
                        at = OFF[j] + P * (j2 - j)
                        ins = pe.matmul(region[e][:, at:at + WID[j2]], (below if j2 == j else ones)[:, :],
                                        att_b[:, e, OFF[j2]:OFF[j2] + WID[j2]], start=j2 == j, stop=j2 == NB - 1)
                ins.then_inc(later_ps, 1)
                mixed(head_unit(h))
                pe.wait_ge(w_masked, h + 1)
                for j in range(NB):
                    ins = pe.matmul(region[e][SBD * e:SBD * e + SBD, j * P:S], v_nat[:, j, SBD * h:SBD * h + SBD],
                                    att_a[:, e, OFF[j]:OFF[j] + WID[j]], start=j == 0, stop=j == NB - 1)
                ins.then_inc(y_ps, 1)
                if h < SINGLE:
                    mixed(head_unit(h) + 1)
                if h + 2 < SBH:
                    scores(h + 2)

            done = [0]

            def fill(point, chunks=None):
                for _ in range(FILL[point] if chunks is None else chunks):
                    m, k = FILL_0 + done[0] // KD, done[0] % KD
                    if m < len(MIXED):
                        mixed(m, k, k + 1)
                        done[0] += 1

            mixed(Z_0)
            for m in range(DNH):
                if m < DNH - 1:
                    mixed(Z_0 + 1 + m)
                else:
                    fill("l2")
                if m == 0:
                    pe.wait_ge(y_lo_ready, SBH)
                for r in (2 * m, 2 * m + 1):
                    pe.wait_ge(l2_sq, r + 1)
                    if r >= 4:
                        pe.wait_ge(l2_rs, 3 * (r - 4) + 1)
                    pe.matmul(bank(r % 4), ones[:, :], work[:, r % 2, :], start=True, stop=True).then_inc(l2_stat, 1)
            fill("start")
            pe.wait_ge(dn_silu, 9)
            for q in range(NB):
                if q >= 2:
                    pe.wait_ge(nat_v_ready, q - 1)
                for h in range(DNH):
                    ins = pe.transpose(bank(4 + q % 2)[:, h * P:(h + 1) * P], conv[:, 8 + h, q * P:(q + 1) * P],
                                       ident[:, :])
                ins.then_inc(nat_ps, 1)
            pe.wait_ge(l2_ready, 8)
            for q in range(NB):
                if q >= 2:
                    pe.wait_ge(nat_ready, q - 1)
                for h in range(DNH):
                    ins = pe.transpose(bank(2 * (q % 2))[:, h * P:(h + 1) * P], conv[:, 4 + h, q * P:(q + 1) * P],
                                       ident[:, :])
                ins.then_inc(nat_ps, 1)

            def output_statistics(b):
                pe.wait_ge(on_sq, b + 1)
                if b < 2:
                    pe.wait_ge(sys_ready, b + 3)
                pe.matmul(bank(3 * (b % 2) + 1), mean_p[:, :], flat(v_dn, b), start=True, stop=True)\
                    .then_inc(on_stat, 1)

            for pair in range(NB // 2):
                both = (2 * pair, 2 * pair + 1)
                for b in both:
                    e, cols = b % 2, slice(b * P, (b + 1) * P)
                    if b < 2:
                        pe.wait_ge(nat_ready, NB)
                        pe.wait_ge(nat_v_ready, NB)
                        pe.wait_ge(gsum_act, 2)
                    else:
                        pe.wait_ge(o_ready, b - 1)
                        pe.wait_ge(state_ready, b - 1)
                        pe.wait_ge(v_new_ready, b - 1)
                    for h in range(DNH):
                        pe.matmul(region[e][:, h * P:(h + 1) * P], small["g"][:, b, h:h + 1].to_broadcast([P, P]),
                                  upto[:, :], start=True, stop=True)
                    for h in range(DNH):
                        pe.matmul(region[e][:, S + h * P:S + (h + 1) * P], conv[:, 4 + h, cols], conv[:, 4 + h, cols],
                                  start=True, stop=True)
                    for h in range(DNH):
                        ins = pe.matmul(region[e][:, 2 * S + h * P:2 * S + (h + 1) * P], conv[:, 4 + h, cols],
                                        conv[:, h, cols], start=True, stop=True)
                    ins.then_inc(prep_ps, 1)
                fill("prep")
                for b in both:
                    e = b % 2
                    pe.wait_ge(inv_t0, b + 1)
                    for h in range(DNH):
                        ins = pe.transpose(region[e][:, h * P:(h + 1) * P], inv_t[:, e, h], ident[:, :])
                    ins.then_inc(inv0_ps, 1)
                fill("inv0")
                if pair:
                    fill("norm")
                    for b in range(2):
                        output_statistics(b)
                for l in range(1, 7):
                    for b in both:
                        e = b % 2
                        pe.wait_ge(link_ready, 12 * pair + 2 * (l - 1) + e + 1)
                        if l == 1:
                            pe.wait_ge(inv0_ready, b + 1)
                        else:
                            pe.wait_ge(inv_ready, 12 * pair + 2 * (l - 2) + e + 1)
                        for h in range(DNH):
                            ins = pe.matmul(region[e][:, h * P:(h + 1) * P], link[:, e, h], inv[:, e, h],
                                            start=True, stop=True)
                        ins.then_inc(prod_ps, 1)
                    for b in both:
                        e = b % 2
                        pe.wait_ge(prod_ready, 12 * pair + 2 * (l - 1) + e + 1)
                        if pair and l == 1:
                            pe.wait_ge(on_rs, 3 * e + 1)
                        if l < 6:
                            for h in range(DNH):
                                pe.matmul(region[e][:, S + h * P:S + (h + 1) * P], inv_t[:, e, h], prod[:, e, h],
                                          start=True, stop=True)
                        for h in range(DNH):
                            ins = pe.matmul(region[e][:, 2 * S + h * P:2 * S + (h + 1) * P], prod[:, e, h],
                                            inv_t[:, e, h], start=True, stop=True)
                        ins.then_inc(corr_ps, 1)
                    fill("level")
                fill("solve")
                for b in both:
                    e = b % 2
                    pe.wait_ge(inv_ready, 12 * pair + 10 + e + 1)
                    pe.wait_ge(kexp_ready, b + 1)
                    for h in range(DNH):
                        pe.matmul(region[e][:, h * P:(h + 1) * P], inv_t[:, e, h], v_dn[:, b, h], start=True, stop=True)
                    for h in range(DNH):
                        ins = pe.matmul(region[e][:, S + h * P:S + (h + 1) * P], prod[:, e, h], inv_t[:, e, h],
                                        start=True, stop=True)
                    ins.then_inc(uw_ps, 1)
                fill("solved")
                for b in both:
                    e, cols = b % 2, slice(b * P, (b + 1) * P)
                    pe.wait_ge(w_ready, b + 1)
                    pe.wait_ge(u_ready, b + 1)
                    if b:
                        pe.wait_ge(state_ready, b)
                        for h in range(DNH):
                            ins = pe.matmul(region[e][:, 2 * S + h * P:2 * S + (h + 1) * P], w_t[:, e, h],
                                            state[:, h], start=True, stop=True)
                        ins.then_inc(ws_ps, 1)
                    pe.wait_ge(att_ready, b + 1)
                    for h in range(DNH if b else 0):
                        pe.matmul(region[e][:, h * P:(h + 1) * P], state[:, h], conv[:, h, cols],
                                  start=h == 0, stop=False)
                    fill("step")
                    if b == NB - 1:
                        output_statistics(b - 1)
                    pe.wait_ge(v_new_ready, b + 1)
                    if b < NB - 1:
                        pe.wait_ge(kdec_ready, b + 1)
                        for h in range(DNH):
                            ins = pe.matmul(region[e][:, S + h * P:S + (h + 1) * P], k_dn[:, b, h], v_new[:, h],
                                            start=True, stop=True)
                        ins.then_inc(ds_ps, 1)
                    for h in range(DNH):
                        ins = pe.matmul(region[e][:, h * P:(h + 1) * P], v_new[:, h], att_t[:, e, h],
                                        start=b == 0 and h == 0, stop=h == DNH - 1)
                    ins.then_inc(o_ps, 1)
            fill("last")
            output_statistics(NB - 1)
            fill("last", 2 * KD * KD)

            pe.wait_ge(on_rs, 3 * (NB - 1))
            pe.wait_ge(o_ready, NB)
            for i in range(2):
                for oo in range(4):
                    e, o = oo % 2, 4 * i + oo
                    if o >= 2:
                        pe.wait_ge(part_ready, 2 * (o - 1))
                    unit(MERGE, i, oo, 2 * e, ysb_hi, ysb_lo, k=4)
                    unit(MERGE, i, oo, 2 * e + 1, ydn_hi, ydn_lo, w0=4, k=4,
                         ready=(lambda k: pe.wait_ge(branch_lo, k + 1)) if o == 0 else None).then_inc(unit_done, 1)
            with pe.Fori(0, 2) as i:
                for u in range(4):
                    pe.wait_ge(h_ready, 2 * KD + 4 * i + u - 1)
                    unit(W_OUT, i, u, 6 + u % 2, m_hi, m_lo,
                         ready=(lambda k: pe.wait_ge(branch_lo, DNH + k + 1)) if u == 0 else None)\
                        .then_inc(unit_done, 1)
            statistics(2)
            ffn_in(1, F2_IN)

            def transpose_out(o, b):
                pe.wait_ge(h_ready, 3 * KD + o + 1)
                if not is_static(o) or o >= 2:
                    pe.wait_ge(out_ready, o - 1)
                for q in range(NB):
                    ins = pe.transpose(bank(b)[:, q * P:(q + 1) * P],
                                       work[:, b, q * P:(q + 1) * P], ident[:, :])
                ins.then_inc(out_ps, 1)

            def transpose_last(i, oo):
                if not (is_static(i) and i == 0 and oo == 0):
                    transpose_out(2 * i + oo - 1, 1 - oo)

            ffn_out(2, 1, F2_OUT, transpose_last)
            transpose_out(KD - 1, 1)


_INS = ["x", "c", "w_ada", "b_ada", "g_ffn1", "w_ffn1_in", "w_ffn1_out", "g_mix", "w_in", "g_q_sb", "g_k_sb", "w_conv",
        "a_log", "dt_bias", "g_dn_out", "w_up_sb", "w_up_dn", "w_out", "g_ffn2", "w_ffn2_in", "w_ffn2_out"]


def kernel(**inputs):
    import numpy as np
    import concourse.bacc as bacc
    from concourse.bass_utils import run_bass_kernel_spmd

    nc = bacc.Bacc("TRN2", target_bir_lowering=False, num_devices=1)
    arrays, args = {}, []
    for name in _INS:
        a = np.ascontiguousarray(inputs[name])
        arrays[f"in_{name}"] = a
        args.append(nc.dram_tensor(f"in_{name}", a.shape, mybir.dt.from_np(a.dtype), kind="ExternalInput").ap())
    out = nc.dram_tensor("out_h", (1, S, D), mybir.dt.float32, kind="ExternalOutput").ap()
    build(nc, *args, out)
    result = run_bass_kernel_spmd(nc, [arrays], core_ids=[0])
    return result.results[0]["out_h"]
```
